# Optimizing a Trainium2 kernel written in Bass

```python
import jax, jax.numpy as jnp
from jax import lax
import numpy as np

D_MODEL = 1024
BATCH = 1
SEQ = 256
DEPTH = 2

D_FF = 2816
FFN_RES_SCALE = 0.5
RMS_EPS = 1e-6
PLE_DIM = 256
QBLK = 128
A_HEADS = 8
A_KV_HEADS = 2
A_GROUP = A_HEADS // A_KV_HEADS
A_HEAD_DIM = 64
WINDOW = 128
B_HEADS = 8
B_Q_LORA = 256
B_KV_LORA = 128
B_NOPE_DIM = 64
B_ROPE_DIM = 32
B_V_DIM = 64
ROPE_THETA = 10000.0
C_HEADS = 16
C_HEAD_DIM = 64
FORGET_BIAS_CENTER = 3.0
N_EVEN = (DEPTH + 1) // 2
N_ODD = DEPTH // 2
EVEN_IN_SPLITS = (A_HEADS * A_HEAD_DIM, A_KV_HEADS * A_HEAD_DIM, A_KV_HEADS * A_HEAD_DIM, B_Q_LORA, B_KV_LORA, B_ROPE_DIM)
EVEN_IN_DIM = A_HEADS * A_HEAD_DIM + 2 * A_KV_HEADS * A_HEAD_DIM + B_Q_LORA + B_KV_LORA + B_ROPE_DIM
EVEN_MIX_DIM = A_HEADS * A_HEAD_DIM + B_HEADS * B_V_DIM
ODD_MIX_DIM = C_HEADS * C_HEAD_DIM
ODD_IN_DIM = 3 * ODD_MIX_DIM + C_HEADS


def rms_norm(x, g):
    xf = x.astype(jnp.float32)
    y = xf * lax.rsqrt(jnp.mean(xf * xf, axis=-1, keepdims=True) + RMS_EPS)
    return (y * g.astype(jnp.float32)).astype(x.dtype)

def swiglu(x, w_gate_up, w_down):
    g, u = jnp.split(x @ w_gate_up, 2, axis=-1)
    return (jax.nn.silu(g) * u) @ w_down

def alibi_slopes(n):
    return 2.0 ** (-8.0 * jnp.arange(1, n + 1, dtype=jnp.float32) / n)

def rope_tables(seq, dim):
    inv = ROPE_THETA ** (-jnp.arange(0, dim, 2, dtype=jnp.float32) / dim)
    ang = jnp.arange(seq, dtype=jnp.float32)[:, None] * inv[None, :]
    return jnp.cos(ang), jnp.sin(ang)

def apply_rope(x, cos, sin):
    half = x.shape[-1] // 2
    x1 = x[..., :half].astype(jnp.float32)
    x2 = x[..., half:].astype(jnp.float32)
    return jnp.concatenate([x1 * cos - x2 * sin, x1 * sin + x2 * cos], axis=-1).astype(x.dtype)

def swa_sink_attention(q, k, v, sinks):
    B, S = q.shape[0], q.shape[1]
    nb = S // WINDOW
    qb = q.reshape(B, nb, WINDOW, A_KV_HEADS, A_GROUP, A_HEAD_DIM)
    pad = jnp.zeros((B, WINDOW, A_KV_HEADS, A_HEAD_DIM), k.dtype)
    kp = jnp.concatenate([pad, k], axis=1).reshape(B, nb + 1, WINDOW, A_KV_HEADS, A_HEAD_DIM)
    vp = jnp.concatenate([pad, v], axis=1).reshape(B, nb + 1, WINDOW, A_KV_HEADS, A_HEAD_DIM)
    kb = jnp.concatenate([kp[:, :-1], kp[:, 1:]], axis=2)
    vb = jnp.concatenate([vp[:, :-1], vp[:, 1:]], axis=2)
    s = jnp.einsum('bnqkgd,bnskd->bnkgqs', qb, kb).astype(jnp.float32) * (A_HEAD_DIM ** -0.5)
    qi = jnp.arange(WINDOW)[:, None]
    kj = jnp.arange(2 * WINDOW)[None, :]
    dist = qi + WINDOW - kj
    band = (dist >= 0) & (dist < WINDOW)
    start_ok = (jnp.arange(nb)[:, None, None] * WINDOW + kj[None] - WINDOW) >= 0
    mask = band[None] & start_ok
    slopes = alibi_slopes(A_HEADS).reshape(A_KV_HEADS, A_GROUP)
    s = s - slopes[None, None, :, :, None, None] * dist.astype(jnp.float32)[None, None, None, None]
    s = jnp.where(mask[None, :, None, None], s, -jnp.inf)
    sink = sinks.astype(jnp.float32).reshape(A_KV_HEADS, A_GROUP)[None, None, :, :, None, None]
    m = jnp.maximum(jnp.max(s, axis=-1, keepdims=True), sink)
    e = jnp.exp(s - m)
    pr = e / (jnp.sum(e, axis=-1, keepdims=True) + jnp.exp(sink - m))
    out = jnp.einsum('bnkgqs,bnskd->bnqkgd', pr.astype(v.dtype), vb)
    return out.reshape(B, S, A_HEADS * A_HEAD_DIM)

def mla_attention(q_nope, q_rope, k_nope, k_rope, v):
    B, S = q_nope.shape[0], q_nope.shape[1]
    nb = S // QBLK
    qn = q_nope.reshape(B, nb, QBLK, B_HEADS, B_NOPE_DIM).transpose(1, 0, 2, 3, 4)
    qr = q_rope.reshape(B, nb, QBLK, B_HEADS, B_ROPE_DIM).transpose(1, 0, 2, 3, 4)
    kpos = jnp.arange(S)
    scale = (B_NOPE_DIM + B_ROPE_DIM) ** -0.5

    def one_block(args):
        qn_b, qr_b, n = args
        s = jnp.einsum('bqhd,bkhd->bhqk', qn_b, k_nope) + jnp.einsum('bqhd,bkd->bhqk', qr_b, k_rope)
        s = s.astype(jnp.float32) * scale
        qpos = n * QBLK + jnp.arange(QBLK)
        s = jnp.where(kpos[None, :] <= qpos[:, None], s, -jnp.inf)
        pr = jax.nn.softmax(s, axis=-1)
        return jnp.einsum('bhqk,bkhd->bqhd', pr.astype(v.dtype), v)

    out = lax.map(one_block, (qn, qr, jnp.arange(nb)))
    return out.transpose(1, 0, 2, 3, 4).reshape(B, S, B_HEADS * B_V_DIM)

def fox_attention(q, k, v, logc):
    B, S = q.shape[0], q.shape[1]
    nb = S // QBLK
    qb = q.reshape(B, nb, QBLK, C_HEADS, C_HEAD_DIM).transpose(1, 0, 2, 3, 4)
    cb = logc.reshape(B, nb, QBLK, C_HEADS).transpose(1, 0, 2, 3)
    c_keys = logc.transpose(0, 2, 1)
    kpos = jnp.arange(S)

    def one_block(args):
        q_b, c_b, n = args
        s = jnp.einsum('bqhd,bkhd->bhqk', q_b, k).astype(jnp.float32) * (C_HEAD_DIM ** -0.5)
        s = s + c_b.transpose(0, 2, 1)[..., None] - c_keys[:, :, None, :]
        qpos = n * QBLK + jnp.arange(QBLK)
        s = jnp.where(kpos[None, :] <= qpos[:, None], s, -jnp.inf)
        pr = jax.nn.softmax(s, axis=-1)
        return jnp.einsum('bhqk,bkhd->bqhd', pr.astype(v.dtype), v)

    out = lax.map(one_block, (qb, cb, jnp.arange(nb)))
    return out.transpose(1, 0, 2, 3, 4).reshape(B, S, C_HEADS * C_HEAD_DIM)

def even_mixer(h, w_in, sinks, cq_norm, w_uq, ckv_norm, w_ukv, w_out):
    B, S = h.shape[0], h.shape[1]
    idx = [int(i) for i in np.cumsum(EVEN_IN_SPLITS)[:-1]]
    a_q, a_k, a_v, c_q, c_kv, k_rope = jnp.split(h @ w_in, idx, axis=-1)
    out_a = swa_sink_attention(a_q.reshape(B, S, A_HEADS, A_HEAD_DIM),
                               a_k.reshape(B, S, A_KV_HEADS, A_HEAD_DIM),
                               a_v.reshape(B, S, A_KV_HEADS, A_HEAD_DIM), sinks)
    q = (rms_norm(c_q, cq_norm) @ w_uq).reshape(B, S, B_HEADS, B_NOPE_DIM + B_ROPE_DIM)
    kv = (rms_norm(c_kv, ckv_norm) @ w_ukv).reshape(B, S, B_HEADS, B_NOPE_DIM + B_V_DIM)
    cos, sin = rope_tables(S, B_ROPE_DIM)
    q_nope = q[..., :B_NOPE_DIM]
    q_rope = apply_rope(q[..., B_NOPE_DIM:], cos[None, :, None], sin[None, :, None])
    k_nope = kv[..., :B_NOPE_DIM]
    v = kv[..., B_NOPE_DIM:]
    k_rope = apply_rope(k_rope, cos[None], sin[None])
    out_b = mla_attention(q_nope, q_rope, k_nope, k_rope, v)
    return jnp.concatenate([out_a, out_b], axis=-1) @ w_out

def odd_mixer(h, w_in, b_f, w_out):
    B, S = h.shape[0], h.shape[1]
    w = ODD_MIX_DIM
    q, k, v, f_logit = jnp.split(h @ w_in, [w, 2 * w, 3 * w], axis=-1)
    logf = jax.nn.log_sigmoid(f_logit.astype(jnp.float32) + b_f.astype(jnp.float32))
    logc = jnp.cumsum(logf, axis=1)
    shp = (B, S, C_HEADS, C_HEAD_DIM)
    out = fox_attention(q.reshape(shp), k.reshape(shp), v.reshape(shp), logc)
    return out @ w_out

def _normal(key, shape, scale):
    return jax.random.normal(key, shape, jnp.float32) * scale

def first_inputs(seed: int = 0) -> dict:
    key = jax.random.key(seed)
    ks = jax.random.split(key, 23)
    D = D_MODEL
    return {
        'x': _normal(ks[0], (BATCH, SEQ, D), 1.0),
        'p': _normal(ks[1], (DEPTH, BATCH, SEQ, PLE_DIM), 1.0),
        'ffa_norm': 1.0 + _normal(ks[2], (DEPTH, D), 0.05),
        'ffa_w_gate_up': _normal(ks[3], (DEPTH, D, 2 * D_FF), D ** -0.5),
        'ffa_w_down': _normal(ks[4], (DEPTH, D_FF, D), D_FF ** -0.5),
        'mix_norm': 1.0 + _normal(ks[5], (DEPTH, D), 0.05),
        'ffb_norm': 1.0 + _normal(ks[6], (DEPTH, D), 0.05),
        'ffb_w_gate_up': _normal(ks[7], (DEPTH, D, 2 * D_FF), D ** -0.5),
        'ffb_w_down': _normal(ks[8], (DEPTH, D_FF, D), D_FF ** -0.5),
        'ple_norm': 1.0 + _normal(ks[9], (DEPTH, D), 0.05),
        'ple_w_gate': _normal(ks[10], (DEPTH, D, D), D ** -0.5),
        'ple_w_proj': _normal(ks[11], (DEPTH, PLE_DIM, D), PLE_DIM ** -0.5),
        'ev_w_in': _normal(ks[12], (N_EVEN, D, EVEN_IN_DIM), D ** -0.5),
        'ev_sinks': _normal(ks[13], (N_EVEN, A_HEADS), 0.5),
        'ev_cq_norm': 1.0 + _normal(ks[14], (N_EVEN, B_Q_LORA), 0.05),
        'ev_w_uq': _normal(ks[15], (N_EVEN, B_Q_LORA, B_HEADS * (B_NOPE_DIM + B_ROPE_DIM)), B_Q_LORA ** -0.5),
        'ev_ckv_norm': 1.0 + _normal(ks[16], (N_EVEN, B_KV_LORA), 0.05),
        'ev_w_ukv': _normal(ks[17], (N_EVEN, B_KV_LORA, B_HEADS * (B_NOPE_DIM + B_V_DIM)), B_KV_LORA ** -0.5),
        'ev_w_out': _normal(ks[18], (N_EVEN, EVEN_MIX_DIM, D), EVEN_MIX_DIM ** -0.5),
        'od_w_in': _normal(ks[19], (N_ODD, D, ODD_IN_DIM), D ** -0.5),
        'od_b_f': FORGET_BIAS_CENTER + _normal(ks[20], (N_ODD, C_HEADS), 0.5),
        'od_w_out': _normal(ks[21], (N_ODD, ODD_MIX_DIM, D), ODD_MIX_DIM ** -0.5),
        'final_norm': 1.0 + _normal(ks[22], (D,), 0.05),
    }

def first_block(x, p, ffa_norm, ffa_w_gate_up, ffa_w_down, mix_norm, ffb_norm, ffb_w_gate_up, ffb_w_down,
              ple_norm, ple_w_gate, ple_w_proj, ev_w_in, ev_sinks, ev_cq_norm, ev_w_uq, ev_ckv_norm,
              ev_w_ukv, ev_w_out, od_w_in, od_b_f, od_w_out, final_norm):
    h = x
    for i in range(DEPTH):
        j = i // 2
        h = h + FFN_RES_SCALE * swiglu(rms_norm(h, ffa_norm[i]), ffa_w_gate_up[i], ffa_w_down[i])
        hn = rms_norm(h, mix_norm[i])
        if i % 2 == 0:
            h = h + even_mixer(hn, ev_w_in[j], ev_sinks[j], ev_cq_norm[j], ev_w_uq[j],
                               ev_ckv_norm[j], ev_w_ukv[j], ev_w_out[j])
        else:
            h = h + odd_mixer(hn, od_w_in[j], od_b_f[j], od_w_out[j])
        h = h + FFN_RES_SCALE * swiglu(rms_norm(h, ffb_norm[i]), ffb_w_gate_up[i], ffb_w_down[i])
        gate = jax.nn.sigmoid(rms_norm(h, ple_norm[i]) @ ple_w_gate[i])
        h = h + gate * (p[i] @ ple_w_proj[i])
    return rms_norm(h, final_norm)


DEPTH_2 = 1

N_MEM = 256
EPS = 1e-6
NEG = -1e30
MOBA_HEADS = 8
MOBA_HD = 64
MOBA_WIDTH = MOBA_HEADS * MOBA_HD
MOBA_BLOCK = 256
MOBA_TOPK = 3
Q_CHUNK = 128
GMLP_GROUPS = 8
GMLP_GD = 64
GMLP_WIDTH = GMLP_GROUPS * GMLP_GD
GMLP_CHUNK = 128
N_BRANCH = 2
IN_COLS = 3 * MOBA_WIDTH + 2 * GMLP_WIDTH + N_BRANCH * D_MODEL
XA_HEADS = 4
XA_HD = 128
XA_WIDTH = XA_HEADS * XA_HD
PEER_HEADS = 8
PEER_NKEYS = 128
PEER_N = PEER_NKEYS * PEER_NKEYS
PEER_DQ = 256
PEER_TOPK = 16
PEER_TOK_CHUNK = 128


def rmsnorm(x, g):
    xf = x.astype(jnp.float32)
    y = xf * lax.rsqrt(jnp.mean(xf * xf, axis=-1, keepdims=True) + EPS)
    return (y * g.astype(jnp.float32)).astype(x.dtype)

def rope(x):
    S, Dh = x.shape[1], x.shape[3]
    half = Dh // 2
    freqs = ROPE_THETA ** (-jnp.arange(half, dtype=jnp.float32) / half)
    ang = jnp.arange(S, dtype=jnp.float32)[:, None] * freqs[None, :]
    c = jnp.cos(ang)[None, :, None, :]
    s = jnp.sin(ang)[None, :, None, :]
    xf = x.astype(jnp.float32)
    x1, x2 = xf[..., :half], xf[..., half:]
    return jnp.concatenate([x1 * c - x2 * s, x2 * c + x1 * s], axis=-1).astype(x.dtype)

def moba_attention(q, k, v):
    B, S, H, Dh = q.shape
    nb = -(-S // MOBA_BLOCK)
    pad = nb * MOBA_BLOCK - S
    nq = S // Q_CHUNK
    top = min(MOBA_TOPK, nb)
    kp = jnp.pad(k, ((0, 0), (0, pad), (0, 0), (0, 0)))
    vp = jnp.pad(v, ((0, 0), (0, pad), (0, 0), (0, 0)))
    kb = kp.reshape(B, nb, MOBA_BLOCK, H, Dh).transpose(0, 3, 1, 2, 4)
    vb = vp.reshape(B, nb, MOBA_BLOCK, H, Dh).transpose(0, 3, 1, 2, 4)
    k_mean = jnp.mean(kb.astype(jnp.float32), axis=3)
    q_blk = jnp.arange(S) // MOBA_BLOCK
    past = jnp.arange(nb)[None, :] < q_blk[:, None]
    gate = jnp.einsum("bshd,bhnd->bhsn", q.astype(jnp.float32), k_mean)
    gate = jnp.where(past[None, None], gate, NEG)
    _, sel = lax.top_k(gate, top)
    q_c = q.reshape(B, nq, Q_CHUNK, H, Dh).transpose(0, 1, 3, 2, 4).reshape(B * nq, H, Q_CHUNK, Dh)
    sel_c = sel.reshape(B, H, nq, Q_CHUNK, top).transpose(0, 2, 1, 3, 4).reshape(B * nq, H, Q_CHUNK, top)
    scale = Dh ** -0.5
    h_idx = jnp.arange(H)[:, None, None]

    def query_block(args):
        i, qc, si = args
        b = i // nq
        c = i % nq
        kb_b = kb[b]
        vb_b = vb[b]
        pos = c * Q_CHUNK + jnp.arange(Q_CHUNK)
        valid = si < (pos // MOBA_BLOCK)[None, :, None]
        k_sel = kb_b[h_idx, si]
        v_sel = vb_b[h_idx, si]
        s_sel = jnp.einsum("hqd,hqnld->hqnl", qc, k_sel).astype(jnp.float32) * scale
        s_sel = jnp.where(valid[..., None], s_sel, NEG).reshape(H, Q_CHUNK, top * MOBA_BLOCK)
        own = (c * Q_CHUNK) // MOBA_BLOCK
        k_own = lax.dynamic_index_in_dim(kb_b, own, axis=1, keepdims=False)
        v_own = lax.dynamic_index_in_dim(vb_b, own, axis=1, keepdims=False)
        s_own = jnp.einsum("hqd,hld->hql", qc, k_own).astype(jnp.float32) * scale
        k_pos = own * MOBA_BLOCK + jnp.arange(MOBA_BLOCK)
        s_own = jnp.where((k_pos[None, :] <= pos[:, None])[None], s_own, NEG)
        p = jax.nn.softmax(jnp.concatenate([s_sel, s_own], axis=-1), axis=-1).astype(qc.dtype)
        p_sel = p[..., :top * MOBA_BLOCK].reshape(H, Q_CHUNK, top, MOBA_BLOCK)
        p_own = p[..., top * MOBA_BLOCK:]
        return (jnp.einsum("hqnl,hqnld->hqd", p_sel, v_sel)
                + jnp.einsum("hql,hld->hqd", p_own, v_own))

    out = lax.map(query_block, (jnp.arange(B * nq), q_c, sel_c))
    return out.reshape(B, nq, H, Q_CHUNK, Dh).transpose(0, 1, 3, 2, 4).reshape(B, S, H * Dh)

def gmlp_spatial_gating(u, v, norm_g, w_s, b_s):
    B, S, _ = u.shape
    nc = S // GMLP_CHUNK
    u = jax.nn.gelu(u)
    v = rmsnorm(jax.nn.gelu(v), norm_g)
    vc = v.reshape(B, nc, GMLP_CHUNK, GMLP_GROUPS, GMLP_GD)
    causal = jnp.tril(jnp.ones((GMLP_CHUNK, GMLP_CHUNK), dtype=bool))
    wm = jnp.where(causal[None], w_s, 0.0).astype(v.dtype)
    z = jnp.einsum("gts,bcsgd->bctgd", wm, vc) + b_s.T.astype(v.dtype)[None, None, :, :, None]
    return u * z.reshape(B, S, GMLP_WIDTH)

def memory_cross_attention(h, m, w_q, w_kv, w_o):
    B, S, _ = h.shape
    M = m.shape[1]
    q = (h @ w_q).reshape(B, S, XA_HEADS, XA_HD)
    k, v = jnp.split(m @ w_kv, 2, axis=-1)
    k = k.reshape(B, M, XA_HEADS, XA_HD)
    v = v.reshape(B, M, XA_HEADS, XA_HD)
    s = jnp.einsum("bshd,bmhd->bhsm", q, k).astype(jnp.float32) * (XA_HD ** -0.5)
    p = jax.nn.softmax(s, axis=-1).astype(h.dtype)
    o = jnp.einsum("bhsm,bmhd->bshd", p, v).reshape(B, S, XA_WIDTH)
    return o @ w_o

def peer_ffn(h, w_q, subkeys, w_down, w_up):
    B, S, D = h.shape
    n_chunks = (B * S) // PEER_TOK_CHUNK
    half = PEER_DQ // 2
    kk = PEER_TOPK * PEER_TOPK

    def token_chunk(xc):
        q = (xc @ w_q).reshape(PEER_TOK_CHUNK, PEER_HEADS, 2, half).astype(jnp.float32)
        s = jnp.einsum("thpd,hpnd->thpn", q, subkeys.astype(jnp.float32))
        s1, i1 = lax.top_k(s[:, :, 0], PEER_TOPK)
        s2, i2 = lax.top_k(s[:, :, 1], PEER_TOPK)
        cand_s = (s1[..., :, None] + s2[..., None, :]).reshape(PEER_TOK_CHUNK, PEER_HEADS, kk)
        cand_i = (i1[..., :, None] * PEER_NKEYS + i2[..., None, :]).reshape(PEER_TOK_CHUNK, PEER_HEADS, kk)
        top_s, top_pos = lax.top_k(cand_s, PEER_TOPK)
        e = jnp.take_along_axis(cand_i, top_pos, axis=-1)
        g = jax.nn.softmax(top_s, axis=-1).astype(xc.dtype)
        a = jax.nn.gelu(jnp.einsum("td,thkd->thk", xc, w_down[e]))
        return jnp.einsum("thk,thkd->td", g * a, w_up[e])

    y = lax.map(token_chunk, h.reshape(n_chunks, PEER_TOK_CHUNK, D))
    return y.reshape(B, S, D)

def second_inputs(seed: int = 0) -> dict:
    key = jax.random.key(seed)
    ks = jax.random.split(key, 24)

    def nrm(k, shape, scale):
        return jax.random.normal(k, shape, jnp.float32) * scale

    def gain(k, shape):
        return 1.0 + 0.01 * jax.random.normal(k, shape, jnp.float32)

    return {
        "x": nrm(ks[0], (BATCH, SEQ, D_MODEL), 1.0),
        "mem": nrm(ks[1], (BATCH, N_MEM, D_MODEL), 1.0),
        "norm_mix_g": gain(ks[2], (DEPTH_2, D_MODEL)),
        "w_in": nrm(ks[3], (DEPTH_2, D_MODEL, IN_COLS), D_MODEL ** -0.5),
        "moba_w_proj": nrm(ks[4], (DEPTH_2, MOBA_WIDTH, D_MODEL), MOBA_WIDTH ** -0.5),
        "gmlp_norm_g": gain(ks[5], (DEPTH_2, GMLP_WIDTH)),
        "gmlp_w_s": nrm(ks[6], (DEPTH_2, GMLP_GROUPS, GMLP_CHUNK, GMLP_CHUNK), GMLP_CHUNK ** -0.5),
        "gmlp_b_s": 1.0 + 0.1 * jax.random.normal(ks[7], (DEPTH_2, GMLP_GROUPS, GMLP_CHUNK), jnp.float32),
        "gmlp_w_proj": nrm(ks[8], (DEPTH_2, GMLP_WIDTH, D_MODEL), GMLP_WIDTH ** -0.5),
        "w_out": nrm(ks[9], (DEPTH_2, D_MODEL, D_MODEL), D_MODEL ** -0.5),
        "norm_xa_g": gain(ks[10], (DEPTH_2, D_MODEL)),
        "norm_mem_g": gain(ks[11], (DEPTH_2, D_MODEL)),
        "xa_w_q": nrm(ks[12], (DEPTH_2, D_MODEL, XA_WIDTH), D_MODEL ** -0.5),
        "xa_w_kv": nrm(ks[13], (DEPTH_2, D_MODEL, 2 * XA_WIDTH), D_MODEL ** -0.5),
        "xa_w_o": nrm(ks[14], (DEPTH_2, XA_WIDTH, D_MODEL), XA_WIDTH ** -0.5),
        "norm_ffn_g": gain(ks[15], (DEPTH_2, D_MODEL)),
        "peer_w_q": nrm(ks[16], (DEPTH_2, D_MODEL, PEER_HEADS * PEER_DQ), D_MODEL ** -0.5),
        "peer_subkeys": nrm(ks[17], (DEPTH_2, PEER_HEADS, 2, PEER_NKEYS, PEER_DQ // 2), (PEER_DQ // 2) ** -0.5),
        "peer_w_down": nrm(ks[18], (DEPTH_2, PEER_N, D_MODEL), D_MODEL ** -0.5),
        "peer_w_up": nrm(ks[19], (DEPTH_2, PEER_N, D_MODEL), 0.3),
        "final_g": gain(ks[20], (D_MODEL,)),
    }

def second_block(x, mem, norm_mix_g, w_in, moba_w_proj, gmlp_norm_g, gmlp_w_s, gmlp_b_s,
              gmlp_w_proj, w_out, norm_xa_g, norm_mem_g, xa_w_q, xa_w_kv, xa_w_o,
              norm_ffn_g, peer_w_q, peer_subkeys, peer_w_down, peer_w_up, final_g):
    B, S, _ = x.shape
    splits = list(np.cumsum([MOBA_WIDTH, MOBA_WIDTH, MOBA_WIDTH, GMLP_WIDTH, GMLP_WIDTH, D_MODEL]))
    for l in range(DEPTH_2):
        h = rmsnorm(x, norm_mix_g[l])
        proj = h @ w_in[l]
        q, k, v, gu, gv, gate_a, gate_b = jnp.split(proj, splits, axis=-1)
        q = rope(q.reshape(B, S, MOBA_HEADS, MOBA_HD))
        k = rope(k.reshape(B, S, MOBA_HEADS, MOBA_HD))
        v = v.reshape(B, S, MOBA_HEADS, MOBA_HD)
        y_a = moba_attention(q, k, v) @ moba_w_proj[l]
        y_b = gmlp_spatial_gating(gu, gv, gmlp_norm_g[l], gmlp_w_s[l], gmlp_b_s[l]) @ gmlp_w_proj[l]
        merged = jax.nn.sigmoid(gate_a) * y_a + jax.nn.sigmoid(gate_b) * y_b
        x = x + merged @ w_out[l]
        h = rmsnorm(x, norm_xa_g[l])
        m = rmsnorm(mem, norm_mem_g[l])
        x = x + memory_cross_attention(h, m, xa_w_q[l], xa_w_kv[l], xa_w_o[l])
        h = rmsnorm(x, norm_ffn_g[l])
        x = x + peer_ffn(h, peer_w_q[l], peer_subkeys[l], peer_w_down[l], peer_w_up[l])
    return rmsnorm(x, final_g)


def setup_inputs(seed=0):
    out = dict(first_inputs(seed))
    for name, value in second_inputs(seed + 1).items():
        if name != "x":
            out[name + "_2"] = value
    return out


def reference(
    x, p, ffa_norm, ffa_w_gate_up, ffa_w_down, mix_norm, ffb_norm, ffb_w_gate_up, ffb_w_down,
    ple_norm, ple_w_gate, ple_w_proj, ev_w_in, ev_sinks, ev_cq_norm, ev_w_uq, ev_ckv_norm,
    ev_w_ukv, ev_w_out, od_w_in, od_b_f, od_w_out, final_norm, mem_2, norm_mix_g_2, w_in_2,
    moba_w_proj_2, gmlp_norm_g_2, gmlp_w_s_2, gmlp_b_s_2, gmlp_w_proj_2, w_out_2, norm_xa_g_2,
    norm_mem_g_2, xa_w_q_2, xa_w_kv_2, xa_w_o_2, norm_ffn_g_2, peer_w_q_2, peer_subkeys_2,
    peer_w_down_2, peer_w_up_2, final_g_2,
):
    x = first_block(
        x, p, ffa_norm, ffa_w_gate_up, ffa_w_down, mix_norm, ffb_norm, ffb_w_gate_up,
        ffb_w_down, ple_norm, ple_w_gate, ple_w_proj, ev_w_in, ev_sinks, ev_cq_norm, ev_w_uq,
        ev_ckv_norm, ev_w_ukv, ev_w_out, od_w_in, od_b_f, od_w_out, final_norm,
    )
    return second_block(
        x, mem_2, norm_mix_g_2, w_in_2, moba_w_proj_2, gmlp_norm_g_2, gmlp_w_s_2, gmlp_b_s_2,
        gmlp_w_proj_2, w_out_2, norm_xa_g_2, norm_mem_g_2, xa_w_q_2, xa_w_kv_2, xa_w_o_2,
        norm_ffn_g_2, peer_w_q_2, peer_subkeys_2, peer_w_down_2, peer_w_up_2, final_g_2,
    )


_drawn_inputs = setup_inputs


def setup_inputs(seed=0):
    import zlib

    import numpy as np

    out = dict(_drawn_inputs(seed))
    spreads = {}
    factors = {'ple_norm': 2.811,
     'ev_sinks': 3.7,
     'ev_cq_norm': 4.412,
     'ev_ckv_norm': 3.123,
     'norm_mix_g_2': 4.866,
     'gmlp_norm_g_2': 8.0,
     'norm_xa_g_2': 8.0,
     'norm_mem_g_2': 8.0,
     'norm_ffn_g_2': 30.88,
     'final_g_2': 31.968}
    for name, (base, spread) in spreads.items():
        noise = np.random.default_rng([zlib.crc32(name.encode()), seed]).standard_normal(out[name].shape)
        drawn = base * np.exp(spread * noise) if base else spread * noise
        out[name] = __import__('jax').numpy.asarray(drawn.astype(out[name].dtype))
    for name, factor in factors.items():
        out[name] = (out[name] * factor).astype(out[name].dtype)
    return out
```

```python
from contextlib import ExitStack, contextmanager

import concourse.bass as bass
from concourse import mybir
import numpy as np

F32 = mybir.dt.float32
F32R = mybir.dt.float32r
U32 = mybir.dt.uint32
ACT = mybir.ActivationFunctionType
ALU = mybir.AluOpType
AX = mybir.AxisListType.X

P = 128
T, D = 256, 1024
NT, KC = T // P, D // P
BLK, UB = 512, 4
FF, FC = 2816, 256
NFC = FF // FC
DEPTH = 2
EPS = 1e-6
HEADS_A, KV_A, DA = 8, 2, 64
HEADS_B, NOPE, ROPE_B, DVB = 8, 64, 32, 64
QLORA, KVLORA = 256, 128
HEADS_C, DC = 16, 64
HEADS_M, DM = 8, 64
G_GRP, G_W = 8, 512
HEADS_X, DX = 4, 128
HEADS_P, NKEYS, TOPK = 8, 128, 16
NEG = -1e30
JH = NKEYS // 2
EC = 4
RING = 3
LEAD = 2


def units(k, n, width=BLK):
    return -(-(k // P) * -(-n // width) // UB)


def stream_plan():
    ffn = NFC * 3
    plan = []
    for l in range(DEPTH):
        plan.append((f"ffa{l}", ffn))
        if l == 0:
            plan += [("ev_in", 6), ("uq", 1), ("ukv", 1), ("ev_out", units(D, D))]
        else:
            plan += [("od_in", units(D, 3 * D)), ("od_out", units(D, D))]
        plan += [(f"ffb{l}", ffn), (f"ple_gate{l}", units(D, D)), (f"ple_proj{l}", 1)]
    plan += [("in2", units(D, 4608)), ("moba", units(512, D)), ("gmlp", units(512, D)),
             ("out2", units(D, D)), ("xkv", units(D, D)), ("xq", units(D, 512)), ("xo", units(512, D)),
             ("peer_q", units(D, 2048)), ("peer", NKEYS // EC * 4)]
    return plan


N_UNITS = sum(n for _, n in stream_plan())

def columns(items):
    at, out = 0, {}
    for name, n in items:
        out[name] = (at, n)
        at += n
    return out, at


GAINS, N_GAINS = columns(
    [(f"{n}{l}", KC) for l in range(DEPTH) for n in ("ffa", "mix", "ffb", "ple")]
    + [("cq", QLORA // P), ("ckv", 1), ("mix2", KC), ("xa", KC), ("mem", KC), ("ffn", KC), ("bs", G_GRP)])
CONSTS, N_CONSTS = columns(
    [("ident", P), ("causal", T), ("trig_b", NT * 2 * (ROPE_B // 2)), ("trig_m", NT * 2 * (DM // 2)),
     ("upto", NT * T), ("iota", NKEYS), ("eps", 1), ("tri", P)])


def constants():
    c = np.zeros((P, N_CONSTS), np.float32)

    def put(name, a):
        at, n = CONSTS[name]
        c[:, at:at + n] = a.reshape(P, n)

    r = np.arange(P)
    put("ident", np.eye(P))
    put("causal", np.concatenate([np.zeros((P, P)), np.where(r[None, :] <= r[:, None], 0, NEG)], 1))
    for name, dim in (("trig_b", ROPE_B), ("trig_m", DM)):
        inv = np.float32(10000.0) ** (-np.arange(0, dim, 2, dtype=np.float32) / np.float32(dim))
        ang = (np.arange(T, dtype=np.float32)[:, None] * inv[None, :].astype(np.float32)).astype(np.float64)
        tab = np.stack([np.cos(ang), np.sin(ang)], 1)
        put(name, tab.reshape(NT, P, 2, dim // 2).transpose(1, 0, 2, 3))
    s = np.arange(T).reshape(NT, P)
    put("upto", (s[:, :, None] <= np.arange(T)[None, None, :]).transpose(1, 0, 2))
    put("iota", np.tile(np.arange(NKEYS), (P, 1)))
    put("eps", np.full((P, 1), EPS))
    put("tri", r[:, None] <= r[None, :])
    slopes = 2.0 ** (-8.0 * np.arange(1, HEADS_A + 1) / HEADS_A)
    dist = r[:, None] + P - np.arange(2 * P)[None, :]
    band = (dist >= 0) & (dist < P)
    alibi = np.where(band[:, None, :], -slopes[None, :, None] * dist[:, None, :], NEG)
    pick = np.zeros((HEADS_C, HEADS_C, P), np.float32)
    for h in range(HEADS_C):
        pick[h, h] = -1.0
    return c, alibi.reshape(P, -1).astype(np.float32), pick.reshape(HEADS_C, -1)


class Ticket:

    def __init__(self, sem, value):
        self.sem, self.value = sem, value


class Program:
    def __init__(self):
        self.engines, self.made = [], None
        self.counts = {}

    def count(self, key, by):
        self.counts[key] = self.counts.get(key, 0) + by
        return self.counts[key]

    def ticket(self, sem, by):
        t = Ticket(sem, self.count(sem, by))
        if self.made is not None:
            self.made.append(t)
        return t

    @contextmanager
    def loop(self, n):
        before = dict(self.counts)
        outer = [e.items for e in self.engines]
        for e in self.engines:
            e.items, e.seen = [], {}
        self.made = []
        yield
        step = {k: v - before.get(k, 0) for k, v in self.counts.items()}
        for e, items in zip(self.engines, outer):
            body, e.items, e.seen = e.items, items, {}
            if body:
                e.items.append((n, body, step))
        for k, v in step.items():
            self.counts[k] += v * (n - 1)
        for t in self.made:
            t.value += step[t.sem] * (n - 1)
        self.made = None


class Engine:
    def __init__(self, program, sem):
        self.program, self.sem, self.items, self.seen = program, sem, [], {}
        program.engines.append(self)

    def wait(self, *tickets):
        for t in tickets:
            if t is not None and self.seen.get(t.sem, 0) < t.value:
                self.seen[t.sem] = t.value
                self.items.append(lambda e, now, s=t.sem, v=t.value: e.wait_ge(s, now(v, s)))

    def do(self, emit, *waits):
        self.wait(*waits)
        self.items.append(lambda e, now: emit(e, now).then_inc(self.sem, 1))
        return self.program.ticket(self.sem, 1)

    def put(self, emit, *waits):
        self.wait(*waits)
        self.items.append(emit)

    def load(self, sem, emit, *waits):
        self.wait(*waits)
        self.items.append(lambda e, now: emit(e, now).then_inc(sem, 16))
        return self.program.ticket(sem, 16)

    def load_dynamic(self, sem, address, emit, wait):
        need = (wait.sem, wait.value) if wait is not None else None

        def both(e, now):
            at = address(now)
            at = at if isinstance(at, int) else e.snap(at)
            if need is not None:
                count = now(need[1], need[0])
                e.wait_ge(need[0], count if isinstance(count, int) else e.snap(count))
            emit(e, at).then_inc(sem, 16)
        self.items.append(both)
        return self.program.ticket(sem, 16)

    def run(self, e):
        def emit(items, now):
            for item in items:
                if isinstance(item, tuple):
                    n, body, step = item
                    with e.Fori(0, n) as i:
                        emit(body, lambda v, k: v + i * step[k] if step.get(k) else v)
                else:
                    item(e, now)
        emit(self.items, lambda v, k: v)


def build(nc, a, stop=None):
    with ExitStack() as ctx:
        def sb(name, cols, dt=F32):
            return ctx.enter_context(nc.sbuf_tensor(name, [P] + list(cols), dt))

        def sem(name):
            return ctx.enter_context(nc.semaphore(name))

        g = Program()
        pe, act, dve = Engine(g, sem("pe_done")), Engine(g, sem("act_done")), Engine(g, sem("dve_done"))
        pool, sp = Engine(g, sem("pool_done")), Engine(g, sem("sp_done"))

        raw = sb("raw", [RING, UB, BLK])
        w_hi, w_lo = sb("w_hi", [RING, UB, BLK], F32R), sb("w_lo", [RING, UB, BLK], F32R)
        h = sb("h", [NT, D])
        x_hi, x_lo = sb("x_hi", [KC, T], F32R), sb("x_lo", [KC, T], F32R)
        a_hi, a_lo = sb("a_hi", [EC, T], F32R), sb("a_lo", [EC, T], F32R)
        mid = sb("mid", [NT, BLK])
        gated = sb("gated", [EC, T])
        gains, consts = sb("gains_sb", [N_GAINS]), sb("consts_sb", [N_CONSTS])
        small = sb("small", [128])
        arena = sb("arena", [17408])
        bank = [ctx.enter_context(nc.psum_tensor(f"bank{b}", [P, BLK], F32)) for b in range(8)]

        def const(name):
            at, n = CONSTS[name]
            return consts[:, at:at + n]

        def gain(name, k):
            return gains[:, GAINS[name][0] + k:GAINS[name][0] + k + 1]

        ident, eps = const("ident"), const("eps")

        s_small = sem("small_loads")

        def small_load(dst, src, *waits):
            t = pool.load(s_small, lambda e, now: e.dma_start(dst, src), *waits)
            pool.wait(t)
            return t

        s_first = [sem(f"first_load{i}") for i in range(3)]
        got_h = sp.load(s_first[0], lambda e, now: e.dma_start(h[:, :, :], a["x"].rearrange("(t p) d -> p t d", p=P)))
        got_consts = sp.load(s_first[1], lambda e, now: e.dma_start(consts[:, :], a["consts"]))
        got_gains = sp.load(s_first[2], lambda e, now: e.dma_start(gains[:, :], a["gains"]))

        s_raw = [sem(f"unit_loaded{i}") for i in range(RING)]
        loaded, split, used = {}, {}, [None] * RING
        raw_read = [(None,)] * RING

        def load_unit():
            u = g.count("loaded", 1) - 1
            if u >= N_UNITS:
                return
            s = u % RING
            loaded[s] = sp.load_dynamic(
                s_raw[s], lambda now: now(u, "loaded") * (P * UB * BLK),
                lambda e, at: e.dma_start(raw[:, s, :, :].rearrange("p b n -> p (b n)"),
                                          a["w"][bass.ds(at, P * UB * BLK)].rearrange("(p n) -> p n", p=P)),
                *raw_read[s])

        def split_unit():
            u = g.count("split", 1) - 1
            if u >= N_UNITS:
                return
            s = u % RING
            hi = act.do(lambda e, now: e.activation(w_hi[:, s, :, :], raw[:, s, :, :], ACT.Copy),
                        loaded[s], used[s])
            lo = dve.do(lambda e, now: e.tensor_tensor(w_lo[:, s, :, :], raw[:, s, :, :],
                                                       w_hi[:, s, :, :].bitcast(F32), ALU.subtract),
                        loaded[s], used[s], hi)
            split[s] = (hi, lo)
            raw_read[s] = (lo,)

        def take_unit():
            u = g.count("taken", 1) - 1
            split_unit()
            load_unit()
            pe.wait(*split[u % RING])
            return u % RING

        for _ in range(RING):
            load_unit()
        for _ in range(LEAD):
            split_unit()
            load_unit()

        def product(out, s, b, width, hi, lo, start, stop):
            for n, (l, w) in enumerate(((hi, w_hi), (hi, w_lo), (lo, w_hi))):
                pe.put(lambda e, now, n=n, l=l, w=w: e.matmul(
                    out, l, w[:, s, b, 0:width], start=start and n == 0, stop=stop and n == 2))

        def signal_pe(emit, *waits):
            return pe.do(emit, *waits)

        def mark_last_pe():
            last = pe.items.pop()
            pe.items.append(lambda e, now: last(e, now).then_inc(pe.sem, 1))
            return g.ticket(pe.sem, 1)

        free = [[] for _ in range(8)]

        def transpose_to(out, src, *waits):
            pe.put(lambda e, now: e.transpose(out, src, ident[0:src.shape[0], 0:src.shape[0]]), *waits)

        def lift(src, chunks, gain_of, hi, lo, ready, banks=(0, 1, 2, 3)):
            done = []
            for k0 in range(0, chunks, 2):
                b = banks[(k0 // 2) % len(banks)]
                pe.wait(*free[b])
                ks = range(k0, min(k0 + 2, chunks))
                for k in ks:
                    for t in range(NT):
                        at = (k - k0) * T + t * P
                        transpose_to(bank[b][:, at:at + P], src(t, k), *ready)
                turned = mark_last_pe()
                readers = []
                for k in ks:
                    part = bank[b][:, (k - k0) * T:(k - k0 + 1) * T]
                    scale = gain_of(k) if gain_of else 1.0
                    up = act.do(lambda e, now, k=k, part=part, scale=scale: e.activation(
                        hi[:, k, :], part, ACT.Copy, scale=scale), turned)
                    readers.append(up)
                for k in ks:
                    part = bank[b][:, (k - k0) * T:(k - k0 + 1) * T]
                    if gain_of:
                        down = dve.do(lambda e, now, k=k, part=part, scale=gain_of(k): e.scalar_tensor_tensor(
                            lo[:, k, :], part, scale, hi[:, k, :].bitcast(F32), ALU.mult, ALU.subtract), up)
                    else:
                        down = dve.do(lambda e, now, k=k, part=part: e.tensor_tensor(
                            lo[:, k, :], part, hi[:, k, :].bitcast(F32), ALU.subtract), up)
                    readers.append(down)
                free[b] = readers
                done += readers
            return done

        square, ss_col, std_col, rstd_col = mid, 0, 2, 4

        def inv_rms(src, width, ready, col=0):
            junk = gated[:, :, :].rearrange("p a b -> p (a b)")
            sums = []
            for t in range(NT):
                sums.append(act.do(lambda e, now, t=t: e.activation(
                    junk[:, 0:width], src(t), ACT.Square, accum_out=small[:, col + t:col + t + 1]),
                    *ready, *sums[-1:], *junk_free))
            junk_free[:] = sums[-1:]
            root = act.do(lambda e, now: e.activation(small[:, col + 2:col + 4], small[:, col:col + 2], ACT.Sqrt,
                                                      bias=eps, scale=1.0 / width), sums[-1])
            return dve.do(lambda e, now: e.reciprocal(small[:, col + 4:col + 6], small[:, col + 2:col + 4]), root)

        junk_free = []

        def rstd(t, col=0):
            return small[:, col + 4 + t:col + 5 + t]

        def project(hi, lo, chunks, blocks, width, ready, leave, banks=(0, 1, 2, 3, 4, 5)):
            pe.wait(*ready)
            slot = None
            for n in range(blocks):
                w = width[n] if isinstance(width, (list, tuple)) else width
                pair = banks[2 * n % len(banks)], banks[(2 * n + 1) % len(banks)]
                for b in pair:
                    pe.wait(*free[b])
                done = [None] * NT
                for k0 in range(0, chunks, UB):
                    ks = range(k0, min(k0 + UB, chunks))
                    first = n * chunks + k0
                    if first % UB == 0:
                        slot = take_unit()
                    for t in range(NT):
                        for k in ks:
                            product(bank[pair[t]][:, 0:w], slot, (n * chunks + k) % UB, w,
                                    hi[:, k, t * P:(t + 1) * P], lo[:, k, t * P:(t + 1) * P],
                                    k == 0, k == chunks - 1)
                        done[t] = mark_last_pe()
                    used[slot] = done[NT - 1]
                for t in range(NT):
                    free[pair[t]] = leave(n, t, bank[pair[t]][:, 0:w], done[t])

        ACC, GU, TR = (0, 1, 2, 3), (4, 5), (6, 7)

        class Gated:

            def __init__(self, nf, activate, turn, x_ready, first=True):
                self.nf, self.activate, self.turn, self.first = nf, activate, turn, first
                self.a_ready, self.down_done = [], None
                pe.wait(*x_ready)
                for b in ACC:
                    pe.wait(*free[b])

            def down(self, last=False):
                pe.wait(*self.a_ready)
                per = UB // 2
                for f0 in range(0, self.nf, per):
                    s = take_unit()
                    for f in range(f0, f0 + per):
                        for t in range(NT):
                            for half in range(2):
                                product(bank[2 * t + half][:, :], s, 2 * (f - f0) + half, BLK,
                                        a_hi[:, f, t * P:(t + 1) * P], a_lo[:, f, t * P:(t + 1) * P],
                                        self.first and f == 0, last and f == self.nf - 1)
                    used[s] = self.down_done = mark_last_pe()
                self.first = False

            def chunk(self, c, with_down=True):
                for b in GU:
                    pe.wait(*free[b])
                for u in range(2):
                    s = take_unit()
                    done = []
                    for t in range(NT):
                        for k in range(UB):
                            kk = u * UB + k
                            product(bank[GU[t]][:, :], s, k, BLK, x_hi[:, kk, t * P:(t + 1) * P],
                                    x_lo[:, kk, t * P:(t + 1) * P], kk == 0, kk == KC - 1)
                        done.append(mark_last_pe())
                    used[s] = done[-1]
                ready = []
                for t in range(NT):
                    readers, r = self.activate(c, t, bank[GU[t]], done[t], self.turned)
                    free[GU[t]] = readers
                    ready += r
                if with_down:
                    self.down()
                pe.wait(*ready)
                for b in range(self.nf // 2):
                    pe.wait(*free[TR[b]])
                    for f in (2 * b, 2 * b + 1):
                        for t in range(NT):
                            at = (f % 2) * T + t * P
                            transpose_to(bank[TR[b]][:, at:at + P], mid[:, t, f * P:(f + 1) * P])
                    self.turned = mark_last_pe()
                    free[TR[b]], r = self.turn(c, b, bank[TR[b]], self.turned, self.down_done)
                    self.a_ready = r if b == 0 else self.a_ready + r

            turned = None

        def split_a(b, src, done, *waits):
            hi = act.do(lambda e, now: e.activation(a_hi[:, 2 * b:2 * b + 2, :].rearrange("p f t -> p (f t)"),
                                                    src, ACT.Copy), done, *waits)
            lo = dve.do(lambda e, now: e.tensor_tensor(
                a_lo[:, 2 * b:2 * b + 2, :].rearrange("p f t -> p (f t)"), src,
                a_hi[:, 2 * b:2 * b + 2, :].rearrange("p f t -> p (f t)").bitcast(F32), ALU.subtract), hi)
            return [hi, lo]

        def add_to_h(scale, done, ready):
            out = []
            for t in range(NT):
                for half in range(2):
                    cols = h[:, t, half * BLK:(half + 1) * BLK]
                    b = 2 * t + half
                    r = dve.do(lambda e, now, b=b, cols=cols: e.scalar_tensor_tensor(
                        cols, bank[b][:, :], scale, cols, ALU.mult, ALU.add), done, *ready)
                    free[b] = [r]
                    out.append(r)
            return out

        h_tile = lambda t: h[:, t, :]
        h_chunk = lambda t, k: h[:, t, k * P:(k + 1) * P]

        def ffn(name, h_ready):
            x_ready = lift(h_chunk, KC, lambda k: gain(name, k), x_hi, x_lo, h_ready)
            scaled = inv_rms(h_tile, D, h_ready)
            dve.wait(scaled)
            act.wait(scaled)

            def activate(c, t, psum, done, turned):
                silu = act.do(lambda e, now: e.activation(gated[:, t, :], psum[:, 0:FC], ACT.Silu, scale=rstd(t)),
                              done, turned)
                both = dve.do(lambda e, now: e.scalar_tensor_tensor(
                    mid[:, t, 0:FC], psum[:, FC:2 * FC], rstd(t), gated[:, t, :], ALU.mult, ALU.mult), done, silu)
                return [silu, both], [both]

            def turn(c, b, psum, turned, down_done):
                both = split_a(b, psum[:, :], turned, down_done)
                return both, both

            p = Gated(2, activate, turn, x_ready)
            p.chunk(0, with_down=False)
            p.chunk(1)
            with g.loop(NFC - 2):
                p.chunk(2)
            p.down(last=True)
            return add_to_h(0.5, p.down_done, h_ready), p

        def view(at, *dims):
            n = int(np.prod(dims))
            flat = arena[:, at:at + n]
            if len(dims) == 1:
                return flat
            names = "abcd"[:len(dims)]
            return flat.rearrange(f"p ({' '.join(names)}) -> p {' '.join(names)}",
                                  **{x: d for x, d in zip(names[1:], dims[1:])})

        def turn(src, rows, n, dst, ready, scale=1.0, banks=(0, 1, 2, 3)):
            done = []
            for i0 in range(0, n, 2):
                b = banks[(i0 // 2) % len(banks)]
                pe.wait(*free[b], *ready)
                pair = range(i0, min(i0 + 2, n))
                for i in pair:
                    for t in range(NT):
                        at = (i - i0) * T + t * P
                        transpose_to(bank[b][0:rows, at:at + P], src(t, i))
                turned = mark_last_pe()
                readers = []
                for r0, r1, c0, c1, place in dst(i0, len(pair)):
                    readers.append(act.do(lambda e, now, b=b, r0=r0, r1=r1, c0=c0, c1=c1, place=place: e.activation(
                        place, bank[b][r0:r1, c0:c1], ACT.Copy, scale=scale), turned))
                free[b] = readers[-1:]
                done += readers[-1:]
            return done

        def whole(dst, rows=P):
            return lambda i, m: [(0, rows, 0, m * T, dst[0:rows, i:i + m, :].rearrange("p a b -> p (a b)"))]

        def halves(dst, top, bottom):
            def places(i, m):
                out = []
                for j in range(m):
                    out.append((0, 64, j * T, (j + 1) * T, dst[0:64, top(i + j), :]))
                    out.append((64, P, j * T, (j + 1) * T, dst[64:P, bottom(i + j), :]))
                return out
            return places

        def scale_out(n, t, psum, done, place, col=0):
            if t == 0:
                r = act.do(lambda e, now: e.activation(place, psum, ACT.Copy, scale=rstd(t, col)), done)
            else:
                r = dve.do(lambda e, now: e.tensor_scalar(place, psum, rstd(t, col), None, ALU.mult), done)
            return r

        def add_out(n, t, psum, done):
            cols = h[:, t, n * BLK:(n + 1) * BLK]
            r = dve.do(lambda e, now: e.tensor_tensor(cols, psum, cols, ALU.add), done)
            h_parts.append(r)
            return [r]

        h_parts = []

        stat = sb("stat", [5, 2 * HEADS_C])

        def attention(heads, dv, keys, q, k, v, bias, out, ready, at, sink=None, gate=None):
            sc, ex, ext = (view(at + 2 * i * BLK, 2, BLK) for i in range(3))
            steps = [(n, h0) for n in range(NT) for h0 in range(0, heads, 2)]
            sums, exts, copies, values, outs = {}, {}, {}, {}, {}
            pe.wait(*ready)
            dve.wait(*ready)

            def col(i, s):
                return stat[:, i, 2 * (s % HEADS_C):2 * (s % HEADS_C) + 2]

            for s in range(len(steps) + 2):
                if s < len(steps):
                    n, h0 = steps[s]
                    nk = len(keys(n)) * P
                    k0 = keys(n)[0] * P
                    b = s % 2
                    pe.wait(*free[b])
                    for j in range(2):
                        psum = bank[b][:, j * nk:(j + 1) * nk]
                        pe.put(lambda e, now, psum=psum, n=n, hd=h0 + j, k0=k0, nk=nk: e.matmul(
                            psum, q(hd, n), k(hd)[:, k0:k0 + nk], start=True, stop=gate is None))
                        if gate is not None:
                            pe.put(lambda e, now, psum=psum, hd=h0 + j, k0=k0, nk=nk: e.matmul(
                                psum, gate[0](hd), gate[1][:, k0:k0 + nk], start=False, stop=True))
                    scored = mark_last_pe()
                if 1 <= s <= len(steps):
                    r = s - 1
                    rn, _ = steps[r]
                    m = 2 * len(keys(rn))
                    b = 2 + r % 2
                    pe.wait(*free[b], sums[r])
                    for j in range(m):
                        transpose_to(bank[b][:, j * P:(j + 1) * P], ex[:, r % 2, j * P:(j + 1) * P])
                    turned = mark_last_pe()
                    copies[r] = act.do(lambda e, now, b=b, r=r, m=m: e.activation(
                        ext[:, r % 2, 0:m * P], bank[b][:, 0:m * P], ACT.Copy), turned, values.get(r - 2))
                    free[b] = [copies[r]]
                if s >= 2:
                    r = s - 2
                    rn, rh = steps[r]
                    tiles = keys(rn)
                    b = 4 + r % 2
                    pe.wait(*free[b], copies[r])
                    for j in range(2):
                        for i, tile in enumerate(tiles):
                            pe.put(lambda e, now, b=b, j=j, i=i, tile=tile, r=r, rh=rh, m=len(tiles): e.matmul(
                                bank[b][:, j * dv:(j + 1) * dv],
                                ext[:, r % 2, (j * m + i) * P:(j * m + i + 1) * P], v(rh + j, tile),
                                start=i == 0, stop=i == m - 1))
                    values[r] = mark_last_pe()
                if s < len(steps):
                    b = s % 2
                    scores = bank[b][:, 0:2 * nk].rearrange("p (a b) -> p a b", a=2)
                    soft = sc[:, b, 0:2 * nk].rearrange("p (a b) -> p a b", a=2)
                    if bias is None:
                        soft, biased = scores, scored
                    elif gate is not None:
                        for j in range(2):
                            biased = dve.do(lambda e, now, j=j, n=n, h0=h0, soft=soft, scores=scores: e.scalar_tensor_tensor(
                                soft[:, j, :], scores[:, j, :], gate[2](h0 + j, n), bias(n, h0)[:, j, :],
                                ALU.add, ALU.add), scored, sums.get(s - 2))
                    else:
                        biased = dve.do(lambda e, now, n=n, h0=h0, soft=soft, scores=scores: e.tensor_tensor(
                            soft, scores, bias(n, h0), ALU.add), scored, sums.get(s - 2))
                    top = dve.do(lambda e, now, s=s, soft=soft: e.reduce_max(col(0, s), soft, AX), biased)
                    if sink is not None:
                        top = dve.do(lambda e, now, s=s, h0=h0: e.tensor_tensor(
                            col(0, s), col(0, s), sink[:, h0:h0 + 2], ALU.max), top)
                        gap = dve.do(lambda e, now, s=s, h0=h0: e.tensor_tensor(
                            col(3, s), sink[:, h0:h0 + 2], col(0, s), ALU.subtract), top)
                    low = dve.do(lambda e, now, s=s: e.tensor_scalar(col(1, s), col(0, s), -1.0, None, ALU.mult), top)
                if s >= 2:
                    r = s - 2
                    rn, rh = steps[r]
                    total = sums[r]
                    if sink is not None:
                        total = dve.do(lambda e, now, r=r: e.tensor_tensor(col(2, r), col(2, r), col(3, r), ALU.add), total)
                    inv = dve.do(lambda e, now, r=r: e.reciprocal(col(4, r), col(2, r)), total)
                    b = 4 + r % 2
                    outs[r] = dve.do(lambda e, now, b=b, r=r, rn=rn, rh=rh: e.tensor_tensor(
                        out(rn, rh), bank[b][:, 0:2 * dv].rearrange("p (a b) -> p a b", a=2),
                        col(4, r).unsqueeze(2).broadcast_to([P, 2, dv]), ALU.mult), inv, values[r])
                    free[b] = [outs[r]]
                if s < len(steps):
                    b = s % 2
                    if sink is not None:
                        act.do(lambda e, now, s=s: e.activation(col(3, s), col(3, s), ACT.Exp), gap, outs.get(s - HEADS_C))
                    for j in range(2):
                        sums[s] = act.do(lambda e, now, b=b, j=j, s=s, soft=soft, nk=nk: e.activation(
                            ex[:, b, j * nk:(j + 1) * nk], soft[:, j, :], ACT.Exp, bias=col(1, s)[:, j:j + 1],
                            accum_out=col(2, s)[:, j:j + 1]), low, copies.get(s - 2))
                    free[b] = [sums[s]] if bias is None else [biased]
            return [outs[len(steps) - 1]]

        def rotate(x1, x2, cos, sin, t1, t2, ready):
            a1 = dve.do(lambda e, now: e.tensor_tensor(t1, x1, sin, ALU.mult), *ready)
            a2 = dve.do(lambda e, now: e.tensor_tensor(t2, x2, sin, ALU.mult))
            b1 = dve.do(lambda e, now: e.tensor_tensor(x1, x1, cos, ALU.mult), a1)
            b2 = dve.do(lambda e, now: e.tensor_tensor(x2, x2, cos, ALU.mult), a2)
            dve.do(lambda e, now: e.tensor_tensor(x1, x1, t2, ALU.subtract), b1)
            return dve.do(lambda e, now: e.tensor_tensor(x2, x2, t1, ALU.add), b2)

        def causal(n, h0):
            mask = const("causal")
            mask = mask[:, P:T] if n == 0 else mask
            return mask.unsqueeze(1).broadcast_to([P, 2, (n + 1) * P])

        up_to = lambda n: list(range(n + 1))

        def trig(name, half, heads):
            tab = const(name).rearrange("p (t c f) -> p t c f", t=NT, c=2)
            return [tab[:, :, c, :].unsqueeze(2).broadcast_to([P, NT, heads, half]) for c in range(2)]

        def ple(l, h_ready):
            p_in, g_out = view(0, 2, T), view(512, NT, D)
            got = small_load(p_in, a[f"p{l}"], *h_ready)
            hi = act.do(lambda e, now: e.activation(a_hi[:, 0:2, :], p_in, ACT.Copy), got, *h_ready)
            lo = dve.do(lambda e, now: e.tensor_tensor(a_lo[:, 0:2, :], p_in, a_hi[:, 0:2, :].bitcast(F32),
                                                       ALU.subtract), hi)
            x_ready = lift(h_chunk, KC, lambda k: gain(f"ple{l}", k), x_hi, x_lo, h_ready)
            act.wait(inv_rms(h_tile, D, h_ready))
            gates = {}

            def gate(n, t, psum, done):
                gates[n, t] = act.do(lambda e, now: e.activation(
                    g_out[:, t, n * BLK:(n + 1) * BLK], psum, ACT.Sigmoid, scale=rstd(t)), done)
                return [gates[n, t]]

            project(x_hi, x_lo, KC, 2, BLK, x_ready, gate)
            out = []

            def leave(n, t, psum, done):
                g = g_out[:, t, n * BLK:(n + 1) * BLK]
                cols = h[:, t, n * BLK:(n + 1) * BLK]
                m = dve.do(lambda e, now: e.tensor_tensor(g, psum, g, ALU.mult), done, gates[n, t])
                out.append(dve.do(lambda e, now: e.tensor_tensor(cols, cols, g, ALU.add), m))
                return [m]

            project(a_hi, a_lo, 2, 2, BLK, [hi, lo], leave, banks=(4, 5, 0, 1))
            return out

        def norm_rows(row, h_ready, got):
            r = inv_rms(h_tile, D, h_ready)
            return [dve.do(lambda e, now, t=t: e.scalar_tensor_tensor(
                h[:, t, :], h[:, t, :], rstd(t), row, ALU.mult, ALU.mult), r, got) for t in range(NT)]

        def even_mixer(h_ready):
            N_IN = 1184
            pin = view(0, NT, N_IN)
            qt_a, kt_a = view(2400, HEADS_A, T), view(4448, 1, T)
            qb, kvb = view(4704, NT, HEADS_B * (NOPE + ROPE_B)), view(6240, NT, HEADS_B * (NOPE + DVB))
            kcat = view(8288, NT, HEADS_B, NOPE + ROPE_B)
            kt_b, mixed, bufs = view(9824, HEADS_B, T), view(11872, NT, D), 13920
            sinks = small[:, 64:64 + HEADS_A]
            table = onehot_i[:, :, :, :].rearrange("p a b c -> p (a b c)")
            alibi = table.rearrange("p (h k) -> p h k", h=HEADS_A)
            tmp = onehot_j[:, :, :, :].rearrange("p a b c -> p (a b c)")
            got_alibi = small_load(table, a["alibi"], *h_ready)
            got_sinks = small_load(sinks, a["sinks"].partition_broadcast(P))
            zeroed = pool.do(lambda e, now: e.memset(qt_a, 0.0), *h_ready)
            x_ready = lift(h_chunk, KC, lambda k: gain("mix0", k), x_hi, x_lo, h_ready)
            r = inv_rms(h_tile, D, h_ready)
            act.wait(r, zeroed)
            dve.wait(r)
            parts = []

            def leave(n, t, psum, done):
                w = min(BLK, N_IN - n * BLK)
                parts.append(scale_out(n, t, psum, done, pin[:, t, n * BLK:n * BLK + w]))
                return parts[-1:]

            project(x_hi, x_lo, KC, 3, [BLK, BLK, N_IN - 2 * BLK], x_ready, leave)
            cq = lambda t, k: pin[:, t, 768 + k * P:768 + (k + 1) * P]
            ckv = lambda t, k: pin[:, t, 1024:1152]
            l1 = lift(cq, 2, lambda k: gain("cq", k), x_hi, x_lo, parts)
            l2 = lift(ckv, 1, lambda k: gain("ckv", k), x_hi[:, 2:3, :], x_lo[:, 2:3, :], parts, banks=(1,))
            r1 = inv_rms(lambda t: pin[:, t, 768:1024], QLORA, parts, 8)
            r2 = inv_rms(lambda t: pin[:, t, 1024:1152], KVLORA, parts, 16)
            act.wait(r1, r2)
            dve.wait(r1, r2)
            parts_q, parts_kv = [], []

            def leave_q(n, t, psum, done):
                parts_q.append(scale_out(n, t, psum, done, qb[:, t, n * 384:(n + 1) * 384], 8))
                return parts_q[-1:]

            def leave_kv(n, t, psum, done):
                parts_kv.append(scale_out(n, t, psum, done, kvb[:, t, n * BLK:(n + 1) * BLK], 16))
                return parts_kv[-1:]

            project(x_hi, x_lo, 2, 2, 384, l1, leave_q)
            project(x_hi[:, 2:3, :], x_lo[:, 2:3, :], 1, 2, BLK, l2, leave_kv)
            ta = turn(lambda t, i: pin[:, t, i * P:(i + 1) * P], P, 4, halves(qt_a, lambda i: i, lambda i: i + 4),
                      parts, DA ** -0.5)
            tk = turn(lambda t, i: pin[:, t, 512:640], P, 1, whole(kt_a), parts, banks=(2,))
            done_a = attention(
                HEADS_A, DA, up_to, lambda hd, n: qt_a[:, hd, n * P:(n + 1) * P], lambda hd: kt_a[:, 0, :],
                lambda hd, t: pin[:, t, 640 + DA * (hd // 4):640 + DA * (hd // 4) + DA],
                lambda n, h0: alibi[:, h0:h0 + 2, (P if n == 0 else 0):T],
                lambda n, h0: mixed[:, n, h0 * DA:(h0 + 2) * DA].rearrange("p (a b) -> p a b", a=2),
                ta + tk + [got_alibi, got_sinks], bufs, sink=sinks)
            half = ROPE_B // 2
            q4 = qb.rearrange("p t (h d) -> p t h d", h=HEADS_B)
            t1, t2 = (tmp[:, i * 256:(i + 1) * 256].rearrange("p (t h f) -> p t h f", t=NT, h=HEADS_B) for i in range(2))
            cos, sin = trig("trig_b", half, HEADS_B)
            rq = rotate(q4[:, :, :, NOPE:NOPE + half], q4[:, :, :, NOPE + half:], cos, sin, t1, t2, parts_q + parts)
            k4 = pin[:, :, 1152:1184].unsqueeze(2)
            t3, t4 = (tmp[:, 512 + i * 32:512 + (i + 1) * 32].rearrange("p (t h f) -> p t h f", t=NT, h=1) for i in range(2))
            cos, sin = trig("trig_b", half, 1)
            rk = rotate(k4[:, :, :, 0:half], k4[:, :, :, half:], cos, sin, t3, t4, [])
            kv4 = kvb.rearrange("p t (h d) -> p t h d", h=HEADS_B)
            kc = dve.do(lambda e, now: e.tensor_copy(kcat[:, :, :, 0:NOPE], kv4[:, :, :, 0:NOPE]), *parts_kv)
            kr = [dve.do(lambda e, now, t=t: e.tensor_copy(
                kcat[:, t, :, NOPE:], pin[:, t, 1152:1184].unsqueeze(1).broadcast_to([P, HEADS_B, ROPE_B])), rk)
                for t in range(NT)]
            w = NOPE + ROPE_B
            tq = turn(lambda t, i: q4[:, t, i, :], w, HEADS_B, whole(qt_a, w), [rq], w ** -0.5)
            tk = turn(lambda t, i: kcat[:, t, i, :], w, HEADS_B, whole(kt_b, w), [kc] + kr)
            done_b = attention(
                HEADS_B, DVB, up_to, lambda hd, n: qt_a[0:w, hd, n * P:(n + 1) * P], lambda hd: kt_b[0:w, hd, :],
                lambda hd, t: kv4[:, t, hd, NOPE:], causal,
                lambda n, h0: mixed[:, n, 512 + h0 * DVB:512 + (h0 + 2) * DVB].rearrange("p (a b) -> p a b", a=2),
                tq + tk, bufs)
            x_ready = lift(lambda t, k: mixed[:, t, k * P:(k + 1) * P], KC, None, x_hi, x_lo, done_a + done_b)
            h_parts.clear()
            project(x_hi, x_lo, KC, 2, BLK, x_ready, add_out)
            return list(h_parts)

        def odd_mixer(h_ready):
            qkv = view(0, NT, 3 * D)
            qt, kt, mixed, bufs = view(6144, HEADS_C, T), view(10240, HEADS_C // 2, T), view(12288, NT, D), 14336
            pick = onehot_i[:, :, :, :].rearrange("p a b c -> p (a b c)").rearrange("p (h q) -> p h q", h=HEADS_C)
            tmp = onehot_j[:, :, :, :].rearrange("p a b c -> p (a b c)")
            f_raw = tmp[:, 0:128].rearrange("p (k f) -> p k f", k=KC)
            bf = tmp[:, 128:144]
            z, nz, lf = (tmp[:, 160 + i * 32:192 + i * 32].rearrange("p (t f) -> p t f", t=NT) for i in range(3))
            rows = tmp[:, 256:512]
            wide = tmp[:, 512:768].rearrange("p (t f) -> p t f", t=NT)
            at_q = tmp[:, 768:800].rearrange("p (t f) -> p t f", t=NT)
            got_pick = small_load(pick[0:HEADS_C, :, :], a["pick"].rearrange("p (h q) -> p h q", h=HEADS_C), *h_ready)
            got_f = small_load(f_raw, a["w_f"])
            got_b = small_load(bf, a["b_f"].partition_broadcast(P))
            zq = pool.do(lambda e, now: e.memset(qt, 0.0), *h_ready)
            zw = pool.do(lambda e, now: e.memset(wide, 0.0))
            x_ready = lift(h_chunk, KC, lambda k: gain("mix1", k), x_hi, x_lo, h_ready)
            r = inv_rms(h_tile, D, h_ready)
            act.wait(r, zq)
            dve.wait(r, zw)
            fh = act.do(lambda e, now: e.activation(f_hi[:, :, :], f_raw, ACT.Copy), got_f)
            fl = dve.do(lambda e, now: e.tensor_tensor(f_lo[:, :, :], f_raw, f_hi[:, :, :].bitcast(F32), ALU.subtract), fh)
            parts = []

            def leave(n, t, psum, done):
                parts.append(scale_out(n, t, psum, done, qkv[:, t, n * BLK:(n + 1) * BLK]))
                return parts[-1:]

            pe.wait(*x_ready, fh, fl, *free[6])
            for t in range(NT):
                for k in range(KC):
                    for i, (l, w) in enumerate(((x_hi, f_hi), (x_hi, f_lo), (x_lo, f_hi))):
                        pe.put(lambda e, now, t=t, k=k, l=l, w=w, i=i: e.matmul(
                            bank[6][:, t * 16:(t + 1) * 16], l[:, k, t * P:(t + 1) * P], w[:, k, :],
                            start=k == 0 and i == 0, stop=k == KC - 1 and i == 2))
            logits = mark_last_pe()
            for t in range(NT):
                zt = dve.do(lambda e, now, t=t: e.scalar_tensor_tensor(
                    z[:, t, :], bank[6][:, t * 16:(t + 1) * 16], rstd(t), bf, ALU.mult, ALU.add), logits, got_b)
            n1 = dve.do(lambda e, now: e.tensor_scalar(nz, z, -1.0, None, ALU.mult), zt)
            n2 = dve.do(lambda e, now: e.tensor_tensor(nz, z, nz, ALU.min), n1)
            e1 = act.do(lambda e, now: e.activation(lf, nz, ACT.Exp), n2)
            e2 = act.do(lambda e, now: e.activation(lf, lf, ACT.Ln, bias=1.0), e1)
            n3 = dve.do(lambda e, now: e.tensor_scalar(z, z, 0.0, None, ALU.min))
            n4 = dve.do(lambda e, now: e.tensor_tensor(lf, z, lf, ALU.subtract), n3, e2)
            n5 = dve.do(lambda e, now: e.tensor_copy(wide[:, :, 0:16], lf), n4)
            project(x_hi, x_lo, KC, 6, BLK, [], leave)
            upto = const("upto").rearrange("p (a t) -> p a t", a=NT)
            pe.wait(n5, *free[6], zt)
            for n in range(NT):
                for s in range(n + 1):
                    pe.put(lambda e, now, n=n, s=s: e.matmul(
                        bank[6][:, n * 16:(n + 1) * 16], upto[:, s, n * P:(n + 1) * P], lf[:, s, :],
                        start=s == 0, stop=s == n))
            m1 = mark_last_pe()
            pe.wait(*free[7])
            for s in range(NT):
                pe.put(lambda e, now, s=s: e.matmul(bank[7][:, 0:T], wide[:, s, :], upto[:, s, :],
                                                    start=s == 0, stop=s == NT - 1))
            m2 = mark_last_pe()
            c1 = dve.do(lambda e, now: e.tensor_copy(at_q, bank[6][:, 0:32].rearrange("p (t f) -> p t f", t=NT)), m1)
            c2 = dve.do(lambda e, now: e.tensor_copy(rows, bank[7][:, 0:T]), m2)
            free[6], free[7] = [c1], [c2]
            tq = turn(lambda t, i: qkv[:, t, i * P:(i + 1) * P], P, 8,
                      halves(qt, lambda i: 2 * i, lambda i: 2 * i + 1), parts, DC ** -0.5)
            tk = turn(lambda t, i: qkv[:, t, D + i * P:D + (i + 1) * P], P, 8, whole(kt), parts)
            done = attention(
                HEADS_C, DC, up_to, lambda hd, n: qt[:, hd, n * P:(n + 1) * P], lambda hd: kt[:, hd // 2, :],
                lambda hd, t: qkv[:, t, 2 * D + hd * DC:2 * D + (hd + 1) * DC], causal,
                lambda n, h0: mixed[:, n, h0 * DC:(h0 + 2) * DC].rearrange("p (a b) -> p a b", a=2),
                tq + tk + [c1, c2, got_pick], bufs,
                gate=(lambda hd: pick[0:HEADS_C, hd, :], rows[0:HEADS_C, :], lambda hd, n: at_q[:, n, hd:hd + 1]))
            x_ready = lift(lambda t, k: mixed[:, t, k * P:(k + 1) * P], KC, None, x_hi, x_lo, done)
            h_parts.clear()
            project(x_hi, x_lo, KC, 2, BLK, x_ready, add_out)
            return list(h_parts)

        def moba_gmlp(h_ready):
            qkv, gates = view(0, NT, 1536), view(3072, NT, 2 * D)
            uv = view(7168, NT, 2 * G_W)
            qt, kt = view(9216, HEADS_M, T), view(11264, HEADS_M // 2, T)
            ya, bufs = view(12288, NT, 512), 13312
            wm_t = onehot_i[:, :, :, :].rearrange("p a b c -> p (a b c)")
            wm = wm_t[:, 0:1024].rearrange("p (g t) -> p g t", g=G_GRP)
            row = wm_t[:, 1024:1536]
            got_w = small_load(wm, a["gmlp_w"], *h_ready)
            got_row = small_load(row, a["gmlp_g"].partition_broadcast(P))
            zq = pool.do(lambda e, now: e.memset(qt, 0.0), *h_ready)
            x_ready = lift(h_chunk, KC, lambda k: gain("mix2", k), x_hi, x_lo, h_ready)
            r = inv_rms(h_tile, D, h_ready)
            act.wait(r, zq)
            dve.wait(r)
            masked = dve.do(lambda e, now: e.tensor_tensor(
                wm, wm, const("tri").unsqueeze(1).broadcast_to([P, G_GRP, P]), ALU.mult), got_w)
            parts, uvs, gs = [], {}, {}

            def leave(n, t, psum, done):
                if n < 3:
                    parts.append(scale_out(n, t, psum, done, qkv[:, t, n * BLK:(n + 1) * BLK]))
                    return parts[-1:]
                place, func, at = (uv, ACT.Gelu_apprx_tanh, n - 3) if n < 5 else (gates, ACT.Sigmoid, n - 5)
                store = uvs if n < 5 else gs
                store[at, t] = act.do(lambda e, now: e.activation(
                    place[:, t, at * BLK:(at + 1) * BLK], psum, func, scale=rstd(t)), done)
                return [store[at, t]]

            project(x_hi, x_lo, KC, 9, BLK, x_ready, leave)
            qk = qkv[:, :, 0:1024].rearrange("p t (h d) -> p t h d", d=DM)
            cos, sin = trig("trig_m", DM // 2, 2 * HEADS_M)
            rot = rotate(qk[:, :, :, 0:32], qk[:, :, :, 32:64], cos, sin, 
                         view(bufs, NT, 16, 32), view(bufs + 1024, NT, 16, 32), parts)
            tq = turn(lambda t, i: qkv[:, t, i * P:(i + 1) * P], P, 4,
                      halves(qt, lambda i: 2 * i, lambda i: 2 * i + 1), [rot], DM ** -0.5)
            tk = turn(lambda t, i: qkv[:, t, 512 + i * P:512 + (i + 1) * P], P, 4, whole(kt), [rot])
            v_at = lambda t: uv[:, t, 512:1024]
            r = inv_rms(v_at, G_W, [uvs[1, 0], uvs[1, 1]], 24)
            vn = [dve.do(lambda e, now, t=t: e.scalar_tensor_tensor(
                v_at(t), v_at(t), rstd(t, 24), row, ALU.mult, ALU.mult), r, got_row) for t in range(NT)]
            uz = []
            for t in range(NT):
                pe.wait(*free[6 + t], vn[t], masked)
                for grp in range(G_GRP):
                    pe.put(lambda e, now, t=t, grp=grp: e.matmul(
                        bank[6 + t][:, grp * 64:(grp + 1) * 64], wm[:, grp, :],
                        uv[:, t, 512 + grp * 64:512 + (grp + 1) * 64], start=True, stop=True))
                m = mark_last_pe()
                at, _ = GAINS["bs"]
                z = dve.do(lambda e, now, t=t: e.tensor_tensor(
                    v_at(t).rearrange("p (g d) -> p g d", g=G_GRP),
                    bank[6 + t][:, :].rearrange("p (g d) -> p g d", g=G_GRP),
                    gains[:, at:at + G_GRP].unsqueeze(2).broadcast_to([P, G_GRP, 64]), ALU.add), m)
                uz.append(dve.do(lambda e, now, t=t: e.tensor_tensor(
                    uv[:, t, 0:512], uv[:, t, 0:512], v_at(t), ALU.mult), z, uvs[0, t]))
                free[6 + t] = [z]
            done = attention(
                HEADS_M, DM, up_to, lambda hd, n: qt[:, hd, n * P:(n + 1) * P], lambda hd: kt[:, hd // 2, :],
                lambda hd, t: qkv[:, t, 1024 + hd * DM:1024 + (hd + 1) * DM], causal,
                lambda n, h0: ya[:, n, h0 * DM:(h0 + 2) * DM].rearrange("p (a b) -> p a b", a=2), tq + tk, bufs)
            la = lift(lambda t, k: ya[:, t, k * P:(k + 1) * P], 4, None, x_hi, x_lo, done)
            lb = lift(lambda t, k: uv[:, t, k * P:(k + 1) * P], 4, None, x_hi[:, 4:8, :], x_lo[:, 4:8, :], uz)
            outs = []

            def weigh(first):
                def leave(n, t, psum, done):
                    place = gates[:, t, first + n * BLK:first + (n + 1) * BLK]
                    r = dve.do(lambda e, now: e.tensor_tensor(place, psum, place, ALU.mult), done, gs[first // BLK + n, t])
                    if first:
                        into = gates[:, t, n * BLK:(n + 1) * BLK]
                        outs.append(dve.do(lambda e, now: e.tensor_tensor(into, into, place, ALU.add), r))
                    return [r]
                return leave

            project(x_hi, x_lo, 4, 2, BLK, la, weigh(0))
            project(x_hi[:, 4:8, :], x_lo[:, 4:8, :], 4, 2, BLK, lb, weigh(D), banks=(4, 5, 0, 1))
            x_ready = lift(lambda t, k: gates[:, t, k * P:(k + 1) * P], KC, None, x_hi, x_lo, outs)
            h_parts.clear()
            project(x_hi, x_lo, KC, 2, BLK, x_ready, add_out)
            return list(h_parts)

        def cross_attention(h_ready, mem, got_mem):
            kv, qn = view(2048, NT, D), view(4096, NT, 512)
            qt, kt, mixed, bufs = view(5120, HEADS_X, T), view(6144, HEADS_X, T), view(7168, NT, 512), 8192
            m_ready = lift(lambda t, k: mem[:, t, k * P:(k + 1) * P], KC, lambda k: gain("mem", k), x_hi, x_lo, [got_mem])
            r = inv_rms(lambda t: mem[:, t, :], D, [got_mem], 32)
            act.wait(r)
            dve.wait(r)
            parts, parts_q = [], []

            def leave(n, t, psum, done):
                parts.append(scale_out(n, t, psum, done, kv[:, t, n * BLK:(n + 1) * BLK], 32))
                return parts[-1:]

            def leave_q(n, t, psum, done):
                parts_q.append(scale_out(n, t, psum, done, qn[:, t, :]))
                return parts_q[-1:]

            project(x_hi, x_lo, KC, 2, BLK, m_ready, leave)
            x_ready = lift(h_chunk, KC, lambda k: gain("xa", k), x_hi, x_lo, h_ready)
            r = inv_rms(h_tile, D, h_ready)
            act.wait(r)
            dve.wait(r)
            tk = turn(lambda t, i: kv[:, t, i * P:(i + 1) * P], P, HEADS_X, whole(kt), parts)
            project(x_hi, x_lo, KC, 1, BLK, x_ready, leave_q, banks=(4, 5))
            tq = turn(lambda t, i: qn[:, t, i * P:(i + 1) * P], P, HEADS_X, whole(qt), parts_q, DX ** -0.5)
            done = attention(
                HEADS_X, DX, lambda n: [0, 1], lambda hd, n: qt[:, hd, n * P:(n + 1) * P], lambda hd: kt[:, hd, :],
                lambda hd, t: kv[:, t, 512 + hd * DX:512 + (hd + 1) * DX], None,
                lambda n, h0: mixed[:, n, h0 * DX:(h0 + 2) * DX].rearrange("p (a b) -> p a b", a=2), tq + tk, bufs)
            x_ready = lift(lambda t, k: mixed[:, t, k * P:(k + 1) * P], 4, None, x_hi, x_lo, done)
            h_parts.clear()
            project(x_hi, x_lo, 4, 2, BLK, x_ready, add_out)
            return list(h_parts)

        def peer(h_ready):
            n_lists = NT * HEADS_P * 2
            qn, qt, keys = view(0, NT, 2048), view(4096, 16, T), view(8192, 16, NKEYS)
            sc = view(10240, n_lists, NKEYS)
            best, where = view(14336, n_lists, TOPK), view(14848, n_lists, TOPK).bitcast(U32)
            where_f = view(15360, n_lists, TOPK)
            routed = view(16384, 3, T)
            cand = view(0, NT * HEADS_P, TOPK * TOPK)
            pool_at = 4096
            names = ("value", "expv", "row_f", "col_f", "row_i", "col_i")
            buf = {n: view(pool_at + i * 256, NT * HEADS_P, TOPK) for i, n in enumerate(names)}
            place = view(pool_at + 1536, NT * HEADS_P, TOPK).bitcast(U32)
            part = view(pool_at + 1792, NT * HEADS_P, TOPK).bitcast(U32)
            part2 = view(pool_at + 2048, NT * HEADS_P, TOPK).bitcast(U32)
            total = view(pool_at + 2304, NT * HEADS_P, 1)
            match = view(8192, HEADS_P, TOPK, TOPK)
            got_keys = small_load(keys, a["subkeys"], *h_ready)
            x_ready = lift(h_chunk, KC, lambda k: gain("ffn", k), x_hi, x_lo, h_ready)
            r = inv_rms(h_tile, D, h_ready)
            act.wait(r)
            dve.wait(r)
            parts = []

            def leave(n, t, psum, done):
                parts.append(scale_out(n, t, psum, done, qn[:, t, n * BLK:(n + 1) * BLK]))
                return parts[-1:]

            project(x_hi, x_lo, KC, 4, BLK, x_ready, leave)
            tq = turn(lambda t, i: qn[:, t, i * P:(i + 1) * P], P, 16, whole(qt), parts)
            pe.wait(*tq, got_keys)
            scs = []
            for t in range(NT):
                for i0 in range(0, 16, 4):
                    b = 4 + (i0 // 4) % 2
                    pe.wait(*free[b])
                    for i in range(i0, i0 + 4):
                        pe.put(lambda e, now, b=b, i=i, i0=i0, t=t: e.matmul(
                            bank[b][:, (i - i0) * P:(i - i0 + 1) * P], qt[:, i, t * P:(t + 1) * P], keys[:, i, :],
                            start=True, stop=True))
                    m = mark_last_pe()
                    scs.append(act.do(lambda e, now, b=b, i0=i0, t=t: e.activation(
                        sc[:, t * 16 + i0:t * 16 + i0 + 4, :], bank[b][:, :].rearrange("p (a b) -> p a b", a=4), ACT.Copy), m))
                    free[b] = scs[-1:]

            def top16(src, values, places, n, ready):
                for half in range(2):
                    cols = slice(8 * half, 8 * half + 8)
                    t1 = [dve.do(lambda e, now, i=i, cols=cols: e.max(values[:, i, cols], src[:, i, :]), *ready) for i in range(n)]
                    t2 = [dve.do(lambda e, now, i=i, cols=cols: e.max_index(places[:, i, cols], values[:, i, cols], src[:, i, :]), t1[i])
                          for i in range(n)]
                    if half == 0:
                        ready = [dve.do(lambda e, now, i=i, cols=cols: e.match_replace(src[:, i, :], values[:, i, cols], src[:, i, :], NEG * 1e3), t2[i])
                                 for i in range(n)][-1:]
                return t2[-1]

            found = top16(sc, best, where, n_lists, scs)
            wf = dve.do(lambda e, now: e.tensor_copy(where_f, where), found)
            sides = best.rearrange("p (l s) k -> p l s k", s=2)
            for l in range(NT * HEADS_P):
                cd = dve.do(lambda e, now, l=l: e.tensor_tensor(
                    cand[:, l, :].rearrange("p (a b) -> p a b", a=TOPK),
                    sides[:, l, 0, :].unsqueeze(2).broadcast_to([P, TOPK, TOPK]),
                    sides[:, l, 1, :].unsqueeze(1).broadcast_to([P, TOPK, TOPK]), ALU.add), found)
            chosen = top16(cand, buf["value"], place, NT * HEADS_P, [cd])
            n_pairs = NT * HEADS_P
            d1 = dve.do(lambda e, now: e.tensor_tensor(
                buf["expv"], buf["value"], buf["value"][:, :, 0:1].broadcast_to([P, n_pairs, TOPK]), ALU.subtract), chosen)
            d2 = act.do(lambda e, now: e.activation(buf["expv"], buf["expv"], ACT.Exp), d1)
            d3 = dve.do(lambda e, now: e.reduce_sum(total, buf["expv"], AX), d2)
            d4 = dve.do(lambda e, now: e.reciprocal(total, total), d3)
            weight = dve.do(lambda e, now: e.tensor_tensor(
                buf["expv"], buf["expv"], total.broadcast_to([P, n_pairs, TOPK]), ALU.mult), d4)
            s1 = dve.do(lambda e, now: e.tensor_scalar(part, place, 4, None, ALU.logical_shift_right))
            s2 = dve.do(lambda e, now: e.tensor_scalar(part2, place, 15, None, ALU.bitwise_and))
            f1 = dve.do(lambda e, now: e.tensor_copy(buf["row_f"], part), s1)
            f2 = dve.do(lambda e, now: e.tensor_copy(buf["col_f"], part2), s2)
            keys_of = where_f.rearrange("p (l s) k -> p l s k", s=2)
            last = None
            for side, (rank, to) in enumerate((("row_f", "row_i"), ("col_f", "col_i"))):
                for t in range(NT):
                    ls = slice(t * HEADS_P, (t + 1) * HEADS_P)
                    m1 = [dve.do(lambda e, now, l=l, rank=rank, t=t: e.tensor_tensor(
                        match[:, l, :, :], buf[rank][:, t * HEADS_P + l, :].unsqueeze(2).broadcast_to([P, TOPK, TOPK]),
                        const("iota")[:, 0:TOPK].unsqueeze(1).broadcast_to([P, TOPK, TOPK]), ALU.is_equal), f1, f2, last)
                        for l in range(HEADS_P)]
                    m2 = [dve.do(lambda e, now, l=l, side=side, t=t: e.tensor_tensor(
                        match[:, l, :, :], match[:, l, :, :],
                        keys_of[:, t * HEADS_P + l, side, :].unsqueeze(1).broadcast_to([P, TOPK, TOPK]), ALU.mult),
                        m1[l], wf) for l in range(HEADS_P)]
                    last = dve.do(lambda e, now, to=to, ls=ls: e.reduce_sum(
                        buf[to][:, ls, :].rearrange("p l k -> p (l k)"),
                        match.rearrange("p l k a -> p (l k) a"), AX), m2[-1])
            for i, name in enumerate(("row_i", "col_i", "expv")):
                b = 0 if i < 2 else 1
                pe.wait(*free[b], last, weight)
                for t in range(NT):
                    at = (i % 2) * T + t * P
                    transpose_to(bank[b][:, at:at + P],
                                 buf[name][:, t * HEADS_P:(t + 1) * HEADS_P, :].rearrange("p l k -> p (l k)"))
                if i == 1:
                    m = mark_last_pe()
                    v1 = act.do(lambda e, now: e.activation(routed[:, 0:2, :].rearrange("p a b -> p (a b)"), bank[0][:, :], ACT.Copy), m)
                    free[0] = [v1]
            m = mark_last_pe()
            v2 = act.do(lambda e, now: e.activation(routed[:, 2, :], bank[1][:, 0:T], ACT.Copy), m)
            free[1] = [v2]

            table = view(0, T, JH)
            OCT = 8
            hot_free = {}

            def scatter(half, ready):
                dve.wait(*ready)
                made = []

                def octet(i, base):
                    slot = i % 2
                    u = g.count("token", OCT) - OCT
                    at = lambda now: now(u, "token") if base == 0 else now(u, "token") - base

                    def token_cols(now, which, n):
                        return routed[:, which, bass.ds(at(now), OCT)].unsqueeze(2).broadcast_to([P, OCT, n])

                    rows_ = dve.do(lambda e, now: e.tensor_tensor(
                        onehot_i[:, slot, :, :], const("iota").unsqueeze(1).broadcast_to([P, OCT, NKEYS]),
                        token_cols(now, 0, NKEYS), ALU.is_equal), hot_free.get(slot))
                    c1 = dve.do(lambda e, now: e.tensor_tensor(
                        onehot_j[:, slot, :, :],
                        const("iota")[:, half * JH:(half + 1) * JH].unsqueeze(1).broadcast_to([P, OCT, JH]),
                        token_cols(now, 1, JH), ALU.is_equal))
                    cols_ = dve.do(lambda e, now: e.tensor_tensor(
                        onehot_j[:, slot, :, :], onehot_j[:, slot, :, :], token_cols(now, 2, JH), ALU.mult), c1)
                    b = 6 + slot
                    pe.wait(rows_, cols_, *free[b])
                    for j in range(OCT):
                        pe.put(lambda e, now, j=j: e.matmul(
                            bank[b][:, j * JH:(j + 1) * JH], onehot_i[:, slot, j, :], onehot_j[:, slot, j, :],
                            start=True, stop=True))
                    hot_free[slot] = mark_last_pe()
                    r = act.do(lambda e, now: e.activation(
                        table[:, bass.ds(at(now), OCT), :], bank[b][:, :].rearrange("p (a b) -> p a b", a=OCT), ACT.Copy),
                        hot_free[slot])
                    free[b] = [r]
                    made.append(r)

                base = g.counts.get("token", 0)
                act.wait(*ready)
                octet(0, base)
                octet(1, base)
                with g.loop(T // OCT // 2 - 1):
                    octet(2, base)
                    octet(3, base)
                return made[-1:]

            def activate(c, t, psum, done, turned):
                r = act.do(lambda e, now: e.activation(mid[:, t, :], psum[:, :], ACT.Gelu_apprx_tanh, scale=rstd(t)),
                           done, turned)
                return [r], [r]

            def weigh(c, b, psum, turned, down_done):
                j = g.count("column", 2) - 2
                base = weigh.base
                both = gated[:, 2 * b:2 * b + 2, :]
                m = dve.do(lambda e, now: e.tensor_tensor(
                    both, psum.rearrange("p (f t) -> p f t", f=2),
                    table[:, :, bass.ds(now(j, "column") - base, 2)].rearrange("p t j -> p j t"), ALU.mult),
                    turned, weigh.read.get(b))
                hl = split_a(b, both.rearrange("p f t -> p (f t)"), m, down_done)
                weigh.read[b] = hl[1]
                return [m], hl

            weigh.read = {}
            dve.wait(r)
            last_done = [v1, v2, weight]
            n_chunks = JH // EC
            pipe = None
            for half in range(2):
                ready = scatter(half, last_done)
                dve.wait(*ready)
                weigh.base = g.counts.get("column", 0)
                if half == 0:
                    pipe = Gated(EC, activate, weigh, x_ready)
                    pipe.chunk(0, with_down=False)
                else:
                    pipe.chunk(0)
                pipe.chunk(1)
                with g.loop((n_chunks - 4) // 3):
                    for c in range(3):
                        pipe.chunk(c)
                pipe.chunk(2)
                pipe.chunk(3)
                last_done = [weigh.read[0], weigh.read[1]]
            pipe.down(last=True)
            return add_to_h(1.0, pipe.down_done, h_ready)

        pe.wait(got_consts)
        act.wait(got_gains, got_consts)
        dve.wait(got_gains, got_consts)
        onehot_i, onehot_j = sb("onehot_i", [2, 8, NKEYS]), sb("onehot_j", [2, 8, JH])
        f_hi, f_lo = sb("f_hi", [KC, HEADS_C], F32R), sb("f_lo", [KC, HEADS_C], F32R)
        engines = (pe, act, dve, pool, sp)

        def stages():
            ready = [got_h]
            for l in range(DEPTH):
                ready, _ = ffn(f"ffa{l}", ready)
                yield f"ffa{l}", ready
                ready = even_mixer(ready) if l == 0 else odd_mixer(ready)
                yield f"mix{l}", ready
                ready, _ = ffn(f"ffb{l}", ready)
                yield f"ffb{l}", ready
                ready = ple(l, ready)
                yield f"ple{l}", ready
            row = view(3072, D)
            got = small_load(row, a["final_norm"].partition_broadcast(P), *ready)
            ready = norm_rows(row, ready, got)
            yield "first", ready
            ready = moba_gmlp(ready)
            yield "moba", ready
            mem = view(0, NT, D)
            got_mem = small_load(mem, a["mem"].rearrange("(t p) d -> p t d", p=P), *ready)
            ready = cross_attention(ready, mem, got_mem)
            yield "cross", ready
            ready = peer(ready)
            yield "peer", ready
            row = onehot_i[:, 0, :, :].rearrange("p a b -> p (a b)")
            got = small_load(row, a["final_g"].partition_broadcast(P), *ready)
            ready = norm_rows(row, ready, got)
            yield "all", ready

        for name, ready in stages():
            if name == (stop or "all"):
                return finish(nc, ctx, a, h, ready, sem, engines)


def finish(nc, ctx, a, out, ready, sem, engines):
    pe, act, dve, pool, sp = engines
    s_out = sem("stored")
    sp.wait(sp.load(s_out, lambda e, now: e.dma_start(
        a["out"].rearrange("(t p) d -> p t d", p=P), out[:, :, :]), *ready))
    block = ctx.enter_context(nc.Block())
    block.tensor(pe.run)
    block.scalar(act.run)
    block.vector(dve.run)
    block.gpsimd(pool.run)
    block.sync(sp.run)


def pack(w, width=BLK):
    k, n = w.shape
    nb = -(-n // width)
    full = np.zeros((k, nb * width), w.dtype)
    full[:, :n] = w
    blocks = full.reshape(k // P, P, nb, width).transpose(2, 0, 1, 3).reshape(-1, P, width)
    nu = -(-len(blocks) // UB)
    out = np.zeros((nu * UB, P, BLK), w.dtype)
    out[:len(blocks), :, :width] = blocks
    return out.reshape(nu, UB, P, BLK).transpose(0, 2, 1, 3)


def pack_pipeline(up, down, c_up, c_down):
    parts = [up[:c_up]]
    n = len(up) // c_up
    for c in range(1, n):
        parts += [up[c * c_up:(c + 1) * c_up], down[(c - 1) * c_down:c * c_down]]
    return np.concatenate(parts + [down[(n - 1) * c_down:]])


def pack_ffn(gate_up, down):
    gu = gate_up.reshape(D, 2, NFC, FC).transpose(0, 2, 1, 3).reshape(D, 2 * FF)
    dn = down.reshape(FF // P, P, 2, BLK).transpose(0, 2, 1, 3).reshape(-1, UB, P, BLK).transpose(0, 2, 1, 3)
    return pack_pipeline(pack(gu), dn, 2, 1)


def lay_out(x):
    def rows(w):
        return w.reshape(-1, P, w.shape[-1]).transpose(1, 0, 2).reshape(P, -1)

    stream = []
    for l in range(DEPTH):
        stream.append(pack_ffn(x["ffa_w_gate_up"][l], x["ffa_w_down"][l]))
        if l == 0:
            w_in = x["ev_w_in"][0]
            n_q = HEADS_A * DA
            q = w_in[:, :n_q].reshape(D, KV_A, HEADS_A // KV_A, DA).transpose(0, 2, 1, 3).reshape(D, n_q)
            stream += [pack(np.concatenate([q, w_in[:, n_q:]], 1)), pack(x["ev_w_uq"][0], 384), pack(x["ev_w_ukv"][0]), pack(x["ev_w_out"][0])]
        else:
            stream += [pack(x["od_w_in"][0][:, :3 * D]), pack(x["od_w_out"][0])]
        stream += [pack_ffn(x["ffb_w_gate_up"][l], x["ffb_w_down"][l]), pack(x["ple_w_gate"][l]), pack(x["ple_w_proj"][l])]
    for name in ("w_in", "moba_w_proj", "gmlp_w_proj", "w_out", "xa_w_kv", "xa_w_q", "xa_w_o", "peer_w_q"):
        stream.append(pack(x[name + "_2"][0]))
    down = x["peer_w_down_2"][0].reshape(NKEYS, NKEYS, D).transpose(2, 1, 0).reshape(D, NKEYS * NKEYS)
    up = x["peer_w_up_2"][0].reshape(NKEYS, NKEYS, 2, BLK).transpose(1, 2, 0, 3)
    up = up.reshape(-1, UB, P, BLK).transpose(0, 2, 1, 3)
    stream.append(pack_pipeline(pack(down), up, 2, 2))
    gains = [None] * len(GAINS)
    cols = {"cq": x["ev_cq_norm"][0], "ckv": x["ev_ckv_norm"][0], "mix2": x["norm_mix_g_2"][0],
            "xa": x["norm_xa_g_2"][0], "mem": x["norm_mem_g_2"][0], "ffn": x["norm_ffn_g_2"][0], "bs": x["gmlp_b_s_2"][0]}
    for l in range(DEPTH):
        for n in ("ffa", "mix", "ffb", "ple"):
            cols[f"{n}{l}"] = x[f"{n}_norm"][l]
    gains = np.concatenate([cols[n].reshape(-1, P).T for n in GAINS], 1)
    consts, alibi, pick = constants()
    return {
        "w": np.concatenate(stream).reshape(-1), "x": x["x"][0], "gains": gains, "consts": consts, "alibi": alibi,
        "pick": pick, "p0": rows(x["p"][0, 0].T), "p1": rows(x["p"][1, 0].T), "sinks": x["ev_sinks"][0],
        "w_f": rows(x["od_w_in"][0][:, 3 * D:]), "b_f": x["od_b_f"][0], "final_norm": x["final_norm"],
        "gmlp_w": x["gmlp_w_s_2"][0].transpose(2, 0, 1).reshape(P, -1), "gmlp_g": x["gmlp_norm_g_2"][0],
        "mem": x["mem_2"][0], "subkeys": x["peer_subkeys_2"][0].transpose(3, 0, 1, 2).reshape(P, -1),
        "final_g": x["final_g_2"],
    }


def kernel(stop=None, **inputs):
    import concourse.bacc as bacc
    from concourse.bass_utils import run_bass_kernel_spmd

    arrays = {n: np.ascontiguousarray(v) for n, v in lay_out({k: np.asarray(v) for k, v in inputs.items()}).items()}
    nc = bacc.Bacc("TRN2", target_bir_lowering=False, num_devices=1)
    a = {n: nc.dram_tensor(f"in_{n}", v.shape, F32, kind="ExternalInput").ap() for n, v in arrays.items()}
    a["out"] = nc.dram_tensor("out", (T, D), F32, kind="ExternalOutput").ap()
    build(nc, a, stop)
    got = run_bass_kernel_spmd(nc, [{f"in_{n}": v for n, v in arrays.items()}], core_ids=[0])
    return got.results[0]["out"].reshape(1, T, D)
```

```python
from contextlib import ExitStack, contextmanager

import concourse.bass as bass
from concourse import mybir
import numpy as np

F32 = mybir.dt.float32
F32R = mybir.dt.float32r
U32 = mybir.dt.uint32
BF16 = mybir.dt.bfloat16
ACT = mybir.ActivationFunctionType
ALU = mybir.AluOpType
AX = mybir.AxisListType.X

P = 128
T, D = 256, 1024
NT, KC = T // P, D // P
BLK, UB = 512, 4
FF, FC = 2816, 256
NFC = FF // FC
DEPTH = 2
EPS = 1e-6
HEADS_A, KV_A, DA = 8, 2, 64
HEADS_B, NOPE, ROPE_B, DVB = 8, 64, 32, 64
QLORA, KVLORA = 256, 128
HEADS_C, DC = 16, 64
HEADS_M, DM = 8, 64
G_GRP, G_W = 8, 512
HEADS_X, DX = 4, 128
HEADS_P, NKEYS, TOPK = 8, 128, 16
NEG = -1e30
WHOLE_ROWS, PART_COLS = 4, 4
N_CAND = WHOLE_ROWS * TOPK + (TOPK - WHOLE_ROWS) * PART_COLS
OCT = 8
JH = NKEYS // 2
EC = 4
RING = 3
LEAD = 2


def units(k, n, width=BLK):
    return -(-(k // P) * -(-n // width) // UB)


def stream_plan():
    ffn = NFC * 3
    plan = []
    for l in range(DEPTH):
        plan.append((f"ffa{l}", ffn))
        if l == 0:
            plan += [("ev_in", 6), ("uq", 1), ("ukv", 1), ("ev_out", units(D, D))]
        else:
            plan += [("od_in", units(D, 3 * D)), ("od_out", units(D, D))]
        plan += [(f"ffb{l}", ffn), (f"ple_gate{l}", units(D, D)), (f"ple_proj{l}", 1)]
    plan += [("in2", units(D, 4608)), ("moba", units(512, D)), ("gmlp", units(512, D)),
             ("out2", units(D, D)), ("xkv", units(D, D)), ("xq", units(D, 512)), ("xo", units(512, D)),
             ("peer_q", units(D, 2048)), ("peer", NKEYS // EC * 4)]
    return plan


N_UNITS = sum(n for _, n in stream_plan())

def columns(items):
    at, out = 0, {}
    for name, n in items:
        out[name] = (at, n)
        at += n
    return out, at


GAINS, N_GAINS = columns(
    [(f"{n}{l}", KC) for l in range(DEPTH) for n in ("ffa", "mix", "ffb", "ple")]
    + [("cq", QLORA // P), ("ckv", 1), ("mix2", KC), ("xa", KC), ("mem", KC), ("ffn", KC), ("bs", G_GRP)])
CONSTS, N_CONSTS = columns(
    [("ident", P), ("causal", T), ("trig_b", NT * 2 * (ROPE_B // 2)), ("trig_m", NT * 2 * (DM // 2)),
     ("upto", NT * T), ("iota", NKEYS), ("power", NT), ("tri", P)])


def constants():
    c = np.zeros((P, N_CONSTS), np.float32)

    def put(name, a):
        at, n = CONSTS[name]
        c[:, at:at + n] = a.reshape(P, n)

    r = np.arange(P)
    put("ident", np.eye(P))
    put("causal", np.concatenate([np.zeros((P, P)), np.where(r[None, :] <= r[:, None], 0, NEG)], 1))
    for name, dim in (("trig_b", ROPE_B), ("trig_m", DM)):
        inv = np.float32(10000.0) ** (-np.arange(0, dim, 2, dtype=np.float32) / np.float32(dim))
        ang = (np.arange(T, dtype=np.float32)[:, None] * inv[None, :].astype(np.float32)).astype(np.float64)
        tab = np.stack([np.cos(ang), np.sin(ang)], 1)
        put(name, tab.reshape(NT, P, 2, dim // 2).transpose(1, 0, 2, 3))
    s = np.arange(T).reshape(NT, P)
    put("upto", (s[:, :, None] <= np.arange(T)[None, None, :]).transpose(1, 0, 2))
    put("iota", np.tile(np.arange(NKEYS), (P, 1)))
    put("power", np.full((P, NT), -0.5))
    put("tri", r[:, None] <= r[None, :])
    slopes = 2.0 ** (-8.0 * np.arange(1, HEADS_A + 1) / HEADS_A)
    dist = r[:, None] + P - np.arange(2 * P)[None, :]
    band = (dist >= 0) & (dist < P)
    alibi = np.where(band[:, None, :], -slopes[None, :, None] * dist[:, None, :], NEG)
    return c, alibi.reshape(P, -1).astype(np.float32)


class Ticket:

    def __init__(self, sem, value):
        self.sem, self.value = sem, value


class Program:
    def __init__(self):
        self.engines, self.made = [], None
        self.counts = {}

    def count(self, key, by):
        self.counts[key] = self.counts.get(key, 0) + by
        return self.counts[key]

    def ticket(self, sem, by):
        t = Ticket(sem, self.count(sem, by))
        if self.made is not None:
            self.made.append(t)
        return t

    @contextmanager
    def loop(self, n):
        before = dict(self.counts)
        outer = [e.items for e in self.engines]
        for e in self.engines:
            e.items, e.seen = [], {}
        self.made = []
        yield
        step = {k: v - before.get(k, 0) for k, v in self.counts.items()}
        for e, items in zip(self.engines, outer):
            body, e.items, e.seen = e.items, items, {}
            if body:
                e.items.append((n, body, step))
        for k, v in step.items():
            self.counts[k] += v * (n - 1)
        for t in self.made:
            t.value += step[t.sem] * (n - 1)
        self.made = None


class Engine:
    def __init__(self, program, sem):
        self.program, self.sem, self.items, self.seen = program, sem, [], {}
        program.engines.append(self)

    def wait(self, *tickets):
        for t in tickets:
            if t is not None and self.seen.get(t.sem, 0) < t.value:
                self.seen[t.sem] = t.value
                self.items.append(lambda e, now, s=t.sem, v=t.value: e.wait_ge(s, now(v, s)))

    def do(self, emit, *waits):
        self.wait(*waits)
        self.items.append(lambda e, now: emit(e, now).then_inc(self.sem, 1))
        return self.program.ticket(self.sem, 1)

    def put(self, emit, *waits):
        self.wait(*waits)
        self.items.append(emit)

    def load(self, sem, emit, *waits):
        self.wait(*waits)
        self.items.append(lambda e, now: emit(e, now).then_inc(sem, 16))
        return self.program.ticket(sem, 16)

    def load_dynamic(self, sem, address, emit, wait):
        need = (wait.sem, wait.value) if wait is not None else None

        def both(e, now):
            at = address(now)
            at = at if isinstance(at, int) else e.snap(at)
            if need is not None:
                count = now(need[1], need[0])
                e.wait_ge(need[0], count if isinstance(count, int) else e.snap(count))
            emit(e, at).then_inc(sem, 16)
        self.items.append(both)
        return self.program.ticket(sem, 16)

    def run(self, e):
        def emit(items, now):
            for item in items:
                if isinstance(item, tuple):
                    n, body, step = item
                    with e.Fori(0, n) as i:
                        emit(body, lambda v, k: v + i * step[k] if step.get(k) else v)
                else:
                    item(e, now)
        emit(self.items, lambda v, k: v)


def build(nc, a, stop=None):
    with ExitStack() as ctx:
        def sb(name, cols, dt=F32):
            return ctx.enter_context(nc.sbuf_tensor(name, [P] + list(cols), dt))

        def sem(name):
            return ctx.enter_context(nc.semaphore(name))

        g = Program()
        pe, act, dve = Engine(g, sem("pe_done")), Engine(g, sem("act_done")), Engine(g, sem("dve_done"))
        pool, sp = Engine(g, sem("pool_done")), Engine(g, sem("sp_done"))

        raw = sb("raw", [RING, UB, BLK])
        w_hi, w_lo = sb("w_hi", [RING, UB, BLK], F32R), sb("w_lo", [RING, UB, BLK], F32R)
        h = sb("h", [NT, D])
        x_hi, x_lo = sb("x_hi", [KC, T], F32R), sb("x_lo", [KC, T], F32R)
        a_hi, a_lo = sb("a_hi", [EC, T], F32R), sb("a_lo", [EC, T], F32R)
        mid = sb("mid", [NT, BLK])
        gated = sb("gated", [EC, T])
        gains, consts = sb("gains_sb", [N_GAINS]), sb("consts_sb", [N_CONSTS])
        small = sb("small", [128])
        one_i, one_j = sb("one_i", [2048])[:, :], sb("one_j", [1024])[:, :]
        iota_rep = sb("iota_rep", [NKEYS, OCT], BF16)
        f_hi, f_lo = sb("f_hi", [KC, HEADS_C], F32R), sb("f_lo", [KC, HEADS_C], F32R)
        arena = sb("arena", [17408])
        bank = [ctx.enter_context(nc.psum_tensor(f"bank{b}", [P, BLK], F32)) for b in range(8)]

        def const(name):
            at, n = CONSTS[name]
            return consts[:, at:at + n]

        def gain(name, k):
            return gains[:, GAINS[name][0] + k:GAINS[name][0] + k + 1]

        ident = const("ident")

        s_small = sem("small_loads")

        def small_load(dst, src, *waits):
            t = pool.load(s_small, lambda e, now: e.dma_start(dst, src), *waits)
            pool.wait(t)
            return t

        s_first = [sem(f"first_load{i}") for i in range(3)]
        got_h = sp.load(s_first[0], lambda e, now: e.dma_start(h[:, :, :], a["x"].rearrange("(t p) d -> p t d", p=P)))
        got_consts = sp.load(s_first[1], lambda e, now: e.dma_start(consts[:, :], a["consts"]))
        got_gains = sp.load(s_first[2], lambda e, now: e.dma_start(gains[:, :], a["gains"]))

        s_raw = [sem(f"unit_loaded{i}") for i in range(RING)]
        loaded, split, used = {}, {}, [None] * RING
        raw_read = [(None,)] * RING

        def load_unit():
            u = g.count("loaded", 1) - 1
            if u >= N_UNITS:
                return
            s = u % RING
            loaded[s] = sp.load_dynamic(
                s_raw[s], lambda now: now(u, "loaded") * (P * UB * BLK),
                lambda e, at: e.dma_start(raw[:, s, :, :].rearrange("p b n -> p (b n)"),
                                          a["w"][bass.ds(at, P * UB * BLK)].rearrange("(p n) -> p n", p=P)),
                *raw_read[s])

        def split_unit():
            u = g.count("split", 1) - 1
            if u >= N_UNITS:
                return
            s = u % RING
            hi = act.do(lambda e, now: e.activation(w_hi[:, s, :, :], raw[:, s, :, :], ACT.Copy),
                        loaded[s], used[s])
            lo = dve.do(lambda e, now: e.tensor_tensor(w_lo[:, s, :, :], raw[:, s, :, :],
                                                       w_hi[:, s, :, :].bitcast(F32), ALU.subtract),
                        loaded[s], used[s], hi)
            split[s] = (hi, lo)
            raw_read[s] = (lo,)

        def take_unit():
            u = g.count("taken", 1) - 1
            split_unit()
            load_unit()
            pe.wait(*split[u % RING])
            return u % RING

        for _ in range(RING):
            load_unit()
        for _ in range(LEAD):
            split_unit()
            load_unit()

        def product(out, s, b, width, hi, lo, start, stop):
            for n, (l, w) in enumerate(((hi, w_hi), (hi, w_lo), (lo, w_hi))):
                pe.put(lambda e, now, n=n, l=l, w=w: e.matmul(
                    out, l, w[:, s, b, 0:width], start=start and n == 0, stop=stop and n == 2))

        def signal_pe(emit, *waits):
            return pe.do(emit, *waits)

        def mark_last_pe():
            last = pe.items.pop()
            pe.items.append(lambda e, now: last(e, now).then_inc(pe.sem, 1))
            return g.ticket(pe.sem, 1)

        free = [[] for _ in range(8)]

        def transpose_to(out, src, *waits):
            pe.put(lambda e, now: e.transpose(out, src, ident[0:src.shape[0], 0:src.shape[0]]), *waits)

        def by_chunk(halves):
            return [halves[k * P // BLK] for k in range(KC)]

        def flat(lists):
            return [t for ts in lists for t in ts]

        def lift(src, chunks, gain_of, hi, lo, ready, banks=(0, 1, 2, 3)):
            done = []
            for k0 in range(0, chunks, 2):
                b = banks[(k0 // 2) % len(banks)]
                pe.wait(*free[b])
                ks = range(k0, min(k0 + 2, chunks))
                for k in ks:
                    for t in range(NT):
                        at = (k - k0) * T + t * P
                        transpose_to(bank[b][:, at:at + P], src(t, k), *ready[k])
                turned = mark_last_pe()
                readers = []
                for k in ks:
                    part = bank[b][:, (k - k0) * T:(k - k0 + 1) * T]
                    scale = gain_of(k) if gain_of else 1.0
                    up = act.do(lambda e, now, k=k, part=part, scale=scale: e.activation(
                        hi[:, k, :], part, ACT.Copy, scale=scale), turned)
                    readers.append(up)
                for k in ks:
                    part = bank[b][:, (k - k0) * T:(k - k0 + 1) * T]
                    if gain_of:
                        down = dve.do(lambda e, now, k=k, part=part, scale=gain_of(k): e.scalar_tensor_tensor(
                            lo[:, k, :], part, scale, hi[:, k, :].bitcast(F32), ALU.mult, ALU.subtract), up)
                    else:
                        down = dve.do(lambda e, now, k=k, part=part: e.tensor_tensor(
                            lo[:, k, :], part, hi[:, k, :].bitcast(F32), ALU.subtract), up)
                    readers.append(down)
                free[b] = readers
                done += [readers] * len(ks)
            return done

        def inv_rms(src, width, ready, col=0):
            junk = gated[:, :, :].rearrange("p a b -> p (a b)")
            sums = []
            for t in range(NT):
                sums.append(act.do(lambda e, now, t=t: e.activation(
                    junk[:, 0:width], src(t), ACT.Square, accum_out=small[:, col + t:col + t + 1]),
                    *ready, *sums[-1:], *junk_free))
            junk_free[:] = sums[-1:]
            mean = dve.do(lambda e, now: e.tensor_scalar(small[:, col + 2:col + 4], small[:, col:col + 2],
                                                         1.0 / width, EPS, ALU.mult, ALU.add), sums[-1])
            return pool.do(lambda e, now: e.tensor_tensor(small[:, col + 4:col + 6], small[:, col + 2:col + 4],
                                                          const("power"), ALU.pow), mean)

        junk_free = []

        def rstd(t, col=0):
            return small[:, col + 4 + t:col + 5 + t]

        def project_steps(hi, lo, chunks, blocks, width, ready, leave, banks=(0, 1, 2, 3, 4, 5)):
            slot = None
            for n in range(blocks):
                w = width[n] if isinstance(width, (list, tuple)) else width
                pair = banks[2 * n % len(banks)], banks[(2 * n + 1) % len(banks)]
                for b in pair:
                    pe.wait(*free[b])
                done = [None] * NT
                for k0 in range(0, chunks, UB):
                    ks = range(k0, min(k0 + UB, chunks))
                    if (n * chunks + k0) % UB == 0:
                        if slot is not None:
                            yield
                        slot = take_unit()
                    for t in range(NT):
                        for k in ks:
                            if n == 0:
                                pe.wait(*ready[k])
                            product(bank[pair[t]][:, 0:w], slot, (n * chunks + k) % UB, w,
                                    hi(k)[:, t * P:(t + 1) * P], lo(k)[:, t * P:(t + 1) * P],
                                    k == 0, k == chunks - 1)
                        done[t] = mark_last_pe()
                    used[slot] = done[NT - 1]
                for t in range(NT):
                    free[pair[t]] = leave(n, t, bank[pair[t]][:, 0:w], done[t])
            yield

        def run_all(*steps):
            steps = list(steps)
            while steps:
                steps = [x for x in steps if next(x, "end") != "end"]

        def project(*args, **more):
            run_all(project_steps(*args, **more))

        def x_at(first=0):
            return (lambda k: x_hi[:, first + k, :]), (lambda k: x_lo[:, first + k, :])

        def a_at(first=0):
            return (lambda k: a_hi[:, first + k, :]), (lambda k: a_lo[:, first + k, :])

        ACC, GU, TR = (0, 1, 2, 3), (4, 5), (6, 7)

        class Gated:

            def __init__(self, nf, activate, turn, x_ready, first=True):
                self.nf, self.activate, self.turn, self.first = nf, activate, turn, first
                self.a_ready, self.down_done, self.x_ready = [], None, x_ready
                for b in ACC:
                    pe.wait(*free[b])

            def down(self, last=False):
                pe.wait(*self.a_ready)
                per = UB // 2
                for f0 in range(0, self.nf, per):
                    s = take_unit()
                    for half in range(2):
                        for f in range(f0, f0 + per):
                            for t in range(NT):
                                product(bank[2 * t + half][:, :], s, 2 * (f - f0) + half, BLK,
                                        a_hi[:, f, t * P:(t + 1) * P], a_lo[:, f, t * P:(t + 1) * P],
                                        self.first and f == 0, last and f == self.nf - 1)
                        self.half_done[half] = mark_last_pe()
                    used[s] = self.down_done = self.half_done[1]
                self.first = False

            def chunk(self, c, with_down=True):
                ready = self.up(c)
                if with_down:
                    self.down()
                self.back(c, ready)

            def up(self, c):
                for b in GU:
                    pe.wait(*free[b])
                for u in range(2):
                    s = take_unit()
                    done = []
                    for t in range(NT):
                        for k in range(UB):
                            kk = u * UB + k
                            if self.x_ready:
                                pe.wait(*self.x_ready[kk])
                            product(bank[GU[t]][:, :], s, k, BLK, x_hi[:, kk, t * P:(t + 1) * P],
                                    x_lo[:, kk, t * P:(t + 1) * P], kk == 0, kk == KC - 1)
                        done.append(mark_last_pe())
                    used[s] = done[-1]
                self.x_ready, ready = None, []
                for t in range(NT):
                    readers, r = self.activate(c, t, bank[GU[t]], done[t], self.turned)
                    free[GU[t]] = readers
                    ready += r
                return ready

            def back(self, c, ready):
                pe.wait(*ready)
                for b in range(self.nf // 2):
                    pe.wait(*free[TR[b]])
                    for f in (2 * b, 2 * b + 1):
                        for t in range(NT):
                            at = (f % 2) * T + t * P
                            transpose_to(bank[TR[b]][:, at:at + P], mid[:, t, f * P:(f + 1) * P])
                    self.turned = mark_last_pe()
                    free[TR[b]], r = self.turn(c, b, bank[TR[b]], self.turned, self.down_done)
                    self.a_ready = r if b == 0 else self.a_ready + r

            turned = None
            half_done = [None, None]

        def split_a(b, src, done, *waits):
            hi = act.do(lambda e, now: e.activation(a_hi[:, 2 * b:2 * b + 2, :].rearrange("p f t -> p (f t)"),
                                                    src, ACT.Copy), done, *waits)
            lo = dve.do(lambda e, now: e.tensor_tensor(
                a_lo[:, 2 * b:2 * b + 2, :].rearrange("p f t -> p (f t)"), src,
                a_hi[:, 2 * b:2 * b + 2, :].rearrange("p f t -> p (f t)").bitcast(F32), ALU.subtract), hi)
            return [hi, lo]

        def add_to_h(scale, done, ready):
            out = []
            for half in range(2):
                out.append([])
                for t in range(NT):
                    cols = h[:, t, half * BLK:(half + 1) * BLK]
                    b = 2 * t + half
                    r = dve.do(lambda e, now, b=b, cols=cols: e.scalar_tensor_tensor(
                        cols, bank[b][:, :], scale, cols, ALU.mult, ALU.add), done[half], *flat(ready))
                    free[b] = [r]
                    out[half].append(r)
            return out

        h_tile = lambda t: h[:, t, :]
        h_chunk = lambda t, k: h[:, t, k * P:(k + 1) * P]

        def ffn(name, h_ready):
            x_ready = lift(h_chunk, KC, lambda k: gain(name, k), x_hi, x_lo, by_chunk(h_ready))
            scaled = inv_rms(h_tile, D, flat(h_ready))
            dve.wait(scaled)
            act.wait(scaled)

            def activate(c, t, psum, done, turned):
                silu = act.do(lambda e, now: e.activation(gated[:, t, :], psum[:, 0:FC], ACT.Silu, scale=rstd(t)),
                              done, turned)
                both = dve.do(lambda e, now: e.scalar_tensor_tensor(
                    mid[:, t, 0:FC], psum[:, FC:2 * FC], rstd(t), gated[:, t, :], ALU.mult, ALU.mult), done, silu)
                return [silu, both], [both]

            def turn(c, b, psum, turned, down_done):
                both = split_a(b, psum[:, :], turned, down_done)
                return both, both

            p = Gated(2, activate, turn, x_ready)
            p.chunk(0, with_down=False)
            p.chunk(1)
            with g.loop(NFC - 2):
                p.chunk(2)
            p.down(last=True)
            return add_to_h(0.5, p.half_done, h_ready)

        arena_free = [None]

        def view(at, *dims):
            return shaped(arena[:, at:at + int(np.prod(dims))], *dims)

        def shaped(cols, *dims):
            if len(dims) == 1:
                return cols
            names = "abcd"[:len(dims)]
            return cols.rearrange(f"p ({' '.join(names)}) -> p {' '.join(names)}",
                                  **{x: d for x, d in zip(names[1:], dims[1:])})


        def turn_steps(src, rows, n, places, ready, done, scale=1.0, banks=(0, 1, 2, 3)):
            for i0 in range(0, n, 2):
                b = banks[(i0 // 2) % len(banks)]
                pe.wait(*free[b], *ready)
                m = min(2, n - i0)
                for i in range(i0, i0 + m):
                    for t in range(NT):
                        at = (i - i0) * T + t * P
                        transpose_to(bank[b][0:rows, at:at + P], src(t, i))
                turned = mark_last_pe()
                for r0, r1, c0, c1, place in places(i0, m):
                    if i0 % 4:
                        last = dve.do(lambda e, now, b=b, r0=r0, r1=r1, c0=c0, c1=c1, place=place: e.tensor_scalar(
                            place, bank[b][r0:r1, c0:c1], scale, None, ALU.mult), turned)
                    else:
                        last = act.do(lambda e, now, b=b, r0=r0, r1=r1, c0=c0, c1=c1, place=place: e.activation(
                            place, bank[b][r0:r1, c0:c1], ACT.Copy, scale=scale), turned)
                free[b] = [last]
                done.append(last)
                yield

        def turn(src, rows, n, places, ready, scale=1.0, banks=(0, 1, 2, 3)):
            done = []
            run_all(turn_steps(src, rows, n, places, ready, done, scale, banks))
            return done

        def whole(dst, rows=P):
            return lambda i, m: [(0, rows, 0, m * T, dst[0:rows, i:i + m, :].rearrange("p a b -> p (a b)"))]

        def halves(dst, top, bottom):
            def places(i, m):
                out = []
                for j in range(m):
                    out.append((0, 64, j * T, (j + 1) * T, dst[0:64, top(i + j), :]))
                    out.append((64, P, j * T, (j + 1) * T, dst[64:P, bottom(i + j), :]))
                return out
            return places

        def scale_out(t, psum, done, place, col=0):
            if t == 0:
                return act.do(lambda e, now: e.activation(place, psum, ACT.Copy, scale=rstd(t, col)), done)
            return dve.do(lambda e, now: e.tensor_scalar(place, psum, rstd(t, col), None, ALU.mult), done)

        def values_out(t, psum, done, padded, heads, col=0, side=None):
            psum = psum.rearrange("p (h d) -> p h d", d=64)
            if side is not None:
                return scale_out(t, psum, done, padded[:, :, side * 64:(side + 1) * 64], col)
            for odd in range(2):
                r = scale_out(t, psum[:, odd:heads:2, :], done, padded[:, odd:heads:2, odd * 64:(odd + 1) * 64], col)
            return r

        def add_out(n, t, psum, done):
            cols = h[:, t, n * BLK:(n + 1) * BLK]
            r = dve.do(lambda e, now: e.tensor_tensor(cols, psum, cols, ALU.add), done)
            h_parts[n].append(r)
            return [r]

        h_parts = [[], []]

        def project_to_h(operand, chunks, ready):
            h_parts[:] = [[], []]
            project(*operand, chunks, 2, BLK, ready, add_out)
            return list(h_parts)

        stat = sb("stat", [5, 2 * HEADS_C])

        def attention_steps(heads, keys, q, k, v, bias, out, ready, sc, ex, done, sink=None, wide=False):
            ext = mid
            steps = [(n, h0) for n in range(NT) for h0 in range(0, heads, 2)]
            totals, scaled, copies, values = {}, {}, {}, {}
            pe.wait(*ready)
            dve.wait(*ready)

            def col(i, s):
                return stat[:, i, 2 * (s % HEADS_C):2 * (s % HEADS_C) + 2]

            for s in range(len(steps) + 3):
                if s < len(steps):
                    n, h0 = steps[s]
                    nk = len(keys(n)) * P
                    k0 = keys(n)[0] * P
                    b = s % 2
                    pe.wait(*free[b])
                    for j in range(2):
                        pe.put(lambda e, now, b=b, j=j, n=n, hd=h0 + j, k0=k0, nk=nk: e.matmul(
                            bank[b][:, j * nk:(j + 1) * nk], q(hd, n), k(hd)[:, k0:k0 + nk], start=True, stop=True))
                    scored = mark_last_pe()
                if 2 <= s < len(steps) + 2:
                    r = s - 2
                    m = 2 * len(keys(steps[r][0]))
                    b = 2 + r % 2
                    pe.wait(*free[b], scaled[r])
                    for j in range(m):
                        transpose_to(bank[b][:, j * P:(j + 1) * P], ex[:, r % 3, j * P:(j + 1) * P])
                    turned = mark_last_pe()
                    copies[r] = act.do(lambda e, now, b=b, r=r, m=m: e.activation(
                        ext[:, r % 2, 0:m * P], bank[b][:, 0:m * P], ACT.Copy), turned, values.get(r - 2))
                    free[b] = [copies[r]]
                if s >= 3:
                    r = s - 3
                    rn, rh = steps[r]
                    tiles = keys(rn)
                    b = 4 + r % 2
                    pe.wait(*free[b], copies[r])
                    for j in range(2):
                        for i, tile in enumerate(tiles):
                            pe.put(lambda e, now, b=b, j=j, i=i, tile=tile, r=r, rh=rh, m=len(tiles): e.matmul(
                                bank[b][:, (j if wide else 0) * P:(j + 1 if wide else 1) * P], v(rh + j, tile),
                                ext[:, r % 2, (j * m + i) * P:(j * m + i + 1) * P],
                                start=i == 0 and (wide or j == 0), stop=i == m - 1 and (wide or j == 1)))
                    values[r] = mark_last_pe()
                if s < len(steps):
                    b = s % 2
                    scores = bank[b][:, 0:2 * nk].rearrange("p (a b) -> p a b", a=2)
                    soft = sc[:, b, 0:2 * nk].rearrange("p (a b) -> p a b", a=2)
                    if bias is None:
                        soft, biased = scores, scored
                    else:
                        biased = dve.do(lambda e, now, n=n, h0=h0, soft=soft, scores=scores: e.tensor_tensor(
                            soft, scores, bias(n, h0), ALU.add), scored, totals.get(s - 2))
                    low = dve.do(lambda e, now, s=s, soft=soft: e.tensor_reduce(
                        col(1, s), soft, AX, ALU.max, negate=True), biased)
                    if sink is not None:
                        low = dve.do(lambda e, now, s=s, h0=h0: e.tensor_tensor(
                            col(1, s), col(1, s), sink[:, h0:h0 + 2], ALU.min), low)
                        gap = dve.do(lambda e, now, s=s, h0=h0: e.tensor_tensor(
                            col(3, s), col(1, s), sink[:, h0:h0 + 2], ALU.subtract), low)
                        act.do(lambda e, now, s=s: e.activation(col(3, s), col(3, s), ACT.Exp), gap)
                    for j in range(2):
                        totals[s] = act.do(lambda e, now, s=s, j=j, soft=soft, nk=nk: e.activation(
                            ex[:, s % 3, j * nk:(j + 1) * nk], soft[:, j, :], ACT.Exp, bias=col(1, s)[:, j:j + 1],
                            accum_out=col(2, s)[:, j:j + 1]), low)
                    free[b] = [totals[s]] if bias is None else [biased]
                if 1 <= s <= len(steps):
                    r = s - 1
                    nk = len(keys(steps[r][0])) * P
                    total = totals[r]
                    if sink is not None:
                        total = dve.do(lambda e, now, r=r: e.tensor_tensor(col(2, r), col(2, r), col(3, r), ALU.add), total)
                    inv = dve.do(lambda e, now, r=r: e.reciprocal(col(4, r), col(2, r)), total)
                    for j in range(2):
                        scaled[r] = dve.do(lambda e, now, r=r, j=j, nk=nk: e.tensor_scalar(
                            ex[:, r % 3, j * nk:(j + 1) * nk], ex[:, r % 3, j * nk:(j + 1) * nk],
                            col(4, r)[:, j:j + 1], None, ALU.mult), inv)
                if s >= 3:
                    r, (rn, rh) = s - 3, steps[s - 3]
                    b = 4 + r % 2
                    parts = []
                    for i, c in enumerate((rh, rh + 1) if wide else (rh // 2,)):
                        hi, lo = out[0](c)[:, rn * P:(rn + 1) * P], out[1](c)[:, rn * P:(rn + 1) * P]
                        psum = bank[b][:, i * P:(i + 1) * P]
                        up = act.do(lambda e, now, hi=hi, psum=psum: e.activation(hi, psum, ACT.Copy), values[r])
                        parts.append((c, hi, lo, psum))
                    for c, hi, lo, psum in parts:
                        down = dve.do(lambda e, now, hi=hi, lo=lo, psum=psum: e.tensor_tensor(
                            lo, psum, hi.bitcast(F32), ALU.subtract), up)
                        done[c] += [up, down]
                    free[b] = [down]
                yield

        def rotate(x1, x2, cos, sin, t1, t2, ready):
            dve.wait(*ready)
            a1 = dve.do(lambda e, now: e.tensor_tensor(t1, x1, sin, ALU.mult))
            a2 = dve.do(lambda e, now: e.tensor_tensor(t2, x2, sin, ALU.mult))
            b1 = dve.do(lambda e, now: e.tensor_tensor(x1, x1, cos, ALU.mult), a1)
            b2 = dve.do(lambda e, now: e.tensor_tensor(x2, x2, cos, ALU.mult), a2)
            dve.do(lambda e, now: e.tensor_tensor(x1, x1, t2, ALU.subtract), b1)
            return dve.do(lambda e, now: e.tensor_tensor(x2, x2, t1, ALU.add), b2)

        def causal(n, h0):
            mask = const("causal")
            mask = mask[:, P:T] if n == 0 else mask
            return mask.unsqueeze(1).broadcast_to([P, 2, (n + 1) * P])

        up_to = lambda n: list(range(n + 1))

        def trig(name, half, heads):
            tab = const(name).rearrange("p (t c f) -> p t c f", t=NT, c=2)
            return [tab[:, :, c, :].unsqueeze(2).broadcast_to([P, NT, heads, half]) for c in range(2)]

        def clear(cols):
            return pool.do(lambda e, now: e.memset(cols, 0.0), *arena_free)

        def ple(l, h_ready):
            p_in, g_out = view(0, 2, T), view(512, NT, D)
            got = small_load(p_in, a[f"p{l}"], *arena_free)
            x_ready = lift(h_chunk, KC, lambda k: gain(f"ple{l}", k), x_hi, x_lo, by_chunk(h_ready))
            act.wait(inv_rms(h_tile, D, flat(h_ready)))
            hi = act.do(lambda e, now: e.activation(a_hi[:, 0:2, :], p_in, ACT.Copy), got, *flat(h_ready))
            lo = dve.do(lambda e, now: e.tensor_tensor(a_lo[:, 0:2, :], p_in, a_hi[:, 0:2, :].bitcast(F32),
                                                       ALU.subtract), hi)
            gates = {}

            def gate(n, t, psum, done):
                gates[n, t] = act.do(lambda e, now: e.activation(
                    g_out[:, t, n * BLK:(n + 1) * BLK], psum, ACT.Sigmoid, scale=rstd(t)), done)
                return [gates[n, t]]

            project(*x_at(), KC, 2, BLK, x_ready, gate)
            out = [[], []]

            def leave(n, t, psum, done):
                g = g_out[:, t, n * BLK:(n + 1) * BLK]
                cols = h[:, t, n * BLK:(n + 1) * BLK]
                m = dve.do(lambda e, now: e.tensor_tensor(g, psum, g, ALU.mult), done, gates[n, t])
                out[n].append(dve.do(lambda e, now: e.tensor_tensor(cols, cols, g, ALU.add), m))
                return [m]

            project(*a_at(), 2, 2, BLK, [[hi, lo]] * 2, leave, banks=(4, 5, 0, 1))
            arena_free[:] = flat(out)
            return out

        def norm_rows(name, h_ready):
            row = one_i[:, 0:D]
            got = small_load(row, a[name].partition_broadcast(P), *row_free)
            r = inv_rms(h_tile, D, flat(h_ready))
            out = [[], []]
            for half in range(2):
                for t in range(NT):
                    cols = slice(half * BLK, (half + 1) * BLK)
                    out[half].append(dve.do(lambda e, now, t=t, cols=cols: e.scalar_tensor_tensor(
                        h[:, t, cols], h[:, t, cols], rstd(t), row[:, cols], ALU.mult, ALU.mult), r, got))
            return out

        row_free = []

        def even_mixer(h_ready):
            N_IN, W = 1184, NOPE + ROPE_B
            pin, v_a = view(0, NT, N_IN), view(2400, NT, KV_A, 2, P)
            qt_a, kt_a = view(3424, HEADS_A, T), view(5472, 1, T)
            qb, kcat, v_b = view(5728, NT, HEADS_B, W), view(7264, NT, HEADS_B, W), view(8800, NT, HEADS_B, P)
            qt_b, kt_b = view(10848, HEADS_B, T), view(12896, HEADS_B, T)
            ex, tmp = view(14944, 3, BLK), view(16480, 576)
            sc = shaped(one_j, 2, BLK)
            sinks = small[:, 64:64 + HEADS_A]
            alibi = one_i.rearrange("p (h k) -> p h k", h=HEADS_A)
            got_alibi = small_load(one_i, a["alibi"])
            got_sinks = small_load(sinks, a["sinks"].partition_broadcast(P))
            cleared = [clear(x) for x in (qt_a, v_a, v_b)]
            x_ready = lift(h_chunk, KC, lambda k: gain("mix0", k), x_hi, x_lo, by_chunk(h_ready))
            r = inv_rms(h_tile, D, flat(h_ready))
            act.wait(r, *cleared)
            dve.wait(r, *cleared)
            neg = dve.do(lambda e, now: e.tensor_scalar(sinks, sinks, -1.0, None, ALU.mult), got_sinks)
            parts = {}

            def leave(n, t, psum, done):
                w = min(BLK, N_IN - n * BLK)
                parts[n, t] = scale_out(t, psum[:, 0:w], done, pin[:, t, n * BLK:n * BLK + w])
                if n == 1:
                    v = psum[:, 128:256]
                    for side in range(2):
                        parts[n, t] = values_out(t, v, done, v_a[:, t, :, side, :], KV_A, side=side)
                return [parts[n, t]]

            project(*x_at(), KC, 3, [BLK, BLK, 256], x_ready, leave, banks=(4, 5, 6, 7))

            def latent():
                cq = lambda t, k: pin[:, t, 768 + k * P:768 + (k + 1) * P]
                ckv = lambda t, k: pin[:, t, 1024:1152]
                p1, p2 = [parts[1, 0], parts[1, 1]], [parts[2, 0], parts[2, 1]]
                l1 = lift(cq, 2, lambda k: gain("cq", k), x_hi, x_lo, [p1] * 2, banks=(6,))
                l2 = lift(ckv, 1, lambda k: gain("ckv", k), x_hi[:, 2:3, :], x_lo[:, 2:3, :], [p2], banks=(7,))
                r1 = inv_rms(lambda t: pin[:, t, 768:1024], QLORA, p1, 8)
                r2 = inv_rms(lambda t: pin[:, t, 1024:1152], KVLORA, p2, 16)
                act.wait(r1, r2)
                dve.wait(r1, r2)
                yield
                flat_q = qb.rearrange("p t h d -> p t (h d)")
                parts_q, parts_kv = [], []

                def leave_q(n, t, psum, done):
                    parts_q.append(scale_out(t, psum, done, flat_q[:, t, n * 384:(n + 1) * 384], 8))
                    return parts_q[-1:]

                def leave_kv(n, t, psum, done):
                    heads = psum.rearrange("p (h d) -> p h d", d=NOPE + DVB)
                    h0, m = n * 4, 4
                    scale_out(t, heads[:, :, 0:NOPE], done, kcat[:, t, h0:h0 + m, 0:NOPE], 16)
                    for odd in range(2):
                        r = scale_out(t, heads[:, odd:m:2, NOPE:], done,
                                      v_b[:, t, h0 + odd:h0 + m:2, odd * 64:(odd + 1) * 64], 16)
                    parts_kv.append(r)
                    return [r]

                half = ROPE_B // 2
                k4 = pin[:, :, 1152:1184].unsqueeze(2)
                t3, t4 = (shaped(tmp[:, 512 + i * 32:512 + (i + 1) * 32], NT, 1, half) for i in range(2))
                cos, sin = trig("trig_b", half, 1)
                rk = rotate(k4[:, :, :, 0:half], k4[:, :, :, half:], cos, sin, t3, t4, p2)
                kr = [dve.do(lambda e, now, t=t: e.tensor_copy(
                    kcat[:, t, :, NOPE:], pin[:, t, 1152:1184].unsqueeze(1).broadcast_to([P, HEADS_B, ROPE_B])), rk)
                    for t in range(NT)]
                yield from project_steps(*x_at(), 2, 2, 384, l1, leave_q, banks=(6, 7))
                t1, t2 = (shaped(tmp[:, i * 256:(i + 1) * 256], NT, HEADS_B, half) for i in range(2))
                cos, sin = trig("trig_b", half, HEADS_B)
                rq = rotate(qb[:, :, :, NOPE:NOPE + half], qb[:, :, :, NOPE + half:], cos, sin, t1, t2, parts_q)
                yield from project_steps(*x_at(2), 1, 2, BLK, l2, leave_kv, banks=(6, 7))
                yield from turn_steps(lambda t, i: qb[:, t, i, :], W, HEADS_B, whole(qt_b, W), [rq], ready_b,
                                      W ** -0.5, banks=(6, 7))
                yield from turn_steps(lambda t, i: kcat[:, t, i, :], W, HEADS_B, whole(kt_b, W), parts_kv + kr,
                                      ready_b, banks=(6, 7))

            ready_b, done_a, done_b = [], [[] for _ in range(4)], [[] for _ in range(4)]
            all_parts = list(parts.values())
            ta = turn(lambda t, i: pin[:, t, i * P:(i + 1) * P], P, 4, halves(qt_a, lambda i: i, lambda i: i + 4),
                      all_parts, DA ** -0.5)
            tk = turn(lambda t, i: pin[:, t, 512:640], P, 1, whole(kt_a), all_parts, banks=(2,))
            run_all(attention_steps(
                HEADS_A, up_to, lambda hd, n: qt_a[:, hd, n * P:(n + 1) * P], lambda hd: kt_a[:, 0, :],
                lambda hd, t: v_a[:, t, hd // 4, hd % 2, :],
                lambda n, h0: alibi[:, h0:h0 + 2, (P if n == 0 else 0):T], a_at(),
                ta + tk + [got_alibi, neg] + all_parts, sc, ex, done_a, sink=sinks), latent())
            run_all(attention_steps(
                HEADS_B, up_to, lambda hd, n: qt_b[0:W, hd, n * P:(n + 1) * P], lambda hd: kt_b[0:W, hd, :],
                lambda hd, t: v_b[:, t, hd, :], causal, x_at(4), ready_b, sc, ex, done_b))
            arena_free[:] = [done_b[-1][-1]]
            (ah, al), (xh, xl) = a_at(), x_at()
            return project_to_h((lambda k: ah(k) if k < 4 else xh(k), lambda k: al(k) if k < 4 else xl(k)), KC,
                                done_a + done_b)

        def odd_mixer(h_ready):
            W, SC = DC + 2, DC ** -0.5
            q_in, k_in = view(0, NT, HEADS_C, W), view(2112, NT, HEADS_C, W)
            values = view(4224, NT, HEADS_C, P)
            qt, kt = view(8320, HEADS_C, T), view(12416, HEADS_C, T)
            sc, ex = shaped(one_j, 2, BLK), shaped(one_i[:, 0:3 * BLK], 3, BLK)
            tmp = one_i[:, 3 * BLK:]
            f_raw, bf, zt = shaped(tmp[:, 0:128], KC, HEADS_C), tmp[:, 128:144], tmp[:, 144:400]
            z, nz, lf = (shaped(tmp[:, 400 + i * 32:432 + i * 32], NT, HEADS_C) for i in range(3))
            got_f = small_load(f_raw, a["w_f"], *arena_free)
            got_b = small_load(bf, a["b_f"].partition_broadcast(P))
            cleared = [clear(values)]
            cleared.append(pool.do(lambda e, now: e.memset(q_in[:, :, :, DC:DC + 1], 1.0 / SC), *arena_free))
            cleared.append(pool.do(lambda e, now: e.memset(k_in[:, :, :, DC + 1:], 1.0), *arena_free))
            x_ready = lift(h_chunk, KC, lambda k: gain("mix1", k), x_hi, x_lo, by_chunk(h_ready))
            r = inv_rms(h_tile, D, flat(h_ready))
            act.wait(r, *cleared)
            dve.wait(r, *cleared)
            fh = act.do(lambda e, now: e.activation(f_hi[:, :, :], f_raw, ACT.Copy), got_f)
            fl = dve.do(lambda e, now: e.tensor_tensor(f_lo[:, :, :], f_raw, f_hi[:, :, :].bitcast(F32), ALU.subtract), fh)

            def forget():
                pe.wait(fh, fl, *free[4], *free[5])
                for k in range(KC):
                    for i, (w, x) in enumerate(((f_hi, x_hi), (f_lo, x_hi), (f_hi, x_lo))):
                        pe.put(lambda e, now, k=k, w=w, x=x, i=i: e.matmul(
                            bank[4][0:HEADS_C, 0:T], w[:, k, :], x[:, k, :],
                            start=k == 0 and i == 0, stop=k == KC - 1 and i == 2))
                m = mark_last_pe()
                c = dve.do(lambda e, now: e.tensor_copy(zt[0:HEADS_C, :], bank[4][0:HEADS_C, 0:T]), m)
                yield
                pe.wait(c)
                for t in range(NT):
                    transpose_to(bank[5][:, t * HEADS_C:(t + 1) * HEADS_C], zt[0:HEADS_C, t * P:(t + 1) * P])
                m = mark_last_pe()
                for t in range(NT):
                    d = dve.do(lambda e, now, t=t: e.scalar_tensor_tensor(
                        z[:, t, :], bank[5][:, t * HEADS_C:(t + 1) * HEADS_C], rstd(t), bf, ALU.mult, ALU.add), m, got_b)
                n1 = dve.do(lambda e, now: e.tensor_scalar(nz, z, -1.0, None, ALU.mult), d)
                n2 = dve.do(lambda e, now: e.tensor_tensor(nz, z, nz, ALU.min), n1)
                e1 = act.do(lambda e, now: e.activation(lf, nz, ACT.Exp), n2)
                e2 = act.do(lambda e, now: e.activation(lf, lf, ACT.Ln, bias=1.0), e1)
                n3 = dve.do(lambda e, now: e.tensor_scalar(z, z, 0.0, None, ALU.min))
                n4 = dve.do(lambda e, now: e.tensor_tensor(lf, z, lf, ALU.subtract), n3, e2)
                yield
                upto = shaped(const("upto"), NT, T)
                pe.wait(n4, c, d)
                for n in range(NT):
                    for s in range(n + 1):
                        pe.put(lambda e, now, n=n, s=s: e.matmul(
                            bank[4][:, n * 16:(n + 1) * 16], upto[:, s, n * P:(n + 1) * P], lf[:, s, :],
                            start=s == 0, stop=s == n))
                m = mark_last_pe()
                sums = shaped(bank[4][:, 0:NT * HEADS_C], NT, HEADS_C, 1)
                to_q = dve.do(lambda e, now: e.tensor_scalar(q_in[:, :, :, DC + 1:], sums, 1.0 / SC, None, ALU.mult), m)
                to_k = dve.do(lambda e, now: e.tensor_scalar(k_in[:, :, :, DC:DC + 1], sums, -1.0, None, ALU.mult), m)
                free[4], free[5] = [to_k], [d]
                forgets.extend([to_q, to_k])
                yield

            forgets, parts = [], {}

            def leave(n, t, psum, done):
                kind, h0 = n % 3, n // 3 * 8
                if kind == 2:
                    parts[n, t] = values_out(t, psum, done, values[:, t, h0:h0 + 8, :], 8)
                else:
                    place = (q_in, k_in)[kind][:, t, h0:h0 + 8, 0:DC]
                    parts[n, t] = scale_out(t, psum.rearrange("p (h d) -> p h d", d=DC), done, place)
                return [parts[n, t]]

            proj = project_steps(*x_at(), KC, 6, BLK, x_ready, leave, banks=(6, 7))
            next(proj)
            next(proj)
            fg = forget()
            for _ in range(4):
                next(fg, None)
                next(proj)
            turned, done = [[], []], [[] for _ in range(8)]

            def turn_in(half, banks):
                for src, dst, kind, scale in ((q_in, qt, 0, SC), (k_in, kt, 1, 1.0)):
                    ready = forgets + [parts[3 * half + kind, t] for t in range(NT)]
                    yield from turn_steps(lambda t, i, src=src: src[:, t, 8 * half + i, :], W, 8,
                                          whole(dst[:, 8 * half:8 * half + 8, :], W), ready, turned[half], scale, banks)

            def attend(half, out):
                h0 = 8 * half
                return attention_steps(
                    8, up_to, lambda hd, n: qt[0:W, h0 + hd, n * P:(n + 1) * P], lambda hd: kt[0:W, h0 + hd, :],
                    lambda hd, t: values[:, t, h0 + hd, :], causal, out,
                    turned[half] + [parts[3 * half + 2, t] for t in range(NT)], sc, ex, done[4 * half:4 * half + 4])

            run_all(turn_in(0, (0, 1, 2, 3)))
            run_all(attend(0, a_at()), proj)
            run_all(turn_in(1, (0, 1, 2, 3)))
            run_all(attend(1, x_at(4)))
            arena_free[:] = [done[-1][-1]]
            row_free[:] = arena_free
            (ah, al), (xh, xl) = a_at(), x_at()
            return project_to_h((lambda k: ah(k) if k < 4 else xh(k), lambda k: al(k) if k < 4 else xl(k)), KC, done)

        def moba_gmlp(h_ready):
            qk, values, gates = view(0, NT, 2 * HEADS_M, DM), view(2048, NT, HEADS_M, P), view(4096, NT, 2 * D)
            uv = view(8192, NT, 2 * G_W)
            qt, kt = view(10240, HEADS_M, T), view(12288, HEADS_M // 2, T)
            sc, ex = view(13312, 2, BLK), view(14336, 3, BLK)
            wm, row = shaped(one_j, G_GRP, P), one_i[:, D:D + G_W]
            got_w = small_load(wm, a["gmlp_w"], *row_free)
            got_row = small_load(row, a["gmlp_g"].partition_broadcast(P))
            cleared = [clear(qt), clear(values)]
            x_ready = lift(h_chunk, KC, lambda k: gain("mix2", k), x_hi, x_lo, by_chunk(h_ready))
            r = inv_rms(h_tile, D, flat(h_ready))
            act.wait(r, *cleared)
            dve.wait(r, *cleared)
            masked = dve.do(lambda e, now: e.tensor_tensor(
                wm, wm, const("tri").unsqueeze(1).broadcast_to([P, G_GRP, P]), ALU.mult), got_w)
            flat_qk = qk.rearrange("p t h d -> p t (h d)")
            parts, uvs, gs = {}, {}, {}

            def leave(n, t, psum, done):
                if n < 2:
                    parts[n, t] = scale_out(t, psum, done, flat_qk[:, t, n * BLK:(n + 1) * BLK])
                    return [parts[n, t]]
                if n == 2:
                    parts[n, t] = values_out(t, psum, done, values[:, t, :, :], HEADS_M)
                    return [parts[n, t]]
                place, func, at = (uv, ACT.Gelu_apprx_tanh, n - 3) if n < 5 else (gates, ACT.Sigmoid, n - 5)
                store = uvs if n < 5 else gs
                store[at, t] = act.do(lambda e, now: e.activation(
                    place[:, t, at * BLK:(at + 1) * BLK], psum, func, scale=rstd(t)), done)
                return [store[at, t]]

            proj = project_steps(*x_at(), KC, 9, BLK, x_ready, leave, banks=(6, 7))
            for _ in range(4):
                next(proj)
            cos, sin = trig("trig_m", DM // 2, 2 * HEADS_M)
            next(proj)
            rot = rotate(qk[:, :, :, 0:32], qk[:, :, :, 32:64], cos, sin, shaped(arena[:, 13312:14336], NT, 16, 32),
                         shaped(arena[:, 14336:15360], NT, 16, 32), [parts[n, t] for n in range(2) for t in range(NT)])
            for _ in range(3):
                next(proj)
            tq, tk, done = [], [], [[] for _ in range(4)]
            run_all(turn_steps(lambda t, i: flat_qk[:, t, i * P:(i + 1) * P], P, 4,
                               halves(qt, lambda i: 2 * i, lambda i: 2 * i + 1), [rot], tq, DM ** -0.5))
            run_all(turn_steps(lambda t, i: flat_qk[:, t, 512 + i * P:512 + (i + 1) * P], P, 4, whole(kt), [rot], tk))
            run_all(attention_steps(
                HEADS_M, up_to, lambda hd, n: qt[:, hd, n * P:(n + 1) * P], lambda hd: kt[:, hd // 2, :],
                lambda hd, t: values[:, t, hd, :], causal, a_at(),
                tq + tk + [parts[2, t] for t in range(NT)], sc, ex, done), proj)
            v_at = lambda t: uv[:, t, 512:1024]
            r = inv_rms(v_at, G_W, [uvs[1, 0], uvs[1, 1]], 24)
            vn = [dve.do(lambda e, now, t=t: e.scalar_tensor_tensor(
                v_at(t), v_at(t), rstd(t, 24), row, ALU.mult, ALU.mult), r, got_row) for t in range(NT)]
            outs = [[], []]

            def weigh(first):
                def leave(n, t, psum, done):
                    place = gates[:, t, first + n * BLK:first + (n + 1) * BLK]
                    r = dve.do(lambda e, now: e.tensor_tensor(place, psum, place, ALU.mult), done, gs[first // BLK + n, t])
                    if first:
                        into = gates[:, t, n * BLK:(n + 1) * BLK]
                        outs[n].append(dve.do(lambda e, now: e.tensor_tensor(into, into, place, ALU.add), r))
                    return [r]
                return leave

            project(*a_at(), 4, 2, BLK, done, weigh(0))
            uz = []
            for t in range(NT):
                pe.wait(*free[6 + t], vn[t], masked)
                for grp in range(G_GRP):
                    pe.put(lambda e, now, t=t, grp=grp: e.matmul(
                        bank[6 + t][:, grp * 64:(grp + 1) * 64], wm[:, grp, :],
                        uv[:, t, 512 + grp * 64:512 + (grp + 1) * 64], start=True, stop=True))
                m = mark_last_pe()
                at, _ = GAINS["bs"]
                z = dve.do(lambda e, now, t=t: e.tensor_tensor(
                    v_at(t).rearrange("p (g d) -> p g d", g=G_GRP),
                    bank[6 + t][:, :].rearrange("p (g d) -> p g d", g=G_GRP),
                    gains[:, at:at + G_GRP].unsqueeze(2).broadcast_to([P, G_GRP, 64]), ALU.add), m)
                uz.append(dve.do(lambda e, now, t=t: e.tensor_tensor(
                    uv[:, t, 0:512], uv[:, t, 0:512], v_at(t), ALU.mult), z, uvs[0, t]))
                free[6 + t] = [z]
            lb = lift(lambda t, k: uv[:, t, k * P:(k + 1) * P], 4, None, x_hi, x_lo, [uz] * 4)
            project(*x_at(), 4, 2, BLK, lb, weigh(D), banks=(4, 5, 0, 1))
            x_ready = lift(lambda t, k: gates[:, t, k * P:(k + 1) * P], KC, None, x_hi, x_lo, by_chunk(outs))
            out = project_to_h(x_at(), KC, x_ready)
            arena_free[:] = flat(out)
            return out

        def cross_attention(h_ready):
            mem, kn, vn, qn = view(0, NT, D), view(2048, NT, 512), view(3072, NT, 512), view(4096, NT, 512)
            qt, kt = view(5120, HEADS_X, T), view(6144, HEADS_X, T)
            sc, ex = view(7168, 2, BLK), view(8192, 3, BLK)
            got_mem = small_load(mem, a["mem"].rearrange("(t p) d -> p t d", p=P), *arena_free)
            m_ready = lift(lambda t, k: mem[:, t, k * P:(k + 1) * P], KC, lambda k: gain("mem", k), x_hi, x_lo,
                           [[got_mem]] * KC)
            r = inv_rms(lambda t: mem[:, t, :], D, [got_mem], 32)
            act.wait(r)
            dve.wait(r)
            parts, parts_q, tk, tq, done = {}, [], [], [], [[] for _ in range(4)]

            def leave(n, t, psum, done):
                parts[n, t] = scale_out(t, psum, done, (kn, vn)[n][:, t, :], 32)
                return [parts[n, t]]

            def leave_q(n, t, psum, done):
                parts_q.append(scale_out(t, psum, done, qn[:, t, :]))
                return parts_q[-1:]

            project(*x_at(), KC, 2, BLK, m_ready, leave)
            x_ready = lift(h_chunk, KC, lambda k: gain("xa", k), x_hi, x_lo, by_chunk(h_ready))
            r = inv_rms(h_tile, D, flat(h_ready))
            act.wait(r)
            dve.wait(r)
            project(*x_at(), KC, 1, BLK, x_ready, leave_q, banks=(4, 5))
            run_all(turn_steps(lambda t, i: kn[:, t, i * P:(i + 1) * P], P, HEADS_X, whole(kt),
                               [parts[0, 0], parts[0, 1]], tk))
            run_all(turn_steps(lambda t, i: qn[:, t, i * P:(i + 1) * P], P, HEADS_X, whole(qt), parts_q, tq, DX ** -0.5))
            run_all(attention_steps(
                HEADS_X, lambda n: [0, 1], lambda hd, n: qt[:, hd, n * P:(n + 1) * P], lambda hd: kt[:, hd, :],
                lambda hd, t: vn[:, t, hd * DX:(hd + 1) * DX], None, a_at(),
                tk + tq + [parts[1, 0], parts[1, 1]], sc, ex, done, wide=True))
            arena_free[:] = [done[-1][-1]]
            return project_to_h(a_at(), 4, done)

        def peer(h_ready):
            N_BLK, PER = 4, 4
            n_pairs = NT * HEADS_P
            n_lists = n_pairs * 2
            qn, qt, keys = view(0, NT, 2048), view(4096, 16, T), view(8192, 16, NKEYS)
            sc = view(10240, n_lists, NKEYS)
            best, where = view(14336, n_lists, TOPK), view(14848, n_lists, TOPK).bitcast(U32)
            place, value = view(15360, n_pairs, TOPK).bitcast(U32), view(15616, n_pairs, TOPK)
            cand = view(15872, PER, N_CAND)
            routed = view(16384, 640).bitcast(BF16).rearrange("p (a t) -> p a t", t=T)
            names = ("expv", "row_i", "col_i", "lt", "a1", "a2", "b1", "b2")
            buf = {n: view(i * 256, n_pairs, TOPK) for i, n in enumerate(names)}
            where_f, total, rest = view(2048, n_lists, TOPK), view(2560, n_pairs, 1), view(2576, T)
            ranks = view(2832, 256).bitcast(BF16).rearrange("p (s l k) -> p s l k", s=2, k=TOPK)
            by_rank = [view(4096 + 2048 * i, 2048).bitcast(BF16).rearrange("p (l a k) -> p l a k", a=TOPK, k=TOPK)
                       for i in range(2)]
            match = view(8192, 2048).bitcast(BF16).rearrange("p (l a k) -> p l a k", a=TOPK, k=TOPK)
            rank_rep = view(3088, 128).bitcast(BF16).rearrange("p (a k) -> p a k", a=TOPK)

            got_keys = small_load(keys, a["subkeys"], *arena_free)
            x_ready = lift(h_chunk, KC, lambda k: gain("ffn", k), x_hi, x_lo, by_chunk(h_ready))
            r = inv_rms(h_tile, D, flat(h_ready))
            act.wait(r)
            dve.wait(r)
            parts = {}
            dve.do(lambda e, now: e.tensor_copy(iota_rep[:, :, :], const("iota").unsqueeze(2).broadcast_to([P, NKEYS, OCT])))

            def leave(n, t, psum, done):
                parts[n, t] = scale_out(t, psum, done, qn[:, t, n * BLK:(n + 1) * BLK])
                return [parts[n, t]]

            def top16(lists, ready):
                for cols in (slice(0, 8), slice(8, 16)):
                    t1 = [dve.do(lambda e, now, src=src, best=best, cols=cols: e.max(best[:, cols], src), *ready)
                          for src, best, _ in lists]
                    t2 = [dve.do(lambda e, now, src=src, best=best, at=at, cols=cols: e.max_index(
                        at[:, cols], best[:, cols], src), t1[i]) for i, (src, best, at) in enumerate(lists)]
                    if cols.start == 0:
                        ready = [dve.do(lambda e, now, src=src, best=best, cols=cols: e.match_replace(
                            src, best[:, cols], src, NEG * 1e3), t2[i]) for i, (src, best, _) in enumerate(lists)][-1:]
                return t2[-1]

            found, chosen = {}, {}

            def route(n):
                tq, scs = [], []
                yield from turn_steps(lambda t, i: qn[:, t, (PER * n + i) * P:(PER * n + i + 1) * P], P, PER,
                                      whole(qt[:, PER * n:PER * n + PER, :]), [parts[n, 0], parts[n, 1]], tq,
                                      banks=(0, 1))
                pe.wait(*tq, got_keys)
                for t in range(NT):
                    b = 2 + t
                    pe.wait(*free[b])
                    for i in range(PER):
                        pe.put(lambda e, now, b=b, i=i, t=t: e.matmul(
                            bank[b][:, i * P:(i + 1) * P], qt[:, PER * n + i, t * P:(t + 1) * P], keys[:, PER * n + i, :],
                            start=True, stop=True))
                    m = mark_last_pe()
                    l0 = t * 16 + PER * n
                    scs.append(act.do(lambda e, now, b=b, l0=l0: e.activation(
                        sc[:, l0:l0 + PER, :], bank[b][:, :].rearrange("p (a b) -> p a b", a=PER), ACT.Copy), m))
                    free[b] = scs[-1:]
                for t in range(NT):
                    l0 = t * 16 + PER * n
                    found[n, t] = top16([(sc[:, l0 + i, :], best[:, l0 + i, :], where[:, l0 + i, :])
                                         for i in range(PER)], [scs[t]])
                    yield
                sides = best.rearrange("p (l s) k -> p l s k", s=2)
                pairs = [t * HEADS_P + 2 * n + i for t in range(NT) for i in range(2)]
                for i, l in enumerate(pairs):
                    for r0, r1, cols, at in ((0, WHOLE_ROWS, TOPK, 0), (WHOLE_ROWS, TOPK, PART_COLS, WHOLE_ROWS * TOPK)):
                        cd = dve.do(lambda e, now, i=i, l=l, r0=r0, r1=r1, cols=cols, at=at: e.tensor_tensor(
                            cand[:, i, at:at + (r1 - r0) * cols].rearrange("p (a b) -> p a b", b=cols),
                            sides[:, l, 0, r0:r1].unsqueeze(2).broadcast_to([P, r1 - r0, cols]),
                            sides[:, l, 1, 0:cols].unsqueeze(1).broadcast_to([P, r1 - r0, cols]), ALU.add),
                            found[n, 0], found[n, 1], *chosen.values())
                chosen[n] = top16([(cand[:, i, :], value[:, l, :], place[:, l, :])
                                   for i, l in enumerate(pairs)], [cd])
                yield

            table = view(0, T, JH)

            def activate(c, t, psum, done, turned):
                r = act.do(lambda e, now: e.activation(mid[:, t, :], psum[:, :], ACT.Gelu_apprx_tanh, scale=rstd(t)),
                           done, turned)
                return [r], [r]

            def weigh(c, b, psum, turned, down_done):
                j = g.count("column", 2) - 2
                base = weigh.base
                both = gated[:, 2 * b:2 * b + 2, :]
                m = dve.do(lambda e, now: e.tensor_tensor(
                    both, psum.rearrange("p (f t) -> p f t", f=2),
                    table[:, :, bass.ds(now(j, "column") - base, 2)].rearrange("p t j -> p j t"), ALU.mult),
                    turned, weigh.read.get(b))
                hl = split_a(b, both.rearrange("p f t -> p (f t)"), m, down_done)
                weigh.read[b] = hl[1]
                return [m], hl

            weigh.read = {}

            proj = project_steps(*x_at(), KC, N_BLK, BLK, x_ready, leave, banks=(4, 5, 6, 7))
            next(proj)
            next(proj)
            routes = []
            for n in range(N_BLK):
                routes.append(route(n))
                for _ in range(2):
                    next(routes[n])
                    for r_ in routes[:n]:
                        next(r_, None)
                    next(proj, None)
            pipe = Gated(EC, activate, weigh, None)
            ready = pipe.up(0)
            run_all(*routes)

            last = chosen[N_BLK - 1]
            d1 = dve.do(lambda e, now: e.tensor_tensor(
                buf["expv"], value, value[:, :, 0:1].broadcast_to([P, n_pairs, TOPK]), ALU.subtract), last)
            d2 = act.do(lambda e, now: e.activation(buf["expv"], buf["expv"], ACT.Exp), d1)
            wf = dve.do(lambda e, now: e.tensor_copy(where_f, where))
            keys_of = where_f.rearrange("p (l s) k -> p l s k", s=2)
            wide = [act.do(lambda e, now, side=side: e.activation(
                by_rank[side], keys_of[:, :, side, :].unsqueeze(3).broadcast_to([P, n_pairs, TOPK, TOPK]), ACT.Copy), wf)
                for side in range(2)]
            u32 = {n: buf[n].bitcast(U32) for n in ("a1", "a2", "b1", "b2")}
            shift = WHOLE_ROWS * TOPK // PART_COLS - WHOLE_ROWS
            rr = dve.do(lambda e, now: e.tensor_copy(
                rank_rep, const("iota")[:, 0:TOPK].unsqueeze(2).broadcast_to([P, TOPK, TOPK])))
            s1 = dve.do(lambda e, now: e.tensor_scalar(u32["a1"], place, 4, None, ALU.logical_shift_right))
            s2 = dve.do(lambda e, now: e.tensor_scalar(u32["a2"], place, 2, None, ALU.logical_shift_right))
            s3 = dve.do(lambda e, now: e.tensor_scalar(u32["b1"], place, 3, None, ALU.bitwise_and))
            s4 = dve.do(lambda e, now: e.tensor_scalar(u32["b2"], place, 12, None, ALU.bitwise_and))
            f0 = dve.do(lambda e, now: e.tensor_copy(buf["lt"], place))
            f1 = dve.do(lambda e, now: e.tensor_copy(buf["a1"], u32["a1"]), s1)
            f2 = dve.do(lambda e, now: e.tensor_copy(buf["a2"], u32["a2"]), s2)
            f3 = dve.do(lambda e, now: e.tensor_copy(buf["b1"], u32["b1"]), s3)
            f4 = dve.do(lambda e, now: e.tensor_copy(buf["b2"], u32["b2"]), s4)
            ra = dve.do(lambda e, now: e.scalar_tensor_tensor(
                ranks[:, 0, :, :], buf["a2"], float(-shift), buf["a1"], ALU.add, ALU.max), f1, f2)
            m1 = dve.do(lambda e, now: e.scalar_tensor_tensor(
                buf["b2"], buf["lt"], float(WHOLE_ROWS * TOPK), buf["b2"], ALU.is_lt, ALU.mult), f0, f4)
            rb = dve.do(lambda e, now: e.tensor_tensor(ranks[:, 1, :, :], buf["b2"], buf["b1"], ALU.add), m1, f3)
            d3 = dve.do(lambda e, now: e.reduce_sum(total, buf["expv"], AX), d2)
            d4 = dve.do(lambda e, now: e.reciprocal(total, total), d3)
            weight = dve.do(lambda e, now: e.tensor_tensor(
                buf["expv"], buf["expv"], total.broadcast_to([P, n_pairs, TOPK]), ALU.mult), d4)
            last, looked = None, []
            for side, to in enumerate(("row_i", "col_i")):
                last = dve.do(lambda e, now, side=side: e.tensor_tensor(
                    match, ranks[:, side, :, :].unsqueeze(2).broadcast_to([P, n_pairs, TOPK, TOPK]),
                    rank_rep.unsqueeze(1).broadcast_to([P, n_pairs, TOPK, TOPK]), ALU.is_equal), ra, rb, rr, last)
                last = dve.do(lambda e, now, side=side: e.tensor_tensor(match, match, by_rank[side], ALU.mult),
                              last, wide[side])
                n = TOPK // 2
                while n:
                    dst = buf[to].unsqueeze(2) if n == 1 else match[:, :, 0:n, :]
                    last = dve.do(lambda e, now, n=n, dst=dst: e.tensor_tensor(
                        dst, match[:, :, 0:n, :], match[:, :, n:2 * n, :], ALU.add), last)
                    n //= 2
                looked.append(last)
            for i, name in enumerate(("expv", "row_i", "col_i")):
                b = min(i, 1)
                pe.wait(*free[b], weight if i == 0 else looked[i - 1])
                for t in range(NT):
                    at = (i == 2) * T + t * P
                    transpose_to(bank[b][:, at:at + P],
                                 buf[name][:, t * HEADS_P:(t + 1) * HEADS_P, :].rearrange("p l k -> p (l k)"))
                if i == 0:
                    m = mark_last_pe()
                    v1 = act.do(lambda e, now: e.activation(routed[:, 2, :], bank[0][:, 0:T], ACT.Copy), m)
                    w1 = dve.do(lambda e, now: e.tensor_tensor(rest, bank[0][:, 0:T], routed[:, 2, :], ALU.subtract), v1)
                    w2 = dve.do(lambda e, now: e.tensor_copy(routed[:, 3, :], rest), w1)
                    w3 = dve.do(lambda e, now: e.tensor_tensor(routed[:, 4, :], rest, routed[:, 3, :], ALU.subtract), w2)
                    free[0] = [w1]
            m = mark_last_pe()
            v2 = act.do(lambda e, now: e.activation(routed[:, 0:2, :].rearrange("p a b -> p (a b)"), bank[1][:, :], ACT.Copy), m)
            free[1] = [v2]

            hot_free = {}
            hot_i = one_j.bitcast(BF16).rearrange("p (s n t) -> p s n t", s=2, t=OCT)
            hot_j = one_i.bitcast(BF16).rearrange("p (s k n t) -> p s k n t", s=2, k=4, t=OCT)

            def scatter(half, ready):
                dve.wait(*ready)
                made = []

                def octet(i, base):
                    slot = i % 2
                    u = g.count("token", OCT) - OCT
                    at = lambda now: now(u, "token") if base == 0 else now(u, "token") - base

                    def token_cols(now, first, k, n):
                        cols = routed[:, first:first + k, bass.ds(at(now), OCT)]
                        return cols.unsqueeze(2).broadcast_to([P, k, n, OCT])

                    rows_ = dve.do(lambda e, now: e.tensor_tensor(
                        hot_i[:, slot, :, :].unsqueeze(1), iota_rep[:, :, :].unsqueeze(1), token_cols(now, 0, 1, NKEYS),
                        ALU.is_equal), hot_free.get(slot))
                    c1 = dve.do(lambda e, now: e.tensor_tensor(
                        hot_j[:, slot, 0:1, :, :], iota_rep[:, half * JH:(half + 1) * JH, :].unsqueeze(1),
                        token_cols(now, 1, 1, JH), ALU.is_equal))
                    cols_ = dve.do(lambda e, now: e.tensor_tensor(
                        hot_j[:, slot, 1:4, :, :], hot_j[:, slot, 0:1, :, :].broadcast_to([P, 3, JH, OCT]),
                        token_cols(now, 2, 3, JH), ALU.mult), c1)
                    b = 6 + slot
                    pe.wait(rows_, cols_, *free[b])
                    for j in range(OCT):
                        for k in range(3):
                            pe.put(lambda e, now, j=j, k=k: e.matmul(
                                bank[b][:, j * JH:(j + 1) * JH], hot_i[:, slot, :, j], hot_j[:, slot, 1 + k, :, j],
                                start=k == 0, stop=k == 2))
                    hot_free[slot] = mark_last_pe()
                    r = act.do(lambda e, now: e.activation(
                        table[:, bass.ds(at(now), OCT), :], bank[b][:, :].rearrange("p (a b) -> p a b", a=OCT), ACT.Copy),
                        hot_free[slot])
                    free[b] = [r]
                    made.append(r)

                base = g.counts.get("token", 0)
                act.wait(*ready)
                octet(0, base)
                octet(1, base)
                with g.loop(T // OCT // 2 - 1):
                    octet(2, base)
                    octet(3, base)
                return made[-1:]

            last_done = [w3, v2]
            n_chunks = JH // EC
            for half in range(2):
                if half:
                    ready = pipe.up(0)
                    pipe.down()
                    last_done += [weigh.read[0], weigh.read[1]]
                filled = scatter(half, last_done)
                dve.wait(*filled)
                weigh.base = g.counts.get("column", 0)
                pipe.back(0, ready)
                pipe.chunk(1)
                with g.loop((n_chunks - 4) // 3):
                    for c in range(3):
                        pipe.chunk(c)
                pipe.chunk(2)
                pipe.chunk(3)
                last_done = []
            row_free[:] = list(hot_free.values())
            pipe.down(last=True)
            return add_to_h(1.0, pipe.half_done, h_ready)

        pe.wait(got_consts)
        act.wait(got_gains, got_consts)
        dve.wait(got_gains, got_consts)
        engines = (pe, act, dve, pool, sp)

        def stages():
            ready = [[got_h], [got_h]]
            for l in range(DEPTH):
                ready = ffn(f"ffa{l}", ready)
                yield f"ffa{l}", ready
                ready = even_mixer(ready) if l == 0 else odd_mixer(ready)
                yield f"mix{l}", ready
                ready = ffn(f"ffb{l}", ready)
                yield f"ffb{l}", ready
                ready = ple(l, ready)
                yield f"ple{l}", ready
            ready = norm_rows("final_norm", ready)
            yield "first", ready
            ready = moba_gmlp(ready)
            yield "moba", ready
            ready = cross_attention(ready)
            yield "cross", ready
            ready = peer(ready)
            yield "peer", ready
            ready = norm_rows("final_g", ready)
            yield "all", ready

        for name, ready in stages():
            if name == (stop or "all"):
                return finish(nc, ctx, a, h, ready, sem, engines)


def finish(nc, ctx, a, out, ready, sem, engines):
    pe, act, dve, pool, sp = engines
    s_out = sem("stored")
    sp.wait(sp.load(s_out, lambda e, now: e.dma_start(
        a["out"].rearrange("(t p) d -> p t d", p=P), out[:, :, :]), *ready[0], *ready[1]))
    block = ctx.enter_context(nc.Block())
    block.tensor(pe.run)
    block.scalar(act.run)
    block.vector(dve.run)
    block.gpsimd(pool.run)
    block.sync(sp.run)


def pack(w, width=BLK):
    k, n = w.shape
    nb = -(-n // width)
    full = np.zeros((k, nb * width), w.dtype)
    full[:, :n] = w
    blocks = full.reshape(k // P, P, nb, width).transpose(2, 0, 1, 3).reshape(-1, P, width)
    nu = -(-len(blocks) // UB)
    out = np.zeros((nu * UB, P, BLK), w.dtype)
    out[:len(blocks), :, :width] = blocks
    return out.reshape(nu, UB, P, BLK).transpose(0, 2, 1, 3)


def pack_pipeline(up, down, c_up, c_down):
    parts = [up[:c_up]]
    n = len(up) // c_up
    for c in range(1, n):
        parts += [up[c * c_up:(c + 1) * c_up], down[(c - 1) * c_down:c * c_down]]
    return np.concatenate(parts + [down[(n - 1) * c_down:]])


def pack_ffn(gate_up, down):
    gu = gate_up.reshape(D, 2, NFC, FC).transpose(0, 2, 1, 3).reshape(D, 2 * FF)
    dn = down.reshape(FF // P, P, 2, BLK).transpose(0, 2, 1, 3).reshape(-1, UB, P, BLK).transpose(0, 2, 1, 3)
    return pack_pipeline(pack(gu), dn, 2, 1)


def lay_out(x):
    def rows(w):
        return w.reshape(-1, P, w.shape[-1]).transpose(1, 0, 2).reshape(P, -1)

    stream = []
    for l in range(DEPTH):
        stream.append(pack_ffn(x["ffa_w_gate_up"][l], x["ffa_w_down"][l]))
        if l == 0:
            w_in = x["ev_w_in"][0]
            n_q = HEADS_A * DA
            q = w_in[:, :n_q].reshape(D, KV_A, HEADS_A // KV_A, DA).transpose(0, 2, 1, 3).reshape(D, n_q)
            stream += [pack(np.concatenate([q, w_in[:, n_q:]], 1)), pack(x["ev_w_uq"][0], 384), pack(x["ev_w_ukv"][0]), pack(x["ev_w_out"][0])]
        else:
            w_in = x["od_w_in"][0][:, :3 * D].reshape(D, 3, 2, BLK)
            stream += [pack(w_in.transpose(0, 2, 1, 3).reshape(D, 3 * D)), pack(x["od_w_out"][0])]
        stream += [pack_ffn(x["ffb_w_gate_up"][l], x["ffb_w_down"][l]), pack(x["ple_w_gate"][l]), pack(x["ple_w_proj"][l])]
    for name in ("w_in", "moba_w_proj", "gmlp_w_proj", "w_out", "xa_w_kv", "xa_w_q", "xa_w_o", "peer_w_q"):
        stream.append(pack(x[name + "_2"][0]))
    down = x["peer_w_down_2"][0].reshape(NKEYS, NKEYS, D).transpose(2, 1, 0).reshape(D, NKEYS * NKEYS)
    up = x["peer_w_up_2"][0].reshape(NKEYS, NKEYS, 2, BLK).transpose(1, 2, 0, 3)
    up = up.reshape(-1, UB, P, BLK).transpose(0, 2, 1, 3)
    stream.append(pack_pipeline(pack(down), up, 2, 2))
    gains = [None] * len(GAINS)
    cols = {"cq": x["ev_cq_norm"][0], "ckv": x["ev_ckv_norm"][0], "mix2": x["norm_mix_g_2"][0],
            "xa": x["norm_xa_g_2"][0], "mem": x["norm_mem_g_2"][0], "ffn": x["norm_ffn_g_2"][0], "bs": x["gmlp_b_s_2"][0]}
    for l in range(DEPTH):
        for n in ("ffa", "mix", "ffb", "ple"):
            cols[f"{n}{l}"] = x[f"{n}_norm"][l]
    gains = np.concatenate([cols[n].reshape(-1, P).T for n in GAINS], 1)
    consts, alibi = constants()
    return {
        "w": np.concatenate(stream).reshape(-1), "x": x["x"][0], "gains": gains, "consts": consts, "alibi": alibi,
        "p0": rows(x["p"][0, 0].T), "p1": rows(x["p"][1, 0].T), "sinks": x["ev_sinks"][0],
        "w_f": rows(x["od_w_in"][0][:, 3 * D:]), "b_f": x["od_b_f"][0], "final_norm": x["final_norm"],
        "gmlp_w": x["gmlp_w_s_2"][0].transpose(2, 0, 1).reshape(P, -1), "gmlp_g": x["gmlp_norm_g_2"][0],
        "mem": x["mem_2"][0], "subkeys": x["peer_subkeys_2"][0].transpose(3, 0, 1, 2).reshape(P, -1),
        "final_g": x["final_g_2"],
    }


def kernel(stop=None, **inputs):
    import concourse.bacc as bacc
    from concourse.bass_utils import run_bass_kernel_spmd

    arrays = {n: np.ascontiguousarray(v) for n, v in lay_out({k: np.asarray(v) for k, v in inputs.items()}).items()}
    nc = bacc.Bacc("TRN2", target_bir_lowering=False, num_devices=1)
    a = {n: nc.dram_tensor(f"in_{n}", v.shape, F32, kind="ExternalInput").ap() for n, v in arrays.items()}
    a["out"] = nc.dram_tensor("out", (T, D), F32, kind="ExternalOutput").ap()
    build(nc, a, stop)
    got = run_bass_kernel_spmd(nc, [{f"in_{n}": v for n, v in arrays.items()}], core_ids=[0])
    return got.results[0]["out"].reshape(1, T, D)
```

```python
from contextlib import ExitStack, contextmanager

import concourse.bass as bass
from concourse import mybir
import numpy as np

F32 = mybir.dt.float32
F32R = mybir.dt.float32r
U32 = mybir.dt.uint32
BF16 = mybir.dt.bfloat16
ACT = mybir.ActivationFunctionType
ALU = mybir.AluOpType
AX = mybir.AxisListType.X

P = 128
T, D = 256, 1024
NT, KC = T // P, D // P
BLK, UB = 512, 4
FF, FC = 2816, 256
NFC = FF // FC
DEPTH = 2
EPS = 1e-6
HEADS_A, KV_A, DA = 8, 2, 64
HEADS_B, NOPE, ROPE_B, DVB = 8, 64, 32, 64
QLORA, KVLORA = 256, 128
HEADS_C, DC = 16, 64
HEADS_M, DM = 8, 64
G_GRP, G_W = 8, 512
HEADS_X, DX = 4, 128
HEADS_P, NKEYS, TOPK = 8, 128, 16
NEG = -1e30
WHOLE_ROWS, PART_COLS = 4, 4
N_CAND = WHOLE_ROWS * TOPK + (TOPK - WHOLE_ROWS) * PART_COLS
OCT = 8
JH = NKEYS // 2
EC = 4
RING = 3
LEAD = 2


def units(k, n, width=BLK):
    return -(-(k // P) * -(-n // width) // UB)


def stream_plan():
    ffn = NFC * 3
    plan = []
    for l in range(DEPTH):
        plan.append((f"ffa{l}", ffn))
        if l == 0:
            plan += [("ev_in", 6), ("uq", 1), ("ukv", 1), ("ev_out", units(D, D))]
        else:
            plan += [("od_in", units(D, 3 * D)), ("od_out", units(D, D))]
        plan += [(f"ffb{l}", ffn), (f"ple_gate{l}", units(D, D)), (f"ple_proj{l}", 1)]
    plan += [("in2", units(D, 4608)), ("moba", units(512, D)), ("gmlp", units(512, D)),
             ("xkv", units(D, D)), ("out2", units(D, D)), ("xq", units(D, 512)), ("xo", units(512, D)),
             ("peer_q", units(D, 2048)), ("peer", NKEYS // EC * 4)]
    return plan


N_UNITS = sum(n for _, n in stream_plan())

def columns(items):
    at, out = 0, {}
    for name, n in items:
        out[name] = (at, n)
        at += n
    return out, at


GAINS, N_GAINS = columns(
    [(f"{n}{l}", KC) for l in range(DEPTH) for n in ("ffa", "mix", "ffb", "ple")]
    + [("cq", QLORA // P), ("ckv", 1), ("mix2", KC), ("xa", KC), ("mem", KC), ("ffn", KC), ("final", KC), ("bs", G_GRP)])
CONSTS, N_CONSTS = columns(
    [("ident", P), ("power", NT), ("trig_b", NT * 2 * (ROPE_B // 2)), ("trig_m", NT * 2 * (DM // 2)),
     ("upto", NT * T), ("iota", NKEYS), ("causal", T), ("tri", P)])


def constants():
    c = np.zeros((P, N_CONSTS), np.float32)

    def put(name, a):
        at, n = CONSTS[name]
        c[:, at:at + n] = a.reshape(P, n)

    r = np.arange(P)
    put("ident", np.eye(P))
    put("causal", np.concatenate([np.zeros((P, P)), np.where(r[None, :] <= r[:, None], 0, NEG)], 1))
    for name, dim in (("trig_b", ROPE_B), ("trig_m", DM)):
        inv = np.float32(10000.0) ** (-np.arange(0, dim, 2, dtype=np.float32) / np.float32(dim))
        ang = (np.arange(T, dtype=np.float32)[:, None] * inv[None, :].astype(np.float32)).astype(np.float64)
        tab = np.stack([np.cos(ang), np.sin(ang)], 1)
        put(name, tab.reshape(NT, P, 2, dim // 2).transpose(1, 0, 2, 3))
    s = np.arange(T).reshape(NT, P)
    put("upto", (s[:, :, None] <= np.arange(T)[None, None, :]).transpose(1, 0, 2))
    put("iota", np.tile(np.arange(NKEYS), (P, 1)))
    put("power", np.full((P, NT), -0.5))
    put("tri", r[:, None] <= r[None, :])
    slopes = 2.0 ** (-8.0 * np.arange(1, HEADS_A + 1) / HEADS_A)
    dist = r[:, None] + P - np.arange(2 * P)[None, :]
    band = (dist >= 0) & (dist < P)
    alibi = np.where(band[:, None, :], -slopes[None, :, None] * dist[:, None, :], NEG)
    return c, alibi.reshape(P, -1).astype(np.float32)


class Ticket:

    def __init__(self, sem, value):
        self.sem, self.value = sem, value


class Later:

    def __init__(self, make):
        self.make, self.made = make, None

    def __iter__(self):
        if self.made is None:
            self.made = list(self.make())
        return iter(self.made)


class Program:
    def __init__(self):
        self.engines, self.made = [], None
        self.counts = {}

    def count(self, key, by):
        self.counts[key] = self.counts.get(key, 0) + by
        return self.counts[key]

    def ticket(self, sem, by):
        t = Ticket(sem, self.count(sem, by))
        if self.made is not None:
            self.made.append(t)
        return t

    @contextmanager
    def loop(self, n):
        before = dict(self.counts)
        outer = [e.items for e in self.engines]
        for e in self.engines:
            e.items, e.seen = [], {}
        self.made = []
        yield
        step = {k: v - before.get(k, 0) for k, v in self.counts.items()}
        for e, items in zip(self.engines, outer):
            body, e.items, e.seen = e.items, items, {}
            if body:
                e.items.append((n, body, step))
        for k, v in step.items():
            self.counts[k] += v * (n - 1)
        for t in self.made:
            t.value += step[t.sem] * (n - 1)
        self.made = None


class Engine:
    def __init__(self, program, sem):
        self.program, self.sem, self.items, self.seen = program, sem, [], {}
        program.engines.append(self)

    def wait(self, *tickets):
        for t in tickets:
            if t is not None and self.seen.get(t.sem, 0) < t.value:
                self.seen[t.sem] = t.value
                self.items.append(lambda e, now, s=t.sem, v=t.value: e.wait_ge(s, now(v, s)))

    def do(self, emit, *waits):
        self.wait(*waits)
        self.items.append(lambda e, now: emit(e, now).then_inc(self.sem, 1))
        return self.program.ticket(self.sem, 1)

    def put(self, emit, *waits):
        self.wait(*waits)
        self.items.append(emit)

    def load(self, sem, emit, *waits):
        self.wait(*waits)
        self.items.append(lambda e, now: emit(e, now).then_inc(sem, 16))
        return self.program.ticket(sem, 16)

    def load_dynamic(self, sem, address, emit, wait):
        need = (wait.sem, wait.value) if wait is not None else None

        def both(e, now):
            at = address(now)
            at = at if isinstance(at, int) else e.snap(at)
            if need is not None:
                count = now(need[1], need[0])
                e.wait_ge(need[0], count if isinstance(count, int) else e.snap(count))
            emit(e, at).then_inc(sem, 16)
        self.items.append(both)
        return self.program.ticket(sem, 16)

    def run(self, e):
        def emit(items, now):
            for item in items:
                if isinstance(item, tuple):
                    n, body, step = item
                    with e.Fori(0, n) as i:
                        emit(body, lambda v, k: v + i * step[k] if step.get(k) else v)
                else:
                    item(e, now)
        emit(self.items, lambda v, k: v)


def build(nc, a, stop=None):
    with ExitStack() as ctx:
        def sb(name, cols, dt=F32):
            return ctx.enter_context(nc.sbuf_tensor(name, [P] + list(cols), dt))

        def sem(name):
            return ctx.enter_context(nc.semaphore(name))

        g = Program()
        pe, act, dve = Engine(g, sem("pe_done")), Engine(g, sem("act_done")), Engine(g, sem("dve_done"))
        pool, sp = Engine(g, sem("pool_done")), Engine(g, sem("sp_done"))

        raw = sb("raw", [RING, UB, BLK])
        w_hi, w_lo = sb("w_hi", [RING, UB, BLK], F32R), sb("w_lo", [RING, UB, BLK], F32R)
        h = sb("h", [NT, D])
        x_hi, x_lo = sb("x_hi", [KC, T], F32R), sb("x_lo", [KC, T], F32R)
        a_hi, a_lo = sb("a_hi", [EC, T], F32R), sb("a_lo", [EC, T], F32R)
        mid = sb("mid", [NT, BLK])
        gated = sb("gated", [EC, T])
        gains, consts = sb("gains_sb", [N_GAINS]), sb("consts_sb", [N_CONSTS])
        small = sb("small", [128])
        one_i, one_j = sb("one_i", [2048])[:, :], sb("one_j", [1024])[:, :]
        iota_rep = sb("iota_rep", [NKEYS, OCT], BF16)
        f_hi, f_lo = sb("f_hi", [KC, HEADS_C], F32R), sb("f_lo", [KC, HEADS_C], F32R)
        arena = sb("arena", [17408])
        bank = [ctx.enter_context(nc.psum_tensor(f"bank{b}", [P, BLK], F32)) for b in range(8)]

        def const(name):
            at, n = CONSTS[name]
            return consts[:, at:at + n]

        def gain(name, k):
            return gains[:, GAINS[name][0] + k:GAINS[name][0] + k + 1]

        ident = const("ident")

        s_small = sem("small_loads")

        def small_load(dst, src, *waits):
            t = pool.load(s_small, lambda e, now: e.dma_start(dst, src), *waits)
            pool.wait(t)
            return t

        s_first = [sem(f"first_load{i}") for i in range(5)]
        n_soon = CONSTS["trig_b"][0]
        got_consts = sp.load(s_first[0], lambda e, now: e.dma_start(consts[:, 0:n_soon], a["consts"][:, 0:n_soon]))
        got_h = [sp.load(s_first[1 + i], lambda e, now, i=i: e.dma_start(
            h[:, :, i * BLK:(i + 1) * BLK], a["x"][:, i * BLK:(i + 1) * BLK].rearrange("(t p) d -> p t d", p=P)))
            for i in range(2)]
        got_gains = sp.load(s_first[3], lambda e, now: e.dma_start(gains[:, :], a["gains"]))

        s_raw = [sem(f"unit_loaded{i}") for i in range(RING)]
        loaded, split, used = {}, {}, [None] * RING
        raw_read = [(None,)] * RING

        def load_unit():
            u = g.count("loaded", 1) - 1
            if u >= N_UNITS:
                return
            s = u % RING
            loaded[s] = sp.load_dynamic(
                s_raw[s], lambda now: now(u, "loaded") * (P * UB * BLK),
                lambda e, at: e.dma_start(raw[:, s, :, :].rearrange("p b n -> p (b n)"),
                                          a["w"][bass.ds(at, P * UB * BLK)].rearrange("(p n) -> p n", p=P)),
                *raw_read[s])

        remainder = [dve]

        def split_unit():
            u = g.count("split", 1) - 1
            if u >= N_UNITS:
                return
            s = u % RING
            hi = act.do(lambda e, now: e.activation(w_hi[:, s, :, :], raw[:, s, :, :], ACT.Copy),
                        loaded[s], used[s])
            lo = remainder[0].do(lambda e, now: e.tensor_tensor(w_lo[:, s, :, :], raw[:, s, :, :],
                                                       w_hi[:, s, :, :].bitcast(F32), ALU.subtract),
                        loaded[s], used[s], hi)
            split[s] = (hi, lo)
            raw_read[s] = (lo,)

        def take_unit():
            u = g.count("taken", 1) - 1
            split_unit()
            load_unit()
            pe.wait(*split[u % RING])
            return u % RING

        for _ in range(LEAD):
            load_unit()
        got_later = sp.load(s_first[4], lambda e, now: e.dma_start(consts[:, n_soon:], a["consts"][:, n_soon:]))
        for _ in range(LEAD, RING):
            load_unit()

        def product(out, s, b, width, hi, lo, start, stop):
            for n, (l, w) in enumerate(((hi, w_hi), (hi, w_lo), (lo, w_hi))):
                pe.put(lambda e, now, n=n, l=l, w=w: e.matmul(
                    out, l, w[:, s, b, 0:width], start=start and n == 0, stop=stop and n == 2))

        def mark_last_pe():
            last = pe.items.pop()
            pe.items.append(lambda e, now: last(e, now).then_inc(pe.sem, 1))
            return g.ticket(pe.sem, 1)

        free = [[] for _ in range(8)]

        def transpose_to(out, src, *waits):
            pe.put(lambda e, now: e.transpose(out, src, ident[0:src.shape[0], 0:src.shape[0]]), *waits)

        def by_chunk(halves):
            return [halves[k * P // BLK] for k in range(KC)]

        def flat(lists):
            return [t for ts in lists for t in ts]

        def lift(src, chunks, gain_of, hi, lo, ready, banks=(6, 7, 2, 3), then=None):
            def pair(k0):
                b = banks[(k0 // 2) % len(banks)]
                pe.wait(*free[b])
                ks = range(k0, min(k0 + 2, chunks))
                for k in ks:
                    for t in range(NT):
                        at = (k - k0) * T + t * P
                        transpose_to(bank[b][:, at:at + P], src(t, k), *ready[k])
                turned = mark_last_pe()
                readers = []
                for k in ks:
                    part = bank[b][:, (k - k0) * T:(k - k0 + 1) * T]
                    scale = gain_of(k) if gain_of else 1.0
                    up = act.do(lambda e, now, k=k, part=part, scale=scale: e.activation(
                        hi[:, k, :], part, ACT.Copy, scale=scale), turned)
                    readers.append(up)
                for k in ks:
                    part = bank[b][:, (k - k0) * T:(k - k0 + 1) * T]
                    if gain_of:
                        down = dve.do(lambda e, now, k=k, part=part, scale=gain_of(k): e.scalar_tensor_tensor(
                            lo[:, k, :], part, scale, hi[:, k, :].bitcast(F32), ALU.mult, ALU.subtract), up)
                    else:
                        down = dve.do(lambda e, now, k=k, part=part: e.tensor_tensor(
                            lo[:, k, :], part, hi[:, k, :].bitcast(F32), ALU.subtract), up)
                    readers.append(down)
                free[b] = readers
                return readers

            done = []
            for k0 in range(0, min(chunks, UB), 2):
                done += [pair(k0)] * min(2, chunks - k0)

            def rest():
                made = [pair(k0) for k0 in range(UB, chunks, 2)]
                if then:
                    then()
                return flat(made)

            if chunks > UB:
                list(ready[UB])
                done += [Later(rest)] * (chunks - UB)
            return done

        def normed_operand(name, ready, *waits, banks=(6, 7, 2, 3)):
            def then():
                r = inv_rms(h_tile, D, flat(ready))
                act.wait(r, *waits)
                dve.wait(r, *waits)
            return lift(h_chunk, KC, lambda k: gain(name, k), x_hi, x_lo, by_chunk(ready), banks, then)

        def inv_rms(src, width, ready, col=0):
            junk = gated[:, :, :].rearrange("p a b -> p (a b)")
            sums = []
            for t in range(NT):
                sums.append(act.do(lambda e, now, t=t: e.activation(
                    junk[:, 0:width], src(t), ACT.Square, accum_out=small[:, col + t:col + t + 1]),
                    *ready, *sums[-1:], *junk_free))
            junk_free[:] = sums[-1:]
            mean = dve.do(lambda e, now: e.tensor_scalar(small[:, col + 2:col + 4], small[:, col:col + 2],
                                                         1.0 / width, EPS, ALU.mult, ALU.add), sums[-1])
            return pool.do(lambda e, now: e.tensor_tensor(small[:, col + 4:col + 6], small[:, col + 2:col + 4],
                                                          const("power"), ALU.pow), mean)

        junk_free = []

        def rstd(t, col=0):
            return small[:, col + 4 + t:col + 5 + t]

        def project_steps(hi, lo, chunks, blocks, width, ready, leave, banks=(4, 5, 0, 1)):
            slot = None
            for n in range(blocks):
                w = width[n] if isinstance(width, (list, tuple)) else width
                pair = banks[2 * n % len(banks)], banks[(2 * n + 1) % len(banks)]
                for b in pair:
                    pe.wait(*free[b])
                done = [None] * NT
                for k0 in range(0, chunks, UB):
                    ks = range(k0, min(k0 + UB, chunks))
                    if (n * chunks + k0) % UB == 0:
                        if slot is not None:
                            yield
                        slot = take_unit()
                    for t in range(NT):
                        if n == 0 and k0 == 0 and t == 1:
                            list(ready[-1])
                        for k in ks:
                            if n == 0:
                                pe.wait(*ready[k])
                            product(bank[pair[t]][:, 0:w], slot, (n * chunks + k) % UB, w,
                                    hi(k)[:, t * P:(t + 1) * P], lo(k)[:, t * P:(t + 1) * P],
                                    k == 0, k == chunks - 1)
                        done[t] = mark_last_pe()
                    used[slot] = done[NT - 1]
                for t in range(NT):
                    free[pair[t]] = leave(n, t, bank[pair[t]][:, 0:w], done[t])
            yield

        def run_all(*steps):
            steps = list(steps)
            while steps:
                steps = [x for x in steps if next(x, "end") != "end"]

        def project(*args, **more):
            run_all(project_steps(*args, **more))

        def x_at(first=0):
            return (lambda k: x_hi[:, first + k, :]), (lambda k: x_lo[:, first + k, :])

        def a_at(first=0):
            return (lambda k: a_hi[:, first + k, :]), (lambda k: a_lo[:, first + k, :])

        ACC, GU, TR = (0, 1, 2, 3), (4, 5), (6, 7)

        class Gated:

            def __init__(self, nf, activate, turn, x_ready, first=True):
                self.nf, self.activate, self.turn, self.first = nf, activate, turn, first
                self.a_ready, self.down_done, self.x_ready = [], None, x_ready

            def down(self, last=False):
                if self.first:
                    for b in ACC:
                        pe.wait(*free[b])
                pe.wait(*self.a_ready)
                per = UB // 2
                for f0 in range(0, self.nf, per):
                    s = take_unit()
                    for half in range(2):
                        for f in range(f0, f0 + per):
                            for t in range(NT):
                                product(bank[2 * t + half][:, :], s, 2 * (f - f0) + half, BLK,
                                        a_hi[:, f, t * P:(t + 1) * P], a_lo[:, f, t * P:(t + 1) * P],
                                        self.first and f == 0, last and f == self.nf - 1)
                        self.half_done[half] = mark_last_pe()
                    used[s] = self.down_done = self.half_done[1]
                self.first = False

            def chunk(self, c, meanwhile=None):
                ready = self.up(c, meanwhile)
                self.down()
                self.back(c, ready)

            def up(self, c, meanwhile=None):
                for u in range(2):
                    s = take_unit()
                    done = []
                    for t in range(NT):
                        if u == 0:
                            pe.wait(*free[GU[t]])
                        if self.x_ready and t == 1:
                            list(self.x_ready[-1])
                        for k in range(UB):
                            kk = u * UB + k
                            if self.x_ready:
                                pe.wait(*self.x_ready[kk])
                            product(bank[GU[t]][:, :], s, k, BLK, x_hi[:, kk, t * P:(t + 1) * P],
                                    x_lo[:, kk, t * P:(t + 1) * P], kk == 0, kk == KC - 1)
                        done.append(mark_last_pe())
                    used[s] = done[-1]
                    if u == 0 and meanwhile:
                        meanwhile()
                self.x_ready, ready = None, []
                for t in range(NT):
                    readers, r = self.activate(c, t, bank[GU[t]], done[t], self.turned)
                    free[GU[t]] = readers
                    ready += r
                return ready

            def back(self, c, ready):
                pe.wait(*ready)
                for b in range(self.nf // 2):
                    pe.wait(*free[TR[b]])
                    for f in (2 * b, 2 * b + 1):
                        for t in range(NT):
                            at = (f % 2) * T + t * P
                            transpose_to(bank[TR[b]][:, at:at + P], mid[:, t, f * P:(f + 1) * P])
                    self.turned = mark_last_pe()
                    free[TR[b]], r = self.turn(c, b, bank[TR[b]], self.turned, self.down_done)
                    self.a_ready = r if b == 0 else self.a_ready + r

            turned = None
            half_done = [None, None]

        def split_a(b, src, done, *waits):
            hi = act.do(lambda e, now: e.activation(a_hi[:, 2 * b:2 * b + 2, :].rearrange("p f t -> p (f t)"),
                                                    src, ACT.Copy), done, *waits)
            lo = dve.do(lambda e, now: e.tensor_tensor(
                a_lo[:, 2 * b:2 * b + 2, :].rearrange("p f t -> p (f t)"), src,
                a_hi[:, 2 * b:2 * b + 2, :].rearrange("p f t -> p (f t)").bitcast(F32), ALU.subtract), hi)
            return [hi, lo]

        def add_to_h(scale, done, ready):
            def adds(half):
                out = []
                for t in range(NT):
                    cols = h[:, t, half * BLK:(half + 1) * BLK]
                    out.append(dve.do(lambda e, now, b=2 * t + half, cols=cols: e.scalar_tensor_tensor(
                        cols, bank[b][:, :], scale, cols, ALU.mult, ALU.add), done[half], *flat(ready)))
                return out

            out = [adds(0), Later(lambda: adds(1))]
            for b in ACC:
                free[b] = out[b % 2]
            return out

        h_tile = lambda t: h[:, t, :]
        h_chunk = lambda t, k: h[:, t, k * P:(k + 1) * P]

        def ffn(name, h_ready, first=False):
            x_ready = normed_operand(name, h_ready)
            for _ in range(LEAD if first else 0):
                split_unit()
                load_unit()
            def activate(c, t, psum, done, turned):
                silu = act.do(lambda e, now: e.activation(gated[:, t, :], psum[:, 0:FC], ACT.Silu, scale=rstd(t)),
                              done, turned)
                both = dve.do(lambda e, now: e.scalar_tensor_tensor(
                    mid[:, t, 0:FC], psum[:, FC:2 * FC], rstd(t), gated[:, t, :], ALU.mult, ALU.mult), done, silu)
                return [silu, both], [both]

            def turn(c, b, psum, turned, down_done):
                both = split_a(b, psum[:, :], turned, down_done)
                return both, both

            p = Gated(2, activate, turn, x_ready)
            ready = p.up(0)
            p.chunk(1, lambda: p.back(0, ready))
            with g.loop(NFC - 2):
                p.chunk(2)
            p.down(last=True)
            return add_to_h(0.5, p.half_done, h_ready)

        arena_free = [None]

        def view(at, *dims):
            return shaped(arena[:, at:at + int(np.prod(dims))], *dims)

        def shaped(cols, *dims):
            if len(dims) == 1:
                return cols
            names = "abcd"[:len(dims)]
            return cols.rearrange(f"p ({' '.join(names)}) -> p {' '.join(names)}",
                                  **{x: d for x, d in zip(names[1:], dims[1:])})


        def turn_steps(src, rows, n, places, ready, done, scale=1.0, banks=(0, 1, 2, 3), share=True):
            for i0 in range(0, n, 2):
                b = banks[(i0 // 2) % len(banks)]
                pe.wait(*free[b], *ready)
                m = min(2, n - i0)
                for i in range(i0, i0 + m):
                    for t in range(NT):
                        at = (i - i0) * T + t * P
                        transpose_to(bank[b][0:rows, at:at + P], src(t, i))
                turned = mark_last_pe()
                for r0, r1, c0, c1, place in places(i0, m):
                    if share and i0 % 4:
                        last = dve.do(lambda e, now, b=b, r0=r0, r1=r1, c0=c0, c1=c1, place=place: e.tensor_scalar(
                            place, bank[b][r0:r1, c0:c1], scale, None, ALU.mult), turned)
                    else:
                        last = act.do(lambda e, now, b=b, r0=r0, r1=r1, c0=c0, c1=c1, place=place: e.activation(
                            place, bank[b][r0:r1, c0:c1], ACT.Copy, scale=scale), turned)
                free[b] = [last]
                done.append(last)
                yield

        def whole(dst, rows=P):
            return lambda i, m: [(0, rows, 0, m * T, dst[0:rows, i:i + m, :].rearrange("p a b -> p (a b)"))]

        def halves(dst, top, bottom):
            def places(i, m):
                out = []
                for j in range(m):
                    out.append((0, 64, j * T, (j + 1) * T, dst[0:64, top(i + j), :]))
                    out.append((64, P, j * T, (j + 1) * T, dst[64:P, bottom(i + j), :]))
                return out
            return places

        def scale_out(t, psum, done, place, col=0):
            if t == 0:
                return act.do(lambda e, now: e.activation(place, psum, ACT.Copy, scale=rstd(t, col)), done)
            return dve.do(lambda e, now: e.tensor_scalar(place, psum, rstd(t, col), None, ALU.mult), done)

        def values_out(t, psum, done, padded, heads, col=0, side=None):
            psum = psum.rearrange("p (h d) -> p h d", d=64)
            if side is not None:
                return scale_out(t, psum, done, padded[:, :, side * 64:(side + 1) * 64], col)
            for odd in range(2):
                r = scale_out(t, psum[:, odd:heads:2, :], done, padded[:, odd:heads:2, odd * 64:(odd + 1) * 64], col)
            return r

        def project_to_h(operand, chunks, ready):
            left, out = [[], []], [None, None]

            def adds(n):
                return [dve.do(lambda e, now, t=t, psum=psum: e.tensor_tensor(
                    h[:, t, n * BLK:(n + 1) * BLK], psum, h[:, t, n * BLK:(n + 1) * BLK], ALU.add), done)
                    for t, psum, done in left[n]]

            def leave(n, t, psum, done):
                left[n].append((t, psum, done))
                if t == 0:
                    out[n] = Later(lambda: adds(n))
                elif n == 0:
                    list(out[0])
                return out[n]

            project(*operand, chunks, 2, BLK, ready, leave)
            return out

        stat = sb("stat", [5, 2 * HEADS_C])

        def attention_steps(heads, keys, q, k, v, bias, out, ready, sc, ex, done, sink=None, wide=False):
            ext = mid
            steps = [(n, h0) for n in range(NT) for h0 in range(0, heads, 2)]
            totals, sunk, scaled, copies, values = {}, {}, {}, {}, {}
            pe.wait(*ready)
            dve.wait(*ready)

            def col(i, s):
                return stat[:, i, 2 * (s % HEADS_C):2 * (s % HEADS_C) + 2]

            for s in range(len(steps) + 4):
                now_s, norm_s, turn_s, value_s, split_s = (0 <= s - i < len(steps) for i in range(5))
                if split_s:
                    r, (rn, rh) = s - 4, steps[s - 4]
                    b, parts = 4 + r % 2, []
                    for i, c in enumerate((rh, rh + 1) if wide else (rh // 2,)):
                        hi, lo = out[0](c)[:, rn * P:(rn + 1) * P], out[1](c)[:, rn * P:(rn + 1) * P]
                        psum = bank[b][:, i * P:(i + 1) * P]
                        up = act.do(lambda e, now, hi=hi, psum=psum: e.activation(hi, psum, ACT.Copy), values[r])
                        parts.append((c, hi, lo, psum))
                if now_s:
                    n, h0 = steps[s]
                    nk = len(keys(n)) * P
                    k0 = keys(n)[0] * P
                    b = s % 2
                    pe.wait(*free[b])
                    for j in range(2):
                        pe.put(lambda e, now, b=b, j=j, n=n, hd=h0 + j, k0=k0, nk=nk: e.matmul(
                            bank[b][:, j * nk:(j + 1) * nk], q(hd, n), k(hd)[:, k0:k0 + nk], start=True, stop=True))
                    scored = mark_last_pe()
                    scores = bank[b][:, 0:2 * nk].rearrange("p (a b) -> p a b", a=2)
                    soft = sc[:, b, 0:2 * nk].rearrange("p (a b) -> p a b", a=2)
                    if bias is None:
                        soft, biased = scores, scored
                    else:
                        biased = dve.do(lambda e, now, n=n, h0=h0, soft=soft, scores=scores: e.tensor_tensor(
                            soft, scores, bias(n, h0), ALU.add), scored, totals.get(s - 2))
                    low = dve.do(lambda e, now, s=s, soft=soft: e.tensor_reduce(
                        col(1, s), soft, AX, ALU.max, negate=True), biased)
                if turn_s:
                    r = s - 2
                    m = 2 * len(keys(steps[r][0]))
                    b = 2 + r % 2
                    pe.wait(*free[b], *scaled[r])
                    for j in range(m):
                        transpose_to(bank[b][:, j * P:(j + 1) * P], ex[:, r % 3, j * P:(j + 1) * P])
                    turned = mark_last_pe()
                    copies[r] = act.do(lambda e, now, b=b, r=r, m=m: e.activation(
                        ext[:, r % 2, 0:m * P], bank[b][:, 0:m * P], ACT.Copy), turned, values.get(r - 2))
                    free[b] = [copies[r]]
                if norm_s:
                    total = totals[s - 1]
                    if sink is not None:
                        total = dve.do(lambda e, now, r=s - 1: e.tensor_tensor(col(2, r), col(2, r), col(3, r), ALU.add),
                                       total, sunk[s - 1])
                if now_s:
                    if sink is not None:
                        low = dve.do(lambda e, now, s=s, h0=h0: e.tensor_tensor(
                            col(1, s), col(1, s), sink[:, h0:h0 + 2], ALU.min), low)
                    for j in range(2):
                        totals[s] = act.do(lambda e, now, s=s, j=j, soft=soft, nk=nk: e.activation(
                            ex[:, s % 3, j * nk:(j + 1) * nk], soft[:, j, :], ACT.Exp, bias=col(1, s)[:, j:j + 1],
                            accum_out=col(2, s)[:, j:j + 1]), low)
                    free[s % 2] = [totals[s]] if bias is None else [biased]
                if norm_s:
                    m = len(keys(steps[s - 1][0])) * P
                    inv = dve.do(lambda e, now, r=s - 1: e.reciprocal(col(4, r), col(2, r)), total)
                if now_s and sink is not None:
                    gap = dve.do(lambda e, now, s=s, h0=h0: e.tensor_tensor(
                        col(3, s), col(1, s), sink[:, h0:h0 + 2], ALU.subtract), low)
                    sunk[s] = act.do(lambda e, now, s=s: e.activation(col(3, s), col(3, s), ACT.Exp), gap)
                if norm_s:
                    scaled[s - 1] = [dve.do(lambda e, now, r=s - 1, m=m, j=j: e.tensor_scalar(
                        ex[:, r % 3, j * m:(j + 1) * m], ex[:, r % 3, j * m:(j + 1) * m],
                        col(4, r)[:, j:j + 1], None, ALU.mult), inv) for j in range(2)]
                if split_s:
                    for c, hi, lo, psum in parts:
                        down = dve.do(lambda e, now, hi=hi, lo=lo, psum=psum: e.tensor_tensor(
                            lo, psum, hi.bitcast(F32), ALU.subtract), up)
                        done[c] += [up, down]
                    free[4 + (s - 4) % 2] = [down]
                if value_s:
                    r = s - 3
                    rn, rh = steps[r]
                    tiles = keys(rn)
                    b = 4 + r % 2
                    pe.wait(*free[b], copies[r])
                    for j in range(2):
                        for i, tile in enumerate(tiles):
                            pe.put(lambda e, now, b=b, j=j, i=i, tile=tile, r=r, rh=rh, m=len(tiles): e.matmul(
                                bank[b][:, (j if wide else 0) * P:(j + 1 if wide else 1) * P], v(rh + j, tile),
                                ext[:, r % 2, (j * m + i) * P:(j * m + i + 1) * P],
                                start=i == 0 and (wide or j == 0), stop=i == m - 1 and (wide or j == 1)))
                    values[r] = mark_last_pe()
                yield

        def rotate(x1, x2, cos, sin, t1, t2, ready):
            dve.wait(*ready)
            a1 = dve.do(lambda e, now: e.tensor_tensor(t1, x1, sin, ALU.mult))
            a2 = dve.do(lambda e, now: e.tensor_tensor(t2, x2, sin, ALU.mult))
            b1 = dve.do(lambda e, now: e.tensor_tensor(x1, x1, cos, ALU.mult), a1)
            b2 = dve.do(lambda e, now: e.tensor_tensor(x2, x2, cos, ALU.mult), a2)
            dve.do(lambda e, now: e.tensor_tensor(x1, x1, t2, ALU.subtract), b1)
            return dve.do(lambda e, now: e.tensor_tensor(x2, x2, t1, ALU.add), b2)

        def causal(n, h0):
            mask = const("causal")
            mask = mask[:, P:T] if n == 0 else mask
            return mask.unsqueeze(1).broadcast_to([P, 2, (n + 1) * P])

        up_to = lambda n: list(range(n + 1))

        def trig(name, half, heads):
            tab = const(name).rearrange("p (t c f) -> p t c f", t=NT, c=2)
            return [tab[:, :, c, :].unsqueeze(2).broadcast_to([P, NT, heads, half]) for c in range(2)]

        def clear(cols):
            return pool.do(lambda e, now: e.memset(cols, 0.0), *arena_free)

        def ple(l, h_ready):
            p_in, g_out = view(14848, 2, T), view(15360, NT, D)
            got = small_load(p_in, a[f"p{l}"], *arena_free)
            x_ready = normed_operand(f"ple{l}", h_ready)
            hi = act.do(lambda e, now: e.activation(a_hi[:, 0:2, :], p_in, ACT.Copy), got, *flat(h_ready))
            lo = dve.do(lambda e, now: e.tensor_tensor(a_lo[:, 0:2, :], p_in, a_hi[:, 0:2, :].bitcast(F32),
                                                       ALU.subtract), hi)
            gates = {}

            def gate(n, t, psum, done):
                gates[n, t] = act.do(lambda e, now: e.activation(
                    g_out[:, t, n * BLK:(n + 1) * BLK], psum, ACT.Sigmoid, scale=rstd(t)), done)
                return [gates[n, t]]

            project(*x_at(), KC, 2, BLK, x_ready, gate)
            left, out = [[], []], [None, None]

            def adds(n):
                tickets = []
                for t, psum, done in left[n]:
                    cols = slice(n * BLK, (n + 1) * BLK)
                    m = dve.do(lambda e, now, t=t, psum=psum, cols=cols: e.tensor_tensor(
                        g_out[:, t, cols], psum, g_out[:, t, cols], ALU.mult), done, gates[n, t])
                    tickets.append(dve.do(lambda e, now, t=t, cols=cols: e.tensor_tensor(
                        h[:, t, cols], h[:, t, cols], g_out[:, t, cols], ALU.add), m))
                return tickets

            def leave(n, t, psum, done):
                left[n].append((t, psum, done))
                if t == 0:
                    out[n] = Later(lambda: adds(n))
                elif n == 0:
                    list(out[0])
                return out[n]

            project(*a_at(), 2, 2, BLK, [[hi, lo]] * 2, leave, banks=(4, 5, 0, 1))
            return out

        def norm_rows(name, h_ready):
            row = one_i[:, 0:D]
            got = small_load(row, a[name].partition_broadcast(P), *row_free)
            r = inv_rms(h_tile, D, flat(h_ready))
            out = [[], []]
            for half in range(2):
                for t in range(NT):
                    cols = slice(half * BLK, (half + 1) * BLK)
                    out[half].append(dve.do(lambda e, now, t=t, cols=cols: e.scalar_tensor_tensor(
                        h[:, t, cols], h[:, t, cols], rstd(t), row[:, cols], ALU.mult, ALU.mult), r, got))
            return out

        row_free = []

        def even_mixer(h_ready):
            N_IN, W = 1184, NOPE + ROPE_B
            pin, v_a = view(0, NT, N_IN), view(2400, NT, KV_A, 2, P)
            qt_a, kt_a = view(3424, HEADS_A, T), view(5472, 1, T)
            qb, kcat, v_b = view(5728, NT, HEADS_B, W), view(7264, NT, HEADS_B, W), view(8800, NT, HEADS_B, P)
            qt_b, kt_b = view(10848, HEADS_B, T), view(12896, HEADS_B, T)
            ex, tmp = view(14944, 3, BLK), view(16480, 576)
            sc = shaped(one_j, 2, BLK)
            sinks = small[:, 64:64 + HEADS_A]
            alibi = one_i.rearrange("p (h k) -> p h k", h=HEADS_A)
            got_alibi = small_load(one_i, a["alibi"])
            got_sinks = small_load(sinks, a["sinks"].partition_broadcast(P))
            cleared = [clear(x) for x in (qt_a, v_a, v_b)]
            x_ready = normed_operand("mix0", h_ready, *cleared)
            neg = dve.do(lambda e, now: e.tensor_scalar(sinks, sinks, -1.0, None, ALU.mult), got_sinks)
            parts = {}

            def leave(n, t, psum, done):
                w = min(BLK, N_IN - n * BLK)
                parts[n, t] = scale_out(t, psum[:, 0:w], done, pin[:, t, n * BLK:n * BLK + w])
                if n == 1:
                    v = psum[:, 128:256]
                    for side in range(2):
                        parts[n, t] = values_out(t, v, done, v_a[:, t, :, side, :], KV_A, side=side)
                return [parts[n, t]]

            project(*x_at(), KC, 3, [BLK, BLK, 256], x_ready, leave, banks=(4, 5, 6, 7))

            def latent():
                cq = lambda t, k: pin[:, t, 768 + k * P:768 + (k + 1) * P]
                ckv = lambda t, k: pin[:, t, 1024:1152]
                p1, p2 = [parts[1, 0], parts[1, 1]], [parts[2, 0], parts[2, 1]]
                l1 = lift(cq, 2, lambda k: gain("cq", k), x_hi, x_lo, [p1] * 2, banks=(6,))
                l2 = lift(ckv, 1, lambda k: gain("ckv", k), x_hi[:, 2:3, :], x_lo[:, 2:3, :], [p2], banks=(7,))
                r1 = inv_rms(lambda t: pin[:, t, 768:1024], QLORA, p1, 8)
                r2 = inv_rms(lambda t: pin[:, t, 1024:1152], KVLORA, p2, 16)
                act.wait(r1, r2)
                dve.wait(r1, r2)
                yield
                flat_q = qb.rearrange("p t h d -> p t (h d)")
                parts_q, parts_kv = [], []

                def leave_q(n, t, psum, done):
                    parts_q.append(scale_out(t, psum, done, flat_q[:, t, n * 384:(n + 1) * 384], 8))
                    return parts_q[-1:]

                def leave_kv(n, t, psum, done):
                    heads = psum.rearrange("p (h d) -> p h d", d=NOPE + DVB)
                    h0, m = n * 4, 4
                    scale_out(t, heads[:, :, 0:NOPE], done, kcat[:, t, h0:h0 + m, 0:NOPE], 16)
                    for odd in range(2):
                        r = scale_out(t, heads[:, odd:m:2, NOPE:], done,
                                      v_b[:, t, h0 + odd:h0 + m:2, odd * 64:(odd + 1) * 64], 16)
                    parts_kv.append(r)
                    return [r]

                half = ROPE_B // 2
                k4 = pin[:, :, 1152:1184].unsqueeze(2)
                t3, t4 = (shaped(tmp[:, 512 + i * 32:512 + (i + 1) * 32], NT, 1, half) for i in range(2))
                cos, sin = trig("trig_b", half, 1)
                rk = rotate(k4[:, :, :, 0:half], k4[:, :, :, half:], cos, sin, t3, t4, p2)
                kr = [dve.do(lambda e, now, t=t: e.tensor_copy(
                    kcat[:, t, :, NOPE:], pin[:, t, 1152:1184].unsqueeze(1).broadcast_to([P, HEADS_B, ROPE_B])), rk)
                    for t in range(NT)]
                yield from project_steps(*x_at(), 2, 2, 384, l1, leave_q, banks=(4, 5, 6, 7))
                t1, t2 = (shaped(tmp[:, i * 256:(i + 1) * 256], NT, HEADS_B, half) for i in range(2))
                cos, sin = trig("trig_b", half, HEADS_B)
                rq = rotate(qb[:, :, :, NOPE:NOPE + half], qb[:, :, :, NOPE + half:], cos, sin, t1, t2, parts_q)
                yield from project_steps(*x_at(2), 1, 2, BLK, l2, leave_kv, banks=(4, 5, 6, 7))
                ready_q.extend([rq])
                ready_k.extend(parts_kv + kr)

            def turn_latent():
                yield from turn_steps(lambda t, i: qb[:, t, i, :], W, HEADS_B, whole(qt_b, W), ready_q, ready_b,
                                      W ** -0.5, banks=(6, 7))
                yield from turn_steps(lambda t, i: kcat[:, t, i, :], W, HEADS_B, whole(kt_b, W), ready_k,
                                      ready_b, banks=(6, 7))

            ready_q, ready_k = [], []
            ready_b, done_a, done_b = [], [[] for _ in range(4)], [[] for _ in range(4)]
            all_parts = list(parts.values())
            ta, tk = [], []
            run_all(latent(), turn_steps(lambda t, i: pin[:, t, i * P:(i + 1) * P], P, 4,
                                         halves(qt_a, lambda i: i, lambda i: i + 4), all_parts, ta, DA ** -0.5,
                                         banks=(0, 1)),
                    turn_steps(lambda t, i: pin[:, t, 512:640], P, 1, whole(kt_a), all_parts, tk, banks=(2,)))
            run_all(attention_steps(
                HEADS_A, up_to, lambda hd, n: qt_a[:, hd, n * P:(n + 1) * P], lambda hd: kt_a[:, 0, :],
                lambda hd, t: v_a[:, t, hd // 4, hd % 2, :],
                lambda n, h0: alibi[:, h0:h0 + 2, (P if n == 0 else 0):T], a_at(),
                ta + tk + [got_alibi, neg] + all_parts, sc, ex, done_a, sink=sinks), turn_latent())
            run_all(attention_steps(
                HEADS_B, up_to, lambda hd, n: qt_b[0:W, hd, n * P:(n + 1) * P], lambda hd: kt_b[0:W, hd, :],
                lambda hd, t: v_b[:, t, hd, :], causal, x_at(4), ready_b, sc, ex, done_b))
            arena_free[:] = [done_b[-1][-1]]
            (ah, al), (xh, xl) = a_at(), x_at()
            return project_to_h((lambda k: ah(k) if k < 4 else xh(k), lambda k: al(k) if k < 4 else xl(k)), KC,
                                done_a + done_b)

        def odd_mixer(h_ready):
            W, SC = DC + 2, DC ** -0.5
            q_in, k_in = view(0, NT, HEADS_C, W), view(2112, NT, HEADS_C, W)
            values = view(4224, NT, HEADS_C, P)
            qt, kt = view(8320, HEADS_C, T), view(12416, HEADS_C, T)
            sc, ex = shaped(one_j, 2, BLK), shaped(one_i[:, 0:3 * BLK], 3, BLK)
            tmp = one_i[:, 3 * BLK:]
            f_raw, bf, zt = shaped(tmp[:, 0:128], KC, HEADS_C), tmp[:, 128:144], tmp[:, 144:400]
            z, nz, lf = (shaped(tmp[:, 400 + i * 32:432 + i * 32], NT, HEADS_C) for i in range(3))
            got_f = small_load(f_raw, a["w_f"], *arena_free)
            got_b = small_load(bf, a["b_f"].partition_broadcast(P))
            cleared = [clear(values)]
            cleared.append(pool.do(lambda e, now: e.memset(q_in[:, :, :, DC:DC + 1], 1.0 / SC), *arena_free))
            cleared.append(pool.do(lambda e, now: e.memset(k_in[:, :, :, DC + 1:], 1.0), *arena_free))
            x_ready = normed_operand("mix1", h_ready, *cleared, banks=(0, 2, 1, 3))
            fh = act.do(lambda e, now: e.activation(f_hi[:, :, :], f_raw, ACT.Copy), got_f)
            fl = dve.do(lambda e, now: e.tensor_tensor(f_lo[:, :, :], f_raw, f_hi[:, :, :].bitcast(F32), ALU.subtract), fh)

            def forget():
                pe.wait(fh, fl, *free[0], *free[1])
                for k in range(KC):
                    for i, (w, x) in enumerate(((f_hi, x_hi), (f_lo, x_hi), (f_hi, x_lo))):
                        pe.put(lambda e, now, k=k, w=w, x=x, i=i: e.matmul(
                            bank[0][0:HEADS_C, 0:T], w[:, k, :], x[:, k, :],
                            start=k == 0 and i == 0, stop=k == KC - 1 and i == 2))
                m = mark_last_pe()
                c = dve.do(lambda e, now: e.tensor_copy(zt[0:HEADS_C, :], bank[0][0:HEADS_C, 0:T]), m)
                yield
                pe.wait(c)
                for t in range(NT):
                    transpose_to(bank[1][:, t * HEADS_C:(t + 1) * HEADS_C], zt[0:HEADS_C, t * P:(t + 1) * P])
                m = mark_last_pe()
                for t in range(NT):
                    d = dve.do(lambda e, now, t=t: e.scalar_tensor_tensor(
                        z[:, t, :], bank[1][:, t * HEADS_C:(t + 1) * HEADS_C], rstd(t), bf, ALU.mult, ALU.add), m, got_b)
                n1 = dve.do(lambda e, now: e.tensor_scalar(nz, z, -1.0, None, ALU.mult), d)
                n2 = dve.do(lambda e, now: e.tensor_tensor(nz, z, nz, ALU.min), n1)
                e1 = act.do(lambda e, now: e.activation(lf, nz, ACT.Exp), n2)
                e2 = act.do(lambda e, now: e.activation(lf, lf, ACT.Ln, bias=1.0), e1)
                n3 = dve.do(lambda e, now: e.tensor_scalar(z, z, 0.0, None, ALU.min))
                n4 = dve.do(lambda e, now: e.tensor_tensor(lf, z, lf, ALU.subtract), n3, e2)
                yield
                upto = shaped(const("upto"), NT, T)
                pe.wait(n4, c, d)
                for n in range(NT):
                    for s in range(n + 1):
                        pe.put(lambda e, now, n=n, s=s: e.matmul(
                            bank[0][:, n * 16:(n + 1) * 16], upto[:, s, n * P:(n + 1) * P], lf[:, s, :],
                            start=s == 0, stop=s == n))
                m = mark_last_pe()
                sums = shaped(bank[0][:, 0:NT * HEADS_C], NT, HEADS_C, 1)
                to_q = dve.do(lambda e, now: e.tensor_scalar(q_in[:, :, :, DC + 1:], sums, 1.0 / SC, None, ALU.mult), m)
                to_k = dve.do(lambda e, now: e.tensor_scalar(k_in[:, :, :, DC:DC + 1], sums, -1.0, None, ALU.mult), m)
                free[0], free[1] = [to_k], [d]
                forgets.extend([to_q, to_k])
                yield

            forgets, parts = [], {}

            def leave(n, t, psum, done):
                kind, h0 = n % 3, n // 3 * 8
                if kind == 2:
                    parts[n, t] = values_out(t, psum, done, values[:, t, h0:h0 + 8, :], 8)
                else:
                    place = (q_in, k_in)[kind][:, t, h0:h0 + 8, 0:DC]
                    parts[n, t] = scale_out(t, psum.rearrange("p (h d) -> p h d", d=DC), done, place)
                return [parts[n, t]]

            proj = project_steps(*x_at(), KC, 6, BLK, x_ready, leave, banks=(4, 5, 6, 7, 4, 5) + (6, 7) * 3)
            next(proj)
            next(proj)
            fg = forget()
            for _ in range(4):
                next(fg, None)
                next(proj)
            turned, done = [[], []], [[] for _ in range(8)]

            def turn_in(half, banks):
                for src, dst, kind, scale in ((q_in, qt, 0, SC), (k_in, kt, 1, 1.0)):
                    ready = forgets + [parts[3 * half + kind, t] for t in range(NT)]
                    yield from turn_steps(lambda t, i, src=src: src[:, t, 8 * half + i, :], W, 8,
                                          whole(dst[:, 8 * half:8 * half + 8, :], W), ready, turned[half], scale, banks)

            def attend(half, out):
                h0 = 8 * half
                return attention_steps(
                    8, up_to, lambda hd, n: qt[0:W, h0 + hd, n * P:(n + 1) * P], lambda hd: kt[0:W, h0 + hd, :],
                    lambda hd, t: values[:, t, h0 + hd, :], causal, out,
                    turned[half] + [parts[3 * half + 2, t] for t in range(NT)], sc, ex, done[4 * half:4 * half + 4])

            run_all(turn_in(0, (0, 1, 2, 3)))
            run_all(attend(0, a_at()), proj)
            run_all(turn_in(1, (0, 1, 2, 3)))
            run_all(attend(1, x_at(4)))
            arena_free[:] = [done[-1][-1]]
            row_free[:] = arena_free
            (ah, al), (xh, xl) = a_at(), x_at()
            return project_to_h((lambda k: ah(k) if k < 4 else xh(k), lambda k: al(k) if k < 4 else xl(k)), KC, done)

        def moba_gmlp(h_ready):
            qk, values, gates = view(0, NT, 2 * HEADS_M, DM), view(2048, NT, HEADS_M, P), view(4096, NT, 2 * D)
            uv = view(8192, NT, 2 * G_W)
            qt, kt = view(10240, HEADS_M, T), view(12288, HEADS_M // 2, T)
            sc, ex = view(13312, 2, BLK), view(14336, 3, BLK)
            wm, row = shaped(one_j, G_GRP, P), one_i[:, D:D + G_W]
            between = one_i[:, 0:D]
            got_w = small_load(wm, a["gmlp_w"], *row_free)
            got_row = small_load(row, a["gmlp_g"].partition_broadcast(P))
            got_between = small_load(between, a["final_norm"].partition_broadcast(P))
            cleared = [clear(qt), clear(values)]
            at_mix, at_first = GAINS["mix2"][0], GAINS["final"][0]
            both = dve.do(lambda e, now: e.tensor_tensor(
                gains[:, at_mix:at_mix + KC], gains[:, at_mix:at_mix + KC], gains[:, at_first:at_first + KC], ALU.mult))
            act.wait(both)
            dve.wait(both)
            norms = {}

            def norm_h():
                r = norms["first"] = inv_rms(h_tile, D, flat(h_ready), 40)
                norms["h"] = [dve.do(lambda e, now, t=t: e.scalar_tensor_tensor(
                    h[:, t, :], h[:, t, :], rstd(t, 40), between, ALU.mult, ALU.mult), r, got_between,
                    *turned_all()) for t in range(NT)]

            def turned_all():
                return [mark for b in (0, 1, 2, 3) for mark in free[b]]

            def scale_both():
                r = inv_rms(h_tile, D, norms["h"])
                r = dve.do(lambda e, now: e.tensor_tensor(small[:, 4:6], small[:, 4:6], small[:, 44:46], ALU.mult), r)
                act.wait(r)
                dve.wait(r)

            x_ready = lift(h_chunk, KC, lambda k: gain("mix2", k), x_hi, x_lo, by_chunk(h_ready), (2, 3, 0, 1), norm_h)
            flat_qk = qk.rearrange("p t h d -> p t (h d)")
            parts, uvs, gs = {}, {}, {}

            def leave(n, t, psum, done):
                if n == 0 and t == 0:
                    scale_both()
                if n < 2:
                    parts[n, t] = scale_out(t, psum, done, flat_qk[:, t, n * BLK:(n + 1) * BLK])
                    return [parts[n, t]]
                if n == 2:
                    act.wait(*cleared)
                    dve.wait(*cleared)
                    parts[n, t] = values_out(t, psum, done, values[:, t, :, :], HEADS_M)
                    return [parts[n, t]]
                place, func, at = (uv, ACT.Gelu_apprx_tanh, n - 3) if n < 5 else (gates, ACT.Sigmoid, n - 5)
                store = uvs if n < 5 else gs
                store[at, t] = act.do(lambda e, now: e.activation(
                    place[:, t, at * BLK:(at + 1) * BLK], psum, func, scale=rstd(t)), done)
                return [store[at, t]]

            proj = project_steps(*x_at(), KC, 9, BLK, x_ready, leave, banks=(4, 5, 6, 7, 4, 5) + (6, 7) * 6)
            for _ in range(4):
                next(proj)
            cos, sin = trig("trig_m", DM // 2, 2 * HEADS_M)
            next(proj)
            rot = rotate(qk[:, :, :, 0:32], qk[:, :, :, 32:64], cos, sin, shaped(arena[:, 13312:14336], NT, 16, 32),
                         shaped(arena[:, 14336:15360], NT, 16, 32), [parts[n, t] for n in range(2) for t in range(NT)])
            for _ in range(3):
                next(proj)
            tq, tk, done = [], [], [[] for _ in range(4)]
            run_all(turn_steps(lambda t, i: flat_qk[:, t, i * P:(i + 1) * P], P, 4,
                               halves(qt, lambda i: 2 * i, lambda i: 2 * i + 1), [rot], tq, DM ** -0.5))
            run_all(turn_steps(lambda t, i: flat_qk[:, t, 512 + i * P:512 + (i + 1) * P], P, 4, whole(kt), [rot], tk))
            run_all(attention_steps(
                HEADS_M, up_to, lambda hd, n: qt[:, hd, n * P:(n + 1) * P], lambda hd: kt[:, hd // 2, :],
                lambda hd, t: values[:, t, hd, :], causal, a_at(),
                tq + tk + [parts[2, t] for t in range(NT)], sc, ex, done), proj)
            masked = dve.do(lambda e, now: e.tensor_tensor(
                wm, wm, const("tri").unsqueeze(1).broadcast_to([P, G_GRP, P]), ALU.mult), got_w)
            memory = view(10240, NT, D)
            got_mem = small_load(memory, a["mem"].rearrange("(t p) d -> p t d", p=P), done[-1][-1])
            v_at = lambda t: uv[:, t, 512:1024]
            r = inv_rms(v_at, G_W, [uvs[1, 0], uvs[1, 1]], 24)
            vn = [dve.do(lambda e, now, t=t: e.scalar_tensor_tensor(
                v_at(t), v_at(t), rstd(t, 24), row, ALU.mult, ALU.mult), r, got_row) for t in range(NT)]
            outs = [[], []]

            def weigh(first):
                def leave(n, t, psum, done):
                    place = gates[:, t, first + n * BLK:first + (n + 1) * BLK]
                    r = dve.do(lambda e, now: e.tensor_tensor(place, psum, place, ALU.mult), done, gs[first // BLK + n, t])
                    if first:
                        into = gates[:, t, n * BLK:(n + 1) * BLK]
                        outs[n].append(dve.do(lambda e, now: e.tensor_tensor(into, into, place, ALU.add), r))
                    return [r]
                return leave

            project(*a_at(), 4, 2, BLK, done, weigh(0))
            uz = []
            for t in range(NT):
                pe.wait(*free[6 + t], vn[t], masked)
                for grp in range(G_GRP):
                    pe.put(lambda e, now, t=t, grp=grp: e.matmul(
                        bank[6 + t][:, grp * 64:(grp + 1) * 64], wm[:, grp, :],
                        uv[:, t, 512 + grp * 64:512 + (grp + 1) * 64], start=True, stop=True))
                m = mark_last_pe()
                at, _ = GAINS["bs"]
                z = dve.do(lambda e, now, t=t: e.tensor_tensor(
                    v_at(t).rearrange("p (g d) -> p g d", g=G_GRP),
                    bank[6 + t][:, :].rearrange("p (g d) -> p g d", g=G_GRP),
                    gains[:, at:at + G_GRP].unsqueeze(2).broadcast_to([P, G_GRP, 64]), ALU.add), m)
                uz.append(dve.do(lambda e, now, t=t: e.tensor_tensor(
                    uv[:, t, 0:512], uv[:, t, 0:512], v_at(t), ALU.mult), z, uvs[0, t]))
                free[6 + t] = [z]
            m_ready = lift(lambda t, k: memory[:, t, k * P:(k + 1) * P], KC, lambda k: gain("mem", k), x_hi, x_lo,
                           [[got_mem]] * KC)
            list(m_ready[-1])
            r_mem = inv_rms(lambda t: memory[:, t, :], D, [got_mem], 32)
            lb = lift(lambda t, k: uv[:, t, k * P:(k + 1) * P], 4, None, a_hi, a_lo, [uz] * 4)
            project(*a_at(), 4, 2, BLK, lb, weigh(D), banks=(4, 5, 0, 1))
            kn, vn = view(0, NT, 512), view(1024, NT, 512)
            act.wait(r_mem)
            dve.wait(r_mem)

            def leave_mem(n, t, psum, done):
                mem_parts[n, t] = scale_out(t, psum, done, (kn, vn)[n][:, t, :], 32)
                return [mem_parts[n, t]]

            project(*x_at(), KC, 2, BLK, m_ready, leave_mem)
            x_ready = lift(lambda t, k: gates[:, t, k * P:(k + 1) * P], KC, None, x_hi, x_lo, by_chunk(outs))
            return project_to_h(x_at(), KC, x_ready)

        mem_parts = {}

        def cross_attention(h_ready):
            kn, vn, kt = view(0, NT, 512), view(1024, NT, 512), view(2048, HEADS_X, T)
            qn, qt = view(4096, NT, 512), view(5120, HEADS_X, T)
            sc, ex = view(6144, 2, BLK), view(7168, 3, BLK)
            parts, parts_q, tk, tq, done = mem_parts, [], [], [], [[] for _ in range(4)]

            def leave_q(n, t, psum, done):
                parts_q.append(scale_out(t, psum, done, qn[:, t, :]))
                return parts_q[-1:]

            run_all(turn_steps(lambda t, i: kn[:, t, i * P:(i + 1) * P], P, HEADS_X, whole(kt),
                               [parts[0, 0], parts[0, 1]], tk, banks=(6, 7)))
            x_ready = normed_operand("xa", h_ready)
            project(*x_at(), KC, 1, BLK, x_ready, leave_q, banks=(4, 5))
            run_all(turn_steps(lambda t, i: qn[:, t, i * P:(i + 1) * P], P, HEADS_X, whole(qt), parts_q, tq, DX ** -0.5))
            run_all(attention_steps(
                HEADS_X, lambda n: [0, 1], lambda hd, n: qt[:, hd, n * P:(n + 1) * P], lambda hd: kt[:, hd, :],
                lambda hd, t: vn[:, t, hd * DX:(hd + 1) * DX], None, a_at(),
                tk + tq + [parts[1, 0], parts[1, 1]], sc, ex, done, wide=True))
            arena_free[:] = [done[-1][-1]]
            return project_to_h(a_at(), 4, done)

        def peer(h_ready):
            N_BLK, PER = 4, 4
            n_pairs = NT * HEADS_P
            n_lists = n_pairs * 2
            qn, qt, keys = view(0, NT, 2048), view(4096, 16, T), view(8192, 16, NKEYS)
            sc = view(10240, n_lists, NKEYS)
            best, where = view(14336, n_lists, TOPK), view(14848, n_lists, TOPK).bitcast(U32)
            place, value = view(15360, n_pairs, TOPK).bitcast(U32), view(15616, n_pairs, TOPK)
            cand = view(15872, PER, N_CAND)
            routed = view(16384, 640).bitcast(BF16).rearrange("p (a t) -> p a t", t=T)
            names = ("expv", "row_i", "col_i", "lt", "a1", "a2", "b1", "b2")
            buf = {n: view(i * 256, n_pairs, TOPK) for i, n in enumerate(names)}
            where_f, total, rest = view(2048, n_lists, TOPK), view(2560, n_pairs, 1), view(2576, T)
            ranks = view(2832, 256).bitcast(BF16).rearrange("p (s l k) -> p s l k", s=2, k=TOPK)
            by_rank = [view(4096 + 2048 * i, 2048).bitcast(BF16).rearrange("p (l a k) -> p l a k", a=TOPK, k=TOPK)
                       for i in range(2)]
            match = view(8192, 2048).bitcast(BF16).rearrange("p (l a k) -> p l a k", a=TOPK, k=TOPK)
            rank_rep = view(3088, 128).bitcast(BF16).rearrange("p (a k) -> p a k", a=TOPK)

            got_keys = small_load(keys, a["subkeys"], *arena_free)
            x_ready = normed_operand("ffn", h_ready)
            parts = {}
            dve.do(lambda e, now: e.tensor_copy(iota_rep[:, :, :], const("iota").unsqueeze(2).broadcast_to([P, NKEYS, OCT])))

            def leave(n, t, psum, done):
                parts[n, t] = act.do(lambda e, now: e.activation(
                    qn[:, t, n * BLK:(n + 1) * BLK], psum, ACT.Copy, scale=rstd(t)), done)
                return [parts[n, t]]

            def top16(lists, ready):
                for cols in (slice(0, 8), slice(8, 16)):
                    t1 = [dve.do(lambda e, now, src=src, best=best, cols=cols: e.max(best[:, cols], src), *ready)
                          for src, best, _ in lists]
                    t2 = [dve.do(lambda e, now, src=src, best=best, at=at, cols=cols: e.max_index(
                        at[:, cols], best[:, cols], src), t1[i]) for i, (src, best, at) in enumerate(lists)]
                    if cols.start == 0:
                        ready = [dve.do(lambda e, now, src=src, best=best, cols=cols: e.match_replace(
                            src, best[:, cols], src, NEG * 1e3), t2[i]) for i, (src, best, _) in enumerate(lists)][-1:]
                return t2[-1]

            found, chosen = {}, {}

            def route(n):
                tq, scs = [], []
                yield from turn_steps(lambda t, i: qn[:, t, (PER * n + i) * P:(PER * n + i + 1) * P], P, PER,
                                      whole(qt[:, PER * n:PER * n + PER, :]), [parts[n, 0], parts[n, 1]], tq,
                                      banks=(0, 1), share=False)
                pe.wait(*tq, got_keys)
                for t in range(NT):
                    b = 2 + t
                    pe.wait(*free[b])
                    for i in range(PER):
                        pe.put(lambda e, now, b=b, i=i, t=t: e.matmul(
                            bank[b][:, i * P:(i + 1) * P], qt[:, PER * n + i, t * P:(t + 1) * P], keys[:, PER * n + i, :],
                            start=True, stop=True))
                    m = mark_last_pe()
                    l0 = t * 16 + PER * n
                    scs.append(act.do(lambda e, now, b=b, l0=l0: e.activation(
                        sc[:, l0:l0 + PER, :], bank[b][:, :].rearrange("p (a b) -> p a b", a=PER), ACT.Copy), m))
                    free[b] = scs[-1:]
                for t in range(NT):
                    l0 = t * 16 + PER * n
                    found[n, t] = top16([(sc[:, l0 + i, :], best[:, l0 + i, :], where[:, l0 + i, :])
                                         for i in range(PER)], [scs[t]])
                    yield
                sides = best.rearrange("p (l s) k -> p l s k", s=2)
                pairs = [t * HEADS_P + 2 * n + i for t in range(NT) for i in range(2)]
                for i, l in enumerate(pairs):
                    for r0, r1, cols, at in ((0, WHOLE_ROWS, TOPK, 0), (WHOLE_ROWS, TOPK, PART_COLS, WHOLE_ROWS * TOPK)):
                        cd = dve.do(lambda e, now, i=i, l=l, r0=r0, r1=r1, cols=cols, at=at: e.tensor_tensor(
                            cand[:, i, at:at + (r1 - r0) * cols].rearrange("p (a b) -> p a b", b=cols),
                            sides[:, l, 0, r0:r1].unsqueeze(2).broadcast_to([P, r1 - r0, cols]),
                            sides[:, l, 1, 0:cols].unsqueeze(1).broadcast_to([P, r1 - r0, cols]), ALU.add),
                            found[n, 0], found[n, 1], *chosen.values())
                chosen[n] = top16([(cand[:, i, :], value[:, l, :], place[:, l, :])
                                   for i, l in enumerate(pairs)], [cd])
                yield

            table = view(0, T, JH)

            def activate(c, t, psum, done, turned):
                r = act.do(lambda e, now: e.activation(mid[:, t, :], psum[:, :], ACT.Gelu_apprx_tanh, scale=rstd(t)),
                           done, turned)
                return [r], [r]

            def weigh(c, b, psum, turned, down_done):
                j = g.count("column", 2) - 2
                base = weigh.base
                both = gated[:, 2 * b:2 * b + 2, :]
                m = dve.do(lambda e, now: e.tensor_tensor(
                    both, psum.rearrange("p (f t) -> p f t", f=2),
                    table[:, :, bass.ds(now(j, "column") - base, 2)].rearrange("p t j -> p j t"), ALU.mult),
                    turned, weigh.read.get(b))
                hl = split_a(b, both.rearrange("p f t -> p (f t)"), m, down_done)
                weigh.read[b] = hl[1]
                return [m], hl

            weigh.read = {}

            remainder[0] = pool
            proj = project_steps(*x_at(), KC, N_BLK, BLK, x_ready, leave, banks=(4, 5, 6, 7))
            next(proj)
            next(proj)
            routes = []
            for n in range(N_BLK):
                routes.append(route(n))
                for steps in ((3, 1) if n == 0 else (1, 2)):
                    for earlier in routes[:n]:
                        next(earlier, None)
                    for _ in range(steps):
                        next(routes[n])
                    next(proj, None)
            pipe = Gated(EC, activate, weigh, None)
            ready = pipe.up(0)
            remainder[0] = dve
            run_all(*routes)

            last = chosen[N_BLK - 1]
            d1 = dve.do(lambda e, now: e.tensor_tensor(
                buf["expv"], value, value[:, :, 0:1].broadcast_to([P, n_pairs, TOPK]), ALU.subtract), last)
            d2 = act.do(lambda e, now: e.activation(buf["expv"], buf["expv"], ACT.Exp), d1)
            wf = dve.do(lambda e, now: e.tensor_copy(where_f, where))
            keys_of = where_f.rearrange("p (l s) k -> p l s k", s=2)
            wide = [act.do(lambda e, now, side=side: e.activation(
                by_rank[side], keys_of[:, :, side, :].unsqueeze(3).broadcast_to([P, n_pairs, TOPK, TOPK]), ACT.Copy), wf)
                for side in range(2)]
            u32 = {n: buf[n].bitcast(U32) for n in ("a1", "a2", "b1", "b2")}
            shift = WHOLE_ROWS * TOPK // PART_COLS - WHOLE_ROWS
            rr = dve.do(lambda e, now: e.tensor_copy(
                rank_rep, const("iota")[:, 0:TOPK].unsqueeze(2).broadcast_to([P, TOPK, TOPK])))
            s1 = dve.do(lambda e, now: e.tensor_scalar(u32["a1"], place, 4, None, ALU.logical_shift_right))
            s2 = dve.do(lambda e, now: e.tensor_scalar(u32["a2"], place, 2, None, ALU.logical_shift_right))
            s3 = dve.do(lambda e, now: e.tensor_scalar(u32["b1"], place, 3, None, ALU.bitwise_and))
            s4 = dve.do(lambda e, now: e.tensor_scalar(u32["b2"], place, 12, None, ALU.bitwise_and))
            f0 = dve.do(lambda e, now: e.tensor_copy(buf["lt"], place))
            f1 = dve.do(lambda e, now: e.tensor_copy(buf["a1"], u32["a1"]), s1)
            f2 = dve.do(lambda e, now: e.tensor_copy(buf["a2"], u32["a2"]), s2)
            f3 = dve.do(lambda e, now: e.tensor_copy(buf["b1"], u32["b1"]), s3)
            f4 = dve.do(lambda e, now: e.tensor_copy(buf["b2"], u32["b2"]), s4)
            ra = dve.do(lambda e, now: e.scalar_tensor_tensor(
                ranks[:, 0, :, :], buf["a2"], float(-shift), buf["a1"], ALU.add, ALU.max), f1, f2)
            m1 = dve.do(lambda e, now: e.scalar_tensor_tensor(
                buf["b2"], buf["lt"], float(WHOLE_ROWS * TOPK), buf["b2"], ALU.is_lt, ALU.mult), f0, f4)
            rb = dve.do(lambda e, now: e.tensor_tensor(ranks[:, 1, :, :], buf["b2"], buf["b1"], ALU.add), m1, f3)
            d3 = dve.do(lambda e, now: e.reduce_sum(total, buf["expv"], AX), d2)
            d4 = dve.do(lambda e, now: e.reciprocal(total, total), d3)
            weight = dve.do(lambda e, now: e.tensor_tensor(
                buf["expv"], buf["expv"], total.broadcast_to([P, n_pairs, TOPK]), ALU.mult), d4)
            last, looked = None, []
            for side, to in enumerate(("row_i", "col_i")):
                last = dve.do(lambda e, now, side=side: e.tensor_tensor(
                    match, ranks[:, side, :, :].unsqueeze(2).broadcast_to([P, n_pairs, TOPK, TOPK]),
                    rank_rep.unsqueeze(1).broadcast_to([P, n_pairs, TOPK, TOPK]), ALU.is_equal), ra, rb, rr, last)
                last = dve.do(lambda e, now, side=side: e.tensor_tensor(match, match, by_rank[side], ALU.mult),
                              last, wide[side])
                n = TOPK // 2
                while n:
                    dst = buf[to].unsqueeze(2) if n == 1 else match[:, :, 0:n, :]
                    last = dve.do(lambda e, now, n=n, dst=dst: e.tensor_tensor(
                        dst, match[:, :, 0:n, :], match[:, :, n:2 * n, :], ALU.add), last)
                    n //= 2
                looked.append(last)
            for i, name in enumerate(("expv", "row_i", "col_i")):
                b = min(i, 1)
                pe.wait(*free[b], weight if i == 0 else looked[i - 1])
                for t in range(NT):
                    at = (i == 2) * T + t * P
                    transpose_to(bank[b][:, at:at + P],
                                 buf[name][:, t * HEADS_P:(t + 1) * HEADS_P, :].rearrange("p l k -> p (l k)"))
                if i == 0:
                    m = mark_last_pe()
                    v1 = act.do(lambda e, now: e.activation(routed[:, 2, :], bank[0][:, 0:T], ACT.Copy), m)
                    w1 = dve.do(lambda e, now: e.tensor_tensor(rest, bank[0][:, 0:T], routed[:, 2, :], ALU.subtract), v1)
                    w2 = dve.do(lambda e, now: e.tensor_copy(routed[:, 3, :], rest), w1)
                    w3 = dve.do(lambda e, now: e.tensor_tensor(routed[:, 4, :], rest, routed[:, 3, :], ALU.subtract), w2)
                    free[0] = [w1]
            m = mark_last_pe()
            v2 = act.do(lambda e, now: e.activation(routed[:, 0:2, :].rearrange("p a b -> p (a b)"), bank[1][:, :],
                                                    ACT.Copy), m)
            free[1] = [v2]

            hot_free = {}
            hot_i = one_j.bitcast(BF16).rearrange("p (s n t) -> p s n t", s=2, t=OCT)
            hot_j = one_i.bitcast(BF16).rearrange("p (s k n t) -> p s k n t", s=2, k=4, t=OCT)

            def scatter(half, ready):
                dve.wait(*ready)
                made = []

                def octet(i, base):
                    slot = i % 2
                    u = g.count("token", OCT) - OCT
                    at = lambda now: now(u, "token") if base == 0 else now(u, "token") - base

                    def token_cols(now, first, k, n):
                        cols = routed[:, first:first + k, bass.ds(at(now), OCT)]
                        return cols.unsqueeze(2).broadcast_to([P, k, n, OCT])

                    c1 = dve.do(lambda e, now: e.tensor_tensor(
                        hot_j[:, slot, 0:1, :, :], iota_rep[:, half * JH:(half + 1) * JH, :].unsqueeze(1),
                        token_cols(now, 1, 1, JH), ALU.is_equal), hot_free.get(slot))
                    rows_ = dve.do(lambda e, now: e.tensor_tensor(
                        hot_i[:, slot, :, :].unsqueeze(1), iota_rep[:, :, :].unsqueeze(1), token_cols(now, 0, 1, NKEYS),
                        ALU.is_equal))
                    cols_ = dve.do(lambda e, now: e.tensor_tensor(
                        hot_j[:, slot, 1:4, :, :], hot_j[:, slot, 0:1, :, :].broadcast_to([P, 3, JH, OCT]),
                        token_cols(now, 2, 3, JH), ALU.mult), c1)
                    b = 6 + slot
                    pe.wait(rows_, cols_, *free[b])
                    for j in range(OCT):
                        for k in range(3):
                            pe.put(lambda e, now, j=j, k=k: e.matmul(
                                bank[b][:, j * JH:(j + 1) * JH], hot_i[:, slot, :, j], hot_j[:, slot, 1 + k, :, j],
                                start=k == 0, stop=k == 2))
                    hot_free[slot] = mark_last_pe()
                    r = act.do(lambda e, now: e.activation(
                        table[:, bass.ds(at(now), OCT), :], bank[b][:, :].rearrange("p (a b) -> p a b", a=OCT), ACT.Copy),
                        hot_free[slot])
                    free[b] = [r]
                    made.append(r)

                base = g.counts.get("token", 0)
                act.wait(*ready)
                octet(0, base)
                octet(1, base)
                with g.loop(T // OCT // 2 - 1):
                    octet(2, base)
                    octet(3, base)
                return made[-1:]

            last_done = [w3, v2]
            n_chunks = JH // EC
            for half in range(2):
                if half:
                    ready = pipe.up(0)
                    pipe.down()
                    last_done += [weigh.read[0], weigh.read[1]]
                filled = scatter(half, last_done)
                dve.wait(*filled)
                weigh.base = g.counts.get("column", 0)
                pipe.chunk(1, lambda: pipe.back(0, ready))
                with g.loop((n_chunks - 4) // 3):
                    for c in range(3):
                        pipe.chunk(c)
                pipe.chunk(2)
                pipe.chunk(3)
                last_done = []
            row_free[:] = list(hot_free.values())
            pipe.down(last=True)
            return add_to_h(1.0, pipe.half_done, h_ready)

        pe.wait(got_consts)
        act.wait(got_gains, got_consts)
        dve.wait(got_gains, got_consts)
        pool.wait(got_consts)
        engines = (pe, act, dve, pool, sp)

        def stages():
            ready = [[got_h[0]], [got_h[1]]]
            for l in range(DEPTH):
                ready = ffn(f"ffa{l}", ready, first=l == 0)
                yield f"ffa{l}", ready
                for e in engines[:3] if l == 0 else ():
                    e.wait(got_later)
                ready = even_mixer(ready) if l == 0 else odd_mixer(ready)
                yield f"mix{l}", ready
                ready = ffn(f"ffb{l}", ready)
                yield f"ffb{l}", ready
                ready = ple(l, ready)
                yield f"ple{l}", ready
            ready = moba_gmlp(ready)
            yield "moba", ready
            ready = cross_attention(ready)
            yield "cross", ready
            ready = peer(ready)
            yield "peer", ready
            ready = norm_rows("final_g", ready)
            yield "all", ready

        for name, ready in stages():
            if name == (stop or "all"):
                return finish(nc, ctx, a, h, ready, sem, engines)


def finish(nc, ctx, a, out, ready, sem, engines):
    pe, act, dve, pool, sp = engines
    s_out = sem("stored")
    sp.wait(sp.load(s_out, lambda e, now: e.dma_start(
        a["out"].rearrange("(t p) d -> p t d", p=P), out[:, :, :]), *ready[0], *ready[1]))
    block = ctx.enter_context(nc.Block())
    block.tensor(pe.run)
    block.scalar(act.run)
    block.vector(dve.run)
    block.gpsimd(pool.run)
    block.sync(sp.run)


def pack(w, width=BLK):
    k, n = w.shape
    nb = -(-n // width)
    full = np.zeros((k, nb * width), w.dtype)
    full[:, :n] = w
    blocks = full.reshape(k // P, P, nb, width).transpose(2, 0, 1, 3).reshape(-1, P, width)
    nu = -(-len(blocks) // UB)
    out = np.zeros((nu * UB, P, BLK), w.dtype)
    out[:len(blocks), :, :width] = blocks
    return out.reshape(nu, UB, P, BLK).transpose(0, 2, 1, 3)


def pack_pipeline(up, down, c_up, c_down):
    parts = [up[:c_up]]
    n = len(up) // c_up
    for c in range(1, n):
        parts += [up[c * c_up:(c + 1) * c_up], down[(c - 1) * c_down:c * c_down]]
    return np.concatenate(parts + [down[(n - 1) * c_down:]])


def pack_ffn(gate_up, down):
    gu = gate_up.reshape(D, 2, NFC, FC).transpose(0, 2, 1, 3).reshape(D, 2 * FF)
    dn = down.reshape(FF // P, P, 2, BLK).transpose(0, 2, 1, 3).reshape(-1, UB, P, BLK).transpose(0, 2, 1, 3)
    return pack_pipeline(pack(gu), dn, 2, 1)


def lay_out(x):
    def rows(w):
        return w.reshape(-1, P, w.shape[-1]).transpose(1, 0, 2).reshape(P, -1)

    stream = []
    for l in range(DEPTH):
        stream.append(pack_ffn(x["ffa_w_gate_up"][l], x["ffa_w_down"][l]))
        if l == 0:
            w_in = x["ev_w_in"][0]
            n_q = HEADS_A * DA
            q = w_in[:, :n_q].reshape(D, KV_A, HEADS_A // KV_A, DA).transpose(0, 2, 1, 3).reshape(D, n_q)
            stream += [pack(np.concatenate([q, w_in[:, n_q:]], 1)), pack(x["ev_w_uq"][0], 384),
                       pack(x["ev_w_ukv"][0]), pack(x["ev_w_out"][0])]
        else:
            w_in = x["od_w_in"][0][:, :3 * D].reshape(D, 3, 2, BLK)
            stream += [pack(w_in.transpose(0, 2, 1, 3).reshape(D, 3 * D)), pack(x["od_w_out"][0])]
        stream += [pack_ffn(x["ffb_w_gate_up"][l], x["ffb_w_down"][l]), pack(x["ple_w_gate"][l]), pack(x["ple_w_proj"][l])]
    for name in ("w_in", "moba_w_proj", "gmlp_w_proj", "xa_w_kv", "w_out", "xa_w_q", "xa_w_o", "peer_w_q"):
        stream.append(pack(x[name + "_2"][0]))
    down = x["peer_w_down_2"][0].reshape(NKEYS, NKEYS, D).transpose(2, 1, 0).reshape(D, NKEYS * NKEYS)
    up = x["peer_w_up_2"][0].reshape(NKEYS, NKEYS, 2, BLK).transpose(1, 2, 0, 3)
    up = up.reshape(-1, UB, P, BLK).transpose(0, 2, 1, 3)
    stream.append(pack_pipeline(pack(down), up, 2, 2))
    gains = [None] * len(GAINS)
    cols = {"cq": x["ev_cq_norm"][0], "ckv": x["ev_ckv_norm"][0], "mix2": x["norm_mix_g_2"][0],
            "xa": x["norm_xa_g_2"][0], "mem": x["norm_mem_g_2"][0], "ffn": x["norm_ffn_g_2"][0],
            "final": x["final_norm"], "bs": x["gmlp_b_s_2"][0]}
    for l in range(DEPTH):
        for n in ("ffa", "mix", "ffb", "ple"):
            cols[f"{n}{l}"] = x[f"{n}_norm"][l]
    gains = np.concatenate([cols[n].reshape(-1, P).T for n in GAINS], 1)
    consts, alibi = constants()
    return {
        "w": np.concatenate(stream).reshape(-1), "x": x["x"][0], "gains": gains, "consts": consts, "alibi": alibi,
        "p0": rows(x["p"][0, 0].T), "p1": rows(x["p"][1, 0].T), "sinks": x["ev_sinks"][0],
        "w_f": rows(x["od_w_in"][0][:, 3 * D:]), "b_f": x["od_b_f"][0], "final_norm": x["final_norm"],
        "gmlp_w": x["gmlp_w_s_2"][0].transpose(2, 0, 1).reshape(P, -1), "gmlp_g": x["gmlp_norm_g_2"][0],
        "mem": x["mem_2"][0], "subkeys": x["peer_subkeys_2"][0].transpose(3, 0, 1, 2).reshape(P, -1),
        "final_g": x["final_g_2"],
    }


def kernel(stop=None, **inputs):
    import concourse.bacc as bacc
    from concourse.bass_utils import run_bass_kernel_spmd

    arrays = {n: np.ascontiguousarray(v) for n, v in lay_out({k: np.asarray(v) for k, v in inputs.items()}).items()}
    nc = bacc.Bacc("TRN2", target_bir_lowering=False, num_devices=1)
    a = {n: nc.dram_tensor(f"in_{n}", v.shape, F32, kind="ExternalInput").ap() for n, v in arrays.items()}
    a["out"] = nc.dram_tensor("out", (T, D), F32, kind="ExternalOutput").ap()
    build(nc, a, stop)
    got = run_bass_kernel_spmd(nc, [{f"in_{n}": v for n, v in arrays.items()}], core_ids=[0])
    return got.results[0]["out"].reshape(1, T, D)
```
